# Optimizing a Trainium2 kernel written in Bass

```python
import math
import jax, jax.numpy as jnp
from jax import lax
import numpy as np

D_MODEL = 1024
BATCH = 1
SEQ = 512
DEPTH = 1

D_MIX = D_MODEL
SB_HEADS = 8
SB_HEAD_DIM = 64
SB_WIDTH = SB_HEADS * SB_HEAD_DIM
RW_HEADS = 8
RW_HEAD_DIM = 64
RW_WIDTH = RW_HEADS * RW_HEAD_DIM
LORA_W = 64
LORA_A = 64
LORA_G = 128
RW_IN = 3 * RW_WIDTH + LORA_W + LORA_A + LORA_G
SB_IN = 3 * SB_WIDTH
N_IN = SB_IN + RW_IN
Q_BLOCK = 128
N_GROUPS = 4
EXPERTS_PER_GROUP = 8
N_EXPERTS = N_GROUPS * EXPERTS_PER_GROUP
TOP_K_IN_GROUP = 2
D_EXPERT = 256
RMS_EPS = 1e-6
GN_EPS = 64e-5


def rmsnorm(x, g):
    xf = x.astype(jnp.float32)
    y = xf * lax.rsqrt(jnp.mean(xf * xf, axis=-1, keepdims=True) + RMS_EPS)
    return (y * g.astype(jnp.float32)).astype(x.dtype)

def token_shift(u):
    return jnp.pad(u, ((0, 0), (1, 0), (0, 0)))[:, :-1]

def stick_breaking_attention(q, k, v):
    B, H, S, dh = q.shape
    scale = 1.0 / math.sqrt(dh)
    outs = []
    for blk in range(S // Q_BLOCK):
        t0 = blk * Q_BLOCK
        kv_len = t0 + Q_BLOCK
        qb = q[:, :, t0:kv_len].astype(jnp.float32)
        kb = k[:, :, :kv_len].astype(jnp.float32)
        vb = v[:, :, :kv_len].astype(jnp.float32)
        z = jnp.einsum('bhqd,bhkd->bhqk', qb, kb) * scale
        t_pos = t0 + jnp.arange(Q_BLOCK)[:, None]
        s_pos = jnp.arange(kv_len)[None, :]
        strict = s_pos < t_pos
        log_rest = jnp.where(strict, jax.nn.log_sigmoid(-z), 0.0)
        suffix = lax.cumsum(log_rest, axis=3, reverse=True) - log_rest
        weights = jnp.where(strict, jnp.exp(jax.nn.log_sigmoid(z) + suffix), 0.0)
        outs.append(jnp.einsum('bhqk,bhkd->bhqd', weights, vb))
    return jnp.concatenate(outs, axis=2)

def rwkv7_scan(r, w, k, v, kk, a):
    B, S, H, N = r.shape
    xs = tuple(jnp.moveaxis(t, 1, 0) for t in (r, w, k, v, kk, a))

    def step(state, inp):
        r_t, w_t, k_t, v_t, kk_t, a_t = inp
        sa = jnp.einsum('bhij,bhj->bhi', state, -kk_t)
        state = (state * w_t[:, :, None, :]
                 + sa[..., None] * (kk_t * a_t)[:, :, None, :]
                 + v_t[..., None] * k_t[:, :, None, :])
        out = jnp.einsum('bhij,bhj->bhi', state, r_t)
        return state, out

    state0 = jnp.zeros((B, H, N, N), jnp.float32)
    _, outs = lax.scan(step, state0, xs)
    return jnp.moveaxis(outs, 0, 1)

def rwkv7_group(u_rw, shift_mu, w0, w2, a0, a2, g2, k_k, k_a, r_k, ln_w, ln_b):
    B, S, _ = u_rw.shape
    uf = u_rw.astype(jnp.float32)
    um = uf + (token_shift(uf) - uf) * shift_mu.astype(jnp.float32)
    o = 0
    r = um[..., o:o + RW_WIDTH]; o += RW_WIDTH
    k = um[..., o:o + RW_WIDTH]; o += RW_WIDTH
    v = um[..., o:o + RW_WIDTH]; o += RW_WIDTH
    xw = um[..., o:o + LORA_W]; o += LORA_W
    xa = um[..., o:o + LORA_A]; o += LORA_A
    xg = um[..., o:o + LORA_G]
    w_log = -jax.nn.softplus(-(w0 + jnp.tanh(xw) @ w2)) - 0.5
    decay = jnp.exp(-jnp.exp(w_log))
    a = jax.nn.sigmoid(a0 + xa @ a2)
    g = jax.nn.sigmoid(xg) @ g2
    hs = lambda t: t.reshape(B, S, RW_HEADS, RW_HEAD_DIM)
    kk = hs(k * k_k)
    kk = kk * lax.rsqrt(jnp.maximum(jnp.sum(kk * kk, axis=-1, keepdims=True), 1e-24))
    k = k * (1.0 + (a - 1.0) * k_a)
    r_h, k_h, v_h, w_h, a_h = hs(r), hs(k), hs(v), hs(decay), hs(a)
    out = rwkv7_scan(r_h, w_h, k_h, v_h, kk, a_h)
    mean = jnp.mean(out, axis=-1, keepdims=True)
    var = jnp.mean(jnp.square(out - mean), axis=-1, keepdims=True)
    out = ((out - mean) * lax.rsqrt(var + GN_EPS)).reshape(B, S, RW_WIDTH) * ln_w + ln_b
    bonus = jnp.sum(r_h * k_h * r_k, axis=-1, keepdims=True) * v_h
    out = (out + bonus.reshape(B, S, RW_WIDTH)) * g
    return out.astype(u_rw.dtype)

def sb_group(u_sb, sb_out_g):
    B, S, _ = u_sb.shape
    heads = lambda t: t.reshape(B, S, SB_HEADS, SB_HEAD_DIM).transpose(0, 2, 1, 3)
    q = heads(u_sb[..., :SB_WIDTH])
    k = heads(u_sb[..., SB_WIDTH:2 * SB_WIDTH])
    v = heads(u_sb[..., 2 * SB_WIDTH:])
    o = stick_breaking_attention(q, k, v).transpose(0, 2, 1, 3)
    o = o * lax.rsqrt(jnp.mean(o * o, axis=-1, keepdims=True) + RMS_EPS)
    return (o.reshape(B, S, SB_WIDTH) * sb_out_g).astype(u_sb.dtype)

def hier_moe(x2d, w_grp, b_grp, w_exp, b_exp, w_gate, w_up, w_down):
    T = x2d.shape[0]
    xf = x2d.astype(jnp.float32)
    grp_prob = jax.nn.softmax(xf @ w_grp.astype(jnp.float32) + b_grp.astype(jnp.float32), axis=-1)
    g_val, g_idx = lax.top_k(grp_prob, 1)
    exp_logits = (xf @ w_exp.astype(jnp.float32) + b_exp.astype(jnp.float32)).reshape(T, N_GROUPS, EXPERTS_PER_GROUP)
    sel = jnp.take_along_axis(exp_logits, g_idx[:, :, None], axis=1)[:, 0]
    e_val, e_idx = lax.top_k(jax.nn.softmax(sel, axis=-1), TOP_K_IN_GROUP)
    weights = g_val * e_val / jnp.sum(e_val, axis=-1, keepdims=True)
    global_idx = g_idx * EXPERTS_PER_GROUP + e_idx
    combine = jnp.sum(jax.nn.one_hot(global_idx, N_EXPERTS, dtype=jnp.float32) * weights[..., None], axis=1)
    combine = combine.astype(x2d.dtype)
    y = jnp.zeros_like(x2d)
    for e in range(N_EXPERTS):
        h = jax.nn.silu(x2d @ w_gate[e]) * (x2d @ w_up[e])
        y = y + combine[:, e:e + 1] * (h @ w_down[e])
    return y

def first_inputs(seed: int = 0) -> dict:
    key = jax.random.key(seed)
    ks = jax.random.split(key, 28)
    f32 = jnp.float32
    nrm = lambda k, shape, s: jax.random.normal(k, shape, f32) * s
    L = DEPTH
    return {
        "x": jax.random.normal(ks[0], (BATCH, SEQ, D_MODEL), f32),
        "norm_mix_g": 1.0 + nrm(ks[1], (L, D_MODEL), 0.02),
        "w_in": nrm(ks[2], (L, D_MODEL, N_IN), D_MODEL ** -0.5),
        "shift_mu": jax.random.uniform(ks[3], (L, RW_IN), f32, 0.1, 0.9),
        "sb_out_g": 1.0 + nrm(ks[4], (L, SB_WIDTH), 0.02),
        "rw_w0": jax.random.uniform(ks[5], (L, RW_WIDTH), f32, -6.5, -1.5),
        "rw_w2": nrm(ks[6], (L, LORA_W, RW_WIDTH), 0.5 * LORA_W ** -0.5),
        "rw_a0": nrm(ks[7], (L, RW_WIDTH), 0.1),
        "rw_a2": nrm(ks[8], (L, LORA_A, RW_WIDTH), LORA_A ** -0.5),
        "rw_g2": nrm(ks[9], (L, LORA_G, RW_WIDTH), LORA_G ** -0.5),
        "rw_k_k": 0.85 + nrm(ks[10], (L, RW_WIDTH), 0.02),
        "rw_k_a": 1.0 + nrm(ks[11], (L, RW_WIDTH), 0.02),
        "rw_r_k": nrm(ks[12], (L, RW_HEADS, RW_HEAD_DIM), 0.1),
        "rw_ln_w": 1.0 + nrm(ks[13], (L, RW_WIDTH), 0.02),
        "rw_ln_b": nrm(ks[14], (L, RW_WIDTH), 0.02),
        "w_out": nrm(ks[15], (L, D_MIX, D_MODEL), D_MIX ** -0.5),
        "norm_ffn_g": 1.0 + nrm(ks[16], (L, D_MODEL), 0.02),
        "router_grp_w": nrm(ks[17], (L, D_MODEL, N_GROUPS), D_MODEL ** -0.5),
        "router_grp_b": nrm(ks[18], (L, N_GROUPS), 0.01),
        "router_exp_w": nrm(ks[19], (L, D_MODEL, N_EXPERTS), D_MODEL ** -0.5),
        "router_exp_b": nrm(ks[20], (L, N_EXPERTS), 0.01),
        "exp_w_gate": nrm(ks[21], (L, N_EXPERTS, D_MODEL, D_EXPERT), D_MODEL ** -0.5),
        "exp_w_up": nrm(ks[22], (L, N_EXPERTS, D_MODEL, D_EXPERT), D_MODEL ** -0.5),
        "exp_w_down": nrm(ks[23], (L, N_EXPERTS, D_EXPERT, D_MODEL), D_EXPERT ** -0.5),
        "final_norm_g": 1.0 + nrm(ks[24], (D_MODEL,), 0.02),
    }

def first_block(x, norm_mix_g, w_in, shift_mu, sb_out_g, rw_w0, rw_w2, rw_a0, rw_a2, rw_g2,
              rw_k_k, rw_k_a, rw_r_k, rw_ln_w, rw_ln_b, w_out, norm_ffn_g,
              router_grp_w, router_grp_b, router_exp_w, router_exp_b,
              exp_w_gate, exp_w_up, exp_w_down, final_norm_g):
    B, S, D = x.shape
    h = x
    for l in range(DEPTH):
        u = rmsnorm(h, norm_mix_g[l]) @ w_in[l]
        o_sb = sb_group(u[..., :SB_IN], sb_out_g[l])
        o_rw = rwkv7_group(u[..., SB_IN:], shift_mu[l], rw_w0[l], rw_w2[l], rw_a0[l], rw_a2[l],
                           rw_g2[l], rw_k_k[l], rw_k_a[l], rw_r_k[l], rw_ln_w[l], rw_ln_b[l])
        h = h + jnp.concatenate([o_sb, o_rw], axis=-1) @ w_out[l]
        xn = rmsnorm(h, norm_ffn_g[l]).reshape(B * S, D)
        y = hier_moe(xn, router_grp_w[l], router_grp_b[l], router_exp_w[l], router_exp_b[l],
                     exp_w_gate[l], exp_w_up[l], exp_w_down[l])
        h = h + y.reshape(B, S, D)
    return rmsnorm(h, final_norm_g)


CHUNK = 64

MIX_WIDTH = D_MODEL
HG_WIDTH = MIX_WIDTH // 2
HG_HEADS = 4
HG_DK = HG_WIDTH // HG_HEADS
FOX_WIDTH = MIX_WIDTH - HG_WIDTH
FOX_HEADS = 8
FOX_DH = FOX_WIDTH // FOX_HEADS
IN_COLS = 4 * HG_WIDTH + 3 * FOX_WIDTH + FOX_HEADS
N_EXPERT_GROUPS = 4
EXPERTS_PER_GROUP_2 = 4
N_EXPERTS_2 = N_EXPERT_GROUPS * EXPERTS_PER_GROUP_2
TOP_K = 2
EXPERT_HIDDEN = D_MODEL // 2
NORM_EPS = 1e-6
NEG_INF = -1e30


def rms_norm(x, gain):
    xf = x.astype(jnp.float32)
    y = xf * lax.rsqrt(jnp.mean(xf * xf, axis=-1, keepdims=True) + NORM_EPS)
    return (y * gain.astype(jnp.float32)).astype(x.dtype)

def hgrn2_mixer(q_raw, f_raw, i_raw, g_raw, lower_bound, norm_gain):
    B, S, _ = q_raw.shape
    nc = S // CHUNK
    f32 = jnp.float32
    q = jax.nn.silu(q_raw.astype(f32))
    lb = lower_bound.astype(f32)
    f = lb + (1.0 - lb) * jax.nn.sigmoid(f_raw.astype(f32))
    log_f = jnp.log(f)
    k = 1.0 - f
    v = i_raw.astype(f32)

    def to_chunks(t):
        return t.reshape(B, nc, CHUNK, HG_HEADS, HG_DK).transpose(1, 0, 3, 2, 4)

    causal = jnp.tril(jnp.ones((CHUNK, CHUNK), dtype=bool))

    def step(state, inp):
        qc, kc, vc, lfc = inp
        b = jnp.cumsum(lfc, axis=2)
        o_inter = jnp.einsum('bhtk,bhkv->bhtv', qc * jnp.exp(b), state)
        diff = b[:, :, :, None, :] - b[:, :, None, :, :]
        decay = jnp.where(causal[:, :, None], jnp.exp(jnp.minimum(diff, 0.0)), 0.0)
        scores = jnp.einsum('bhtk,bhtsk,bhsk->bhts', qc, decay, kc)
        o_intra = jnp.einsum('bhts,bhsv->bhtv', scores, vc)
        b_last = b[:, :, -1:, :]
        new_state = (jnp.exp(b_last[:, :, 0, :])[..., None] * state
                     + jnp.einsum('bhsk,bhsv->bhkv', kc * jnp.exp(b_last - b), vc))
        return new_state, o_inter + o_intra

    s0 = jnp.zeros((B, HG_HEADS, HG_DK, HG_DK), f32)
    _, o = lax.scan(step, s0, (to_chunks(q), to_chunks(k), to_chunks(v), to_chunks(log_f)))
    o = o.transpose(1, 0, 3, 2, 4).reshape(B, S, HG_HEADS, HG_DK)
    o = rms_norm(o, norm_gain)
    o = o.reshape(B, S, HG_WIDTH) * jax.nn.silu(g_raw.astype(f32))
    return o.astype(q_raw.dtype)

def fox_mixer(q_raw, k_raw, v_raw, f_raw, f_bias, norm_gain):
    B, S, _ = q_raw.shape
    f32 = jnp.float32

    def heads(t):
        return t.astype(f32).reshape(B, S, FOX_HEADS, FOX_DH).transpose(0, 2, 1, 3)

    q = heads(q_raw) * (FOX_DH ** -0.5)
    k = heads(k_raw)
    v = heads(v_raw)
    log_f = jax.nn.log_sigmoid(f_raw.astype(f32) + f_bias.astype(f32))
    cum = jnp.cumsum(log_f, axis=1).transpose(0, 2, 1)
    key_pos = jnp.arange(S)

    def block(i):
        start = i * Q_BLOCK
        qb = lax.dynamic_slice_in_dim(q, start, Q_BLOCK, axis=2)
        cb = lax.dynamic_slice_in_dim(cum, start, Q_BLOCK, axis=2)
        logits = jnp.einsum('bhtd,bhsd->bhts', qb, k) + (cb[..., :, None] - cum[..., None, :])
        mask = (start + jnp.arange(Q_BLOCK))[:, None] >= key_pos[None, :]
        logits = jnp.where(mask, logits, NEG_INF)
        p = jax.nn.softmax(logits, axis=-1)
        return jnp.einsum('bhts,bhsd->bhtd', p, v)

    o = lax.map(block, jnp.arange(S // Q_BLOCK))
    o = o.transpose(1, 0, 3, 2, 4).reshape(B, S, FOX_HEADS, FOX_DH)
    o = rms_norm(o, norm_gain)
    return o.reshape(B, S, FOX_WIDTH).astype(q_raw.dtype)

def hier_moe_2(x, w_group, b_group, w_expert, b_expert, w_gate, w_up, w_down):
    B, S, D = x.shape
    t = x.reshape(-1, D)
    pg = jax.nn.softmax((t @ w_group + b_group).astype(jnp.float32), axis=-1)
    gsel = jnp.argmax(pg, axis=-1)
    pg_sel = jnp.max(pg, axis=-1)
    e_logits = (t @ w_expert + b_expert).astype(jnp.float32).reshape(-1, N_EXPERT_GROUPS, EXPERTS_PER_GROUP_2)
    e_logits = jnp.take_along_axis(e_logits, gsel[:, None, None], axis=1)[:, 0]
    pe = jax.nn.softmax(e_logits, axis=-1)
    top_p, top_i = lax.top_k(pe, TOP_K)
    top_p = top_p / jnp.sum(top_p, axis=-1, keepdims=True)
    expert_id = gsel[:, None] * EXPERTS_PER_GROUP_2 + top_i
    weights = pg_sel[:, None] * top_p
    gates = jnp.sum(jax.nn.one_hot(expert_id, N_EXPERTS_2, dtype=jnp.float32) * weights[..., None], axis=1)
    gates = gates.astype(t.dtype)
    y = jnp.zeros_like(t)
    for e in range(N_EXPERTS_2):
        h = jax.nn.silu(t @ w_gate[e]) * (t @ w_up[e])
        y = y + gates[:, e:e + 1] * (h @ w_down[e])
    return y.reshape(B, S, D)

def second_inputs(seed: int = 0) -> dict:
    key = jax.random.key(seed)
    ks = jax.random.split(key, 20)
    f32 = jnp.float32
    L, D = DEPTH, D_MODEL
    nrm = lambda k, shape, scale: jax.random.normal(k, shape, f32) * scale
    return {
        "x": jax.random.normal(ks[0], (BATCH, SEQ, D), f32),
        "attn_norm": 1.0 + nrm(ks[1], (L, D), 0.02),
        "w_in": nrm(ks[2], (L, D, IN_COLS), D ** -0.5),
        "hg_lb_logits": nrm(ks[3], (L + 1, HG_WIDTH), 0.5),
        "hg_norm": 1.0 + nrm(ks[4], (L, HG_DK), 0.02),
        "fox_f_bias": nrm(ks[5], (L, FOX_HEADS), 0.1),
        "fox_norm": 1.0 + nrm(ks[6], (L, FOX_DH), 0.02),
        "w_out": nrm(ks[7], (L, MIX_WIDTH, D), MIX_WIDTH ** -0.5),
        "ffn_norm": 1.0 + nrm(ks[8], (L, D), 0.02),
        "w_group": nrm(ks[9], (L, D, N_EXPERT_GROUPS), D ** -0.5),
        "b_group": nrm(ks[10], (L, N_EXPERT_GROUPS), 0.01),
        "w_expert": nrm(ks[11], (L, D, N_EXPERTS_2), D ** -0.5),
        "b_expert": nrm(ks[12], (L, N_EXPERTS_2), 0.01),
        "w_gate": nrm(ks[13], (L, N_EXPERTS_2, D, EXPERT_HIDDEN), D ** -0.5),
        "w_up": nrm(ks[14], (L, N_EXPERTS_2, D, EXPERT_HIDDEN), D ** -0.5),
        "w_down": nrm(ks[15], (L, N_EXPERTS_2, EXPERT_HIDDEN, D), EXPERT_HIDDEN ** -0.5),
        "final_norm": 1.0 + nrm(ks[16], (D,), 0.02),
    }

def second_block(x, attn_norm, w_in, hg_lb_logits, hg_norm, fox_f_bias, fox_norm, w_out, ffn_norm,
              w_group, b_group, w_expert, b_expert, w_gate, w_up, w_down, final_norm):
    lb_all = jnp.cumsum(jax.nn.softmax(hg_lb_logits.astype(jnp.float32), axis=0), axis=0)
    o0 = 0
    o1 = o0 + HG_WIDTH
    o2 = o1 + HG_WIDTH
    o3 = o2 + HG_WIDTH
    o4 = o3 + HG_WIDTH
    o5 = o4 + FOX_WIDTH
    o6 = o5 + FOX_WIDTH
    o7 = o6 + FOX_WIDTH
    h = x
    for l in range(DEPTH):
        xn = rms_norm(h, attn_norm[l])
        u = xn @ w_in[l]
        o_a = hgrn2_mixer(u[..., o0:o1], u[..., o1:o2], u[..., o2:o3], u[..., o3:o4],
                          lb_all[l], hg_norm[l])
        o_b = fox_mixer(u[..., o4:o5], u[..., o5:o6], u[..., o6:o7], u[..., o7:IN_COLS],
                        fox_f_bias[l], fox_norm[l])
        h = h + jnp.concatenate([o_a, o_b], axis=-1) @ w_out[l]
        h = h + hier_moe_2(rms_norm(h, ffn_norm[l]), w_group[l], b_group[l], w_expert[l], b_expert[l],
                         w_gate[l], w_up[l], w_down[l])
    return rms_norm(h, final_norm)


def setup_inputs(seed=0):
    out = dict(first_inputs(seed))
    for name, value in second_inputs(seed + 1).items():
        if name != "x":
            out[name + "_2"] = value
    return out


def reference(
    x, norm_mix_g, w_in, shift_mu, sb_out_g, rw_w0, rw_w2, rw_a0, rw_a2, rw_g2, rw_k_k, rw_k_a,
    rw_r_k, rw_ln_w, rw_ln_b, w_out, norm_ffn_g, router_grp_w, router_grp_b, router_exp_w,
    router_exp_b, exp_w_gate, exp_w_up, exp_w_down, final_norm_g, attn_norm_2, w_in_2,
    hg_lb_logits_2, hg_norm_2, fox_f_bias_2, fox_norm_2, w_out_2, ffn_norm_2, w_group_2,
    b_group_2, w_expert_2, b_expert_2, w_gate_2, w_up_2, w_down_2, final_norm_2,
):
    x = first_block(
        x, norm_mix_g, w_in, shift_mu, sb_out_g, rw_w0, rw_w2, rw_a0, rw_a2, rw_g2, rw_k_k,
        rw_k_a, rw_r_k, rw_ln_w, rw_ln_b, w_out, norm_ffn_g, router_grp_w, router_grp_b,
        router_exp_w, router_exp_b, exp_w_gate, exp_w_up, exp_w_down, final_norm_g,
    )
    return second_block(
        x, attn_norm_2, w_in_2, hg_lb_logits_2, hg_norm_2, fox_f_bias_2, fox_norm_2, w_out_2,
        ffn_norm_2, w_group_2, b_group_2, w_expert_2, b_expert_2, w_gate_2, w_up_2, w_down_2,
        final_norm_2,
    )


_drawn_inputs = setup_inputs


def setup_inputs(seed=0):
    import zlib

    import numpy as np

    out = dict(_drawn_inputs(seed))
    spreads = {}
    factors = {'rw_w2': 3.358,
     'rw_k_k': 2.695,
     'rw_k_a': 2.86,
     'rw_ln_b': 2.962,
     'router_grp_b': 5.49,
     'router_exp_b': 3.545,
     'hg_norm_2': 5.109,
     'fox_norm_2': 3.688,
     'ffn_norm_2': 2.999,
     'b_group_2': 3.71,
     'b_expert_2': 22.606,
     'final_norm_2': 7.471}
    for name, (base, spread) in spreads.items():
        noise = np.random.default_rng([zlib.crc32(name.encode()), seed]).standard_normal(out[name].shape)
        drawn = base * np.exp(spread * noise) if base else spread * noise
        out[name] = __import__('jax').numpy.asarray(drawn.astype(out[name].dtype))
    for name, factor in factors.items():
        out[name] = (out[name] * factor).astype(out[name].dtype)
    return out
```

```python
from contextlib import ExitStack

import numpy as np

import concourse.bass as bass
from concourse import mybir

ALU = mybir.AluOpType
ACT = mybir.ActivationFunctionType
F32 = mybir.dt.float32
I32 = mybir.dt.int32
U32 = mybir.dt.uint32
AX_X = mybir.AxisListType.X

P = 128
S = 512
NT = S // P
D = 1024
DC = D // P
EPS = 1e-6
GN_EPS = 64e-5
HW = 512
HC = HW // P
CH = 64
NCH = S // CH
DECAY = float(np.exp(-0.5))
RING = 6144
LEVELS = (1, 2, 4, 8, 16, 32)


class Phase:

    def __init__(self, nc, name):
        self.nc, self.name, self.sems = nc, name, {}

    def sem(self, name):
        if name not in self.sems:
            self.sems[name] = self.nc.alloc_semaphore(f"{self.name}_{name}")
        return self.sems[name]

    def close(self):
        self.nc.clear_and_free_semaphores(list(self.sems.values()))
        self.nc.all_engine_barrier()


class Chain:

    def __init__(self, engine, sem):
        self.engine, self.sem, self.n = engine, sem, 0

    def mark(self, instruction):
        self.n += 1
        instruction.then_inc(self.sem, 1)
        return self.n

    def wait(self, n=None):
        self.engine.wait_ge(self.sem, self.n if n is None else n)

    def link(self, instruction):
        self.mark(instruction)
        self.wait()


class Memory:

    def __init__(self, nc, ctx):
        self.nc = nc

        def sb(name, shape, dt=F32):
            return ctx.enter_context(nc.sbuf_tensor(name, shape, dt))

        self.ring01 = sb("ring01", [P, 2, RING])
        self.mixT = sb("mixT", [P, DC, S])
        self.params = sb("params", [P, 96])
        self.ident = sb("ident", [P, P])
        self.masks = sb("masks", [P, len(LEVELS), P])
        self.m1low = sb("m1low", [P, P])
        self.tri3 = sb("tri3", [P, 3, P])
        self.after = sb("after", [P, P])
        self.negtri = sb("negtri", [P, P])
        self.negones = sb("negones", [P, P])
        self.ones = sb("ones", [P, P])
        self.same64 = sb("same64", [P, P])
        self.centre = sb("centre", [P, P])
        self.sel8 = sb("sel8", [8, 8, P])
        self.restart = sb("restart", [P, S])
        self.slots = sb("slots", [P, 2, P])
        self.experts = sb("experts", [P, 32])
        self.small = sb("small", [P, 64])
        self.rounds = sb("rounds", [P, 1], I32)
        arena = (229368 - 64 - nc.sbuf_base) // 4
        self.arena_size = arena
        self.arena = sb("arena", [P, arena])
        self.banks = [ctx.enter_context(nc.psum_tensor(f"bank{i}", [P, 512], F32)) for i in range(8)]

    def view(self, at, *shape, partitions=P, dt=None):
        n = int(np.prod(shape))
        assert at + n <= self.arena_size, (at, shape, self.arena_size)
        v = self.arena[0:partitions, at:at + n]
        if dt is not None:
            v = v.bitcast(dt)
        if len(shape) > 1:
            names = "abcdef"[:len(shape)]
            v = v.rearrange(f"p ({' '.join(names)}) -> p {' '.join(names)}", **dict(zip(names[1:], shape[1:])))
        return v, at + n


def bcast(ap, *shape):
    return ap.broadcast_to([ap.shape[0], *shape])


VECTORS = [("norm_mix_g", 8), ("shift_mu", 14), ("sb_out_g", 4), ("rw_w0", 4), ("rw_a0", 4), ("rw_k_k", 4),
           ("rw_k_a", 4), ("rw_r_k", 4), ("rw_ln_w", 4), ("rw_ln_b", 4), ("norm_ffn_g", 8),
           ("attn_norm_2", 8), ("hg_lb_logits_2", 8), ("hg_norm_2", 1), ("fox_norm_2", 1), ("ffn_norm_2", 8)]
COLUMN = {}
_at = 0
for _name, _n in VECTORS:
    COLUMN[_name] = _at
    _at += _n
NVEC = _at


def setup_phase(nc, m, io):
    ph = Phase(nc, "setup")
    raw, at = m.view(0, P)
    count, at = m.view(at, 2 * P, dt=I32)
    count2, at = m.view(at, 32, dt=I32)
    with nc.Block() as block:
        @block.sync
        def _(sp):
            for name, n in VECTORS:
                src = io[name]
                c = COLUMN[name]
                if name == "fox_norm_2":
                    for half in range(2):
                        sp.dma_start(raw[c:c + 1, 64 * half:64 * half + 64], src).then_inc(ph.sem("vectors"), 16)
                    continue
                if len(src.shape) == 3:
                    src = src.rearrange("l h d -> l (h d)")
                sp.dma_start(raw[c:c + n, :], src.rearrange("l (c p) -> (l c) p", p=P)).then_inc(ph.sem("vectors"), 16)

        @block.gpsimd
        def _(pool):
            g = Chain(pool, ph.sem("made"))

            def select(view, pattern, base, mult, op=ALU.is_ge, fill=0.0):
                g.link(pool.affine_select(out=view, in_=view, compare_op=op, fill=fill, base=base,
                                          pattern=pattern, channel_multiplier=mult))

            def same_block(t, n):
                v = t.rearrange("p (b c) -> p b c", c=n)
                select(v, [[-n, P // n], [0, n]], 0, 1)
                select(v, [[n, P // n], [0, n]], n - 1, -1)

            for t in (m.ident, m.masks, m.m1low, m.sel8):
                g.mark(pool.memset(t[:], 0.0))
            for t in (m.ones, m.same64, m.tri3, m.after, m.restart):
                g.mark(pool.memset(t[:], 1.0))
            g.mark(pool.memset(m.negones[:], -1.0))
            g.mark(pool.memset(m.negtri[:], -1.0))
            g.mark(pool.iota(count.rearrange("p (a b c) -> p a b c", a=2, b=2)[:, 0], [[0, 2], [1, 64]], base=0,
                             channel_multiplier=0))
            g.mark(pool.iota(count[:, P:2 * P], [[1, P]], base=0, channel_multiplier=0))
            g.link(pool.iota(count2, [[1, 32]], base=0, channel_multiplier=0))
            g.mark(pool.tensor_copy(m.slots[:].rearrange("p a b -> p (a b)"), count))
            g.mark(pool.tensor_copy(m.experts[:], count2))
            select(m.ident[:], [[-1, P]], 0, 1, ALU.not_equal, 1.0)
            select(m.sel8[:], [[-1, 8], [0, P]], 0, 1, ALU.not_equal, 1.0)
            for i, n in enumerate(LEVELS):
                v = m.masks[:, i, :].rearrange("p (b c) -> p b c", c=2 * n)
                g.link(pool.memset(v[:, :, n:2 * n], 1.0))
                select(v, [[-2 * n, P // (2 * n)], [0, 2 * n]], 0, 1)
                select(v, [[2 * n, P // (2 * n)], [0, 2 * n]], n - 1, -1)
            v = m.m1low[:].rearrange("p (b c) -> p b c", c=2)
            g.link(pool.memset(v[:, :, 0:1], 1.0))
            select(v, [[-2, P // 2], [0, 2]], -1, 1)
            select(v, [[2, P // 2], [0, 2]], 1, -1)
            same_block(m.same64[:], 64)
            for i in range(3):
                same_block(m.tri3[:, i, :], CH)
            select(m.tri3[:, 0, :], [[1, P]], -1, -1)
            select(m.tri3[:, 1, :], [[1, P]], 0, -1)
            select(m.tri3[:, 2, :], [[-1, P]], -1, 1)
            select(m.after[:], [[1, P]], -1, -1)
            select(m.negtri[:], [[-1, P]], 0, 1)
            v = m.restart[:].rearrange("p (b c) -> p b c", c=CH)
            g.link(pool.memset(v[:, :, 0:1], 0.0))
            pool.memset(m.small[:], 0.0).then_inc(ph.sem("constants"), 1)

        @block.vector
        def _(dve):
            v = Chain(dve, ph.sem("dve"))
            dve.wait_ge(ph.sem("constants"), 1)
            v.link(dve.tensor_scalar(m.centre[:], m.same64[:], -1.0 / 64, None, ALU.mult))
            v.link(dve.tensor_tensor(m.centre[:], m.centre[:], m.ident[:], ALU.add))
            dve.wait_ge(ph.sem("turned"), 1)
            v.link(dve.tensor_copy(m.params[:, 0:NVEC], m.banks[0][:, 0:NVEC]))

        @block.tensor
        def _(pe):
            pe.wait_ge(ph.sem("constants"), 1)
            pe.wait_ge(ph.sem("vectors"), 16 * (len(VECTORS) + 1))
            pe.transpose(m.banks[0][:, 0:NVEC], raw[0:NVEC, :], m.ident[0:NVEC, 0:NVEC]).then_inc(ph.sem("turned"), 1)
    ph.close()


def weight_item(sp, m, ring_sem, n, src, cols):
    v = m.ring01[:, n % 2, 0:DC * cols].rearrange("p (c n) -> p c n", n=cols)
    s = src.rearrange("(c p) n -> p c n", p=P)
    for a, b in ((0, 3), (3, 6), (6, 8)):
        sp.dma_start(v[:, a:b, :], s[:, a:b, :]).then_inc(ring_sem(n % 2), 16)


def item_view(m, n, cols):
    return m.ring01[:, n % 2, 0:DC * cols].rearrange("p (c n) -> p c n", n=cols)
def norm_act(act, ph, m, rows, scaled, arrived):
    for t in range(NT):
        arrived(act, t)
        act.activation(scaled[:, t, :], rows[:, t, :], ACT.Square, accum_out=m.small[:, t:t + 1]).then_inc(ph.sem("squares"), 1)
    act.wait_ge(ph.sem("mean"), 1)
    act.activation(m.small[:, 8:12], m.small[:, 4:8], ACT.Sqrt).then_inc(ph.sem("deviation"), 1)


def norm_scale_dve(dve, ph, m, rows, scaled, v):
    dve.wait_ge(ph.sem("squares"), NT)
    dve.tensor_scalar(m.small[:, 4:8], m.small[:, 0:4], 1.0 / D, EPS, ALU.mult, ALU.add).then_inc(ph.sem("mean"), 1)
    dve.wait_ge(ph.sem("deviation"), 1)
    v.link(dve.reciprocal(m.small[:, 12:16], m.small[:, 8:12]))
    for t in range(NT):
        dve.tensor_scalar(scaled[:, t, :], rows[:, t, :], m.small[:, 12 + t:13 + t], None, ALU.mult).then_inc(ph.sem("scaled"), 1)


def norm_turn_pe(pe, ph, m, scaled):
    for t in range(NT):
        pe.wait_ge(ph.sem("scaled"), t + 1)
        for half in range(2):
            for j in range(4):
                c = 4 * half + j
                last = pe.transpose(m.banks[2 * t + half][:, j * P:(j + 1) * P], scaled[:, t, c * P:(c + 1) * P], m.ident[:])
            last.then_inc(ph.sem("turned"), 1)


def norm_gain_dve(dve, ph, m, gain):
    for t in range(NT):
        for half in range(2):
            dve.wait_ge(ph.sem("turned"), 2 * t + half + 1)
            g = m.params[:, gain + 4 * half:gain + 4 * half + 4].unsqueeze(2).broadcast_to([P, 4, P])
            dve.tensor_tensor(m.mixT[:, 4 * half:4 * half + 4, t * P:(t + 1) * P],
                              m.banks[2 * t + half][:].rearrange("p (a b) -> p a b", b=P), g,
                              ALU.mult).then_inc(ph.sem("normed"), 1)


NORMED = 2 * NT


def project_pe(pe, ph, m, n, cols, chunks, first, ring_count, rows_form):
    w = item_view(m, n, cols)
    pe.wait_ge(ph.sem(f"ring{n % 2}"), ring_count)
    for i in range(chunks):
        k = first + i
        bank = m.banks[k % 6]
        if k >= 6:
            pe.wait_ge(ph.sem("taken"), k - 5)
        for c in range(DC):
            if rows_form:
                last = pe.matmul(bank[:, 0:4 * P], m.mixT[:, c, i * P:(i + 1) * P], w[:, c, 0:4 * P],
                                 start=(c == 0), stop=(c == DC - 1))
            else:
                last = pe.matmul(bank[:], w[:, c, i * P:(i + 1) * P], m.mixT[:, c, :],
                                 start=(c == 0), stop=(c == DC - 1))
        last.then_inc(ph.sem("projected"), 1)


class Mix1:

    def __init__(self, m):
        at = 0
        self.k, at = m.view(at, HC, S + 1)
        self.r, at = m.view(at, HC, S + 1)
        self.v_at = at
        self.v, at = m.view(at, HC, S + 1)
        self.x, at = m.view(at, 2, S + 1)
        self.ar, at = m.view(at, HC, NT, 2, P)
        self.ar_flat = self.ar.rearrange("p a b c d -> p (a b c d)")
        self.kk, at = m.view(at, HC, S)
        self.bonus = self.r
        self.dc, at = m.view(at, HC, NCH)
        self.free1 = at
        self.w1, at = m.view(at, HC, S)
        self.w2, at = m.view(at, HC, S)
        self.a, at = m.view(at, HC, S)
        self.sc, at = m.view(at, HC, S)
        self.tmp, at = m.view(at, 2, S)
        self.lw, at = m.view(at, S)
        self.omka, at = m.view(at, HC)
        self.sb = at
        self.q, at = m.view(at, HC, S)
        self.kb, at = m.view(at, HC, S)
        self.vb, at = m.view(at, NT, HW)
        self.end = at
        self.rows, end = m.view(self.free1, NT, D)
        self.scaled, end = m.view(end, NT, D)


def phase_project1(nc, m, io, g2s):
    ph = Phase(nc, "p1")
    x = Mix1(m)
    w_in = io["w_in"].rearrange("l d n -> (l d) n")
    SB = 3 * HW
    items = [[(SB + 3 * HW, 256), (SB + 2 * HW, HW)], [(SB + HW, HW)], [(SB, HW)], [(0, HW)], [(HW, HW)], [(2 * HW, HW)]]
    sizes = [6, 4, 4, 4, 4, 4]
    first = [sum(sizes[:i]) for i in range(6)]
    mu = COLUMN["shift_mu"]
    dest = [(x.x, 0, mu + 12), (x.x, 1, mu + 13)] + [(x.v, c, mu + 8 + c) for c in range(4)] \
        + [(x.k, c, mu + 4 + c) for c in range(4)] + [(x.r, c, mu + c) for c in range(4)]
    col = lambda name, c: m.params[:, COLUMN[name] + c:COLUMN[name] + c + 1]
    cols4 = lambda name: m.params[:, COLUMN[name]:COLUMN[name] + 4].unsqueeze(2).broadcast_to([P, 4, S])
    K, R, V = x.k[:, :, 1:], x.r[:, :, 1:], x.v[:, :, 1:]
    A4 = x.ar[:, :, :, 0, :]
    R4 = x.ar[:, :, :, 1, :]
    t4 = lambda ap: ap.rearrange("p a (t n) -> p a t n", n=P)

    with nc.Block() as block:
        @block.sync
        def _(sp):
            xin = io["x"].rearrange("b (t p) d -> p (b t) d", p=P)
            for t in range(NT):
                sp.dma_start(x.rows[:, t, :], xin[:, t, :]).then_inc(ph.sem("rows"), 16)
            for n, parts in enumerate(items):
                if n >= 2:
                    sp.wait_ge(ph.sem("projected"), first[n - 1])
                at = 0
                width = sum(w for _, w in parts)
                v = item_view(m, n, width)
                for c0, w in parts:
                    src = w_in[:, c0:c0 + w].rearrange("(c p) n -> p c n", p=P)
                    for a, b in ((0, 4), (4, 8)):
                        sp.dma_start(v[:, a:b, at:at + w], src[:, a:b, :]).then_inc(ph.sem(f"ring{n % 2}"), 16)
                    at += w
                if n == 0:
                    sp.dma_start(x.lw[0:64, :], io["rw_w2"][0]).then_inc(ph.sem("low"), 16)
                    sp.dma_start(x.lw[64:128, :], io["rw_a2"][0]).then_inc(ph.sem("low"), 16)
                    sp.dma_start(g2s, io["rw_g2"][0]).then_inc(ph.sem("low"), 16)
            sp.wait_ge(ph.sem("low"), 48)

        ring_counts = [64, 32, 96, 64, 128, 96]

        @block.scalar
        def _(act):
            a = Chain(act, ph.sem("act"))
            norm_act(act, ph, m, x.rows, x.scaled, lambda e, t: e.wait_ge(ph.sem("rows"), 64))

            def take(k):
                act.wait_ge(ph.sem("projected"), k + 1)
                bank = m.banks[k % 6][:]
                if k < 14:
                    out, scale = dest[k][0][:, dest[k][1], 1:], 1.0
                elif k < 18:
                    out, scale = x.q[:, k - 14, :], 0.125
                elif k < 22:
                    out, scale = x.kb[:, k - 18, :], 1.0
                else:
                    out, scale = x.vb[:, k - 22, :], 1.0
                act.activation(out, bank, ACT.Copy, scale=scale).then_inc(ph.sem("taken"), 1)

            for k in range(10):
                take(k)
            act.wait_ge(ph.sem("mixed"), 1)
            act.activation(x.x[0:64, 0, 1:], x.x[0:64, 0, 1:], ACT.Tanh).then_inc(ph.sem("low_in"), 1)
            act.wait_ge(ph.sem("mixed"), 2)
            a.mark(act.activation(x.x[:, 1, 1:], x.x[:, 1, 1:], ACT.Sigmoid))
            for c in range(HC):
                act.wait_ge(ph.sem("low_out"), 2 * c + 1)
                act.activation(x.w1[:, c, :], m.banks[6][:], ACT.Sigmoid, bias=col("rw_w0", c)).then_inc(ph.sem("gates"), 1)
                act.wait_ge(ph.sem("low_out"), 2 * c + 2)
                act.activation(x.a[:, c, :], m.banks[7][:], ACT.Sigmoid, bias=col("rw_a0", c)).then_inc(ph.sem("gates"), 1)
            for k in range(10, 14):
                take(k)
            act.wait_ge(ph.sem("kk"), 1)
            act.activation(x.sc[:], x.kk[:], ACT.Square).then_inc(ph.sem("kk_squares"), 1)
            act.wait_ge(ph.sem("kk_bounded"), HC)
            act.activation(x.sc[:], x.sc[:], ACT.Sqrt).then_inc(ph.sem("kk_length"), 1)
            act.wait_ge(ph.sem("cumulated"), 1)
            for c in range(HC):
                act.activation(A4[:, c], t4(x.w1)[:, c], ACT.Exp).then_inc(ph.sem("decays"), 1)
                act.activation(R4[:, c], t4(x.w2)[:, c], ACT.Exp).then_inc(ph.sem("decays"), 1)
            ends = x.w2.rearrange("p a (c n) -> p a c n", n=CH)[:, :, :, CH - 1]
            a.link(act.activation(x.dc[:], ends, ACT.Exp))
            act.activation(x.w2[:], x.w2[:], ACT.Exp, scale=-1.0).then_inc(ph.sem("inverse"), 1)
            for k in range(14, 26):
                take(k)

        @block.vector
        def _(dve):
            v = Chain(dve, ph.sem("dve"))
            for t in (x.k, x.r, x.v, x.x):
                v.mark(dve.memset(t[:, :, 0:1], 0.0))
            norm_scale_dve(dve, ph, m, x.rows, x.scaled, v)
            norm_gain_dve(dve, ph, m, COLUMN["norm_mix_g"])

            def shift(k):
                buf, c, mu_col = dest[k]
                dve.wait_ge(ph.sem("taken"), k + 1)
                if k >= 2:
                    dve.wait_ge(ph.sem("mixed"), k - 1)
                v.link(dve.tensor_tensor(x.tmp[:, k % 2, :], buf[:, c, 0:S], buf[:, c, 1:], ALU.subtract))
                dve.scalar_tensor_tensor(buf[:, c, 1:], x.tmp[:, k % 2, :], m.params[:, mu_col:mu_col + 1],
                                         buf[:, c, 1:], ALU.mult, ALU.add).then_inc(ph.sem("mixed"), 1)

            v.wait()
            for k in range(10):
                shift(k)
            dve.wait_ge(ph.sem("mixed"), 10)
            dve.tensor_tensor(x.kk[:], K, cols4("rw_k_k"), ALU.mult).then_inc(ph.sem("kk"), 1)
            v.link(dve.tensor_scalar(x.omka[:], m.params[:, COLUMN["rw_k_a"]:COLUMN["rw_k_a"] + 4], -1.0, 1.0, ALU.mult, ALU.add))
            dve.wait_ge(ph.sem("gates"), 2 * HC)
            v.link(dve.tensor_scalar(x.w1[:], x.w1[:], -DECAY, None, ALU.mult))
            for c in range(HC):
                v.mark(dve.tensor_tensor_scan(x.w2[:, c, :], m.restart[:], x.w1[:, c, :], 0.0, ALU.mult, ALU.add))
            v.wait()
            dve.tensor_tensor(x.w1[:], x.w2[:], x.w1[:], ALU.subtract).then_inc(ph.sem("cumulated"), 1)
            for c in range(HC):
                dve.wait_ge(ph.sem("kk_sums"), c + 1)
                dve.tensor_scalar(x.sc[:, c, :], m.banks[6 + c % 2][:], 1e-24, None, ALU.max).then_inc(ph.sem("kk_bounded"), 1)
            dve.wait_ge(ph.sem("kk_length"), 1)
            v.link(dve.reciprocal(x.sc[:], x.sc[:]))
            v.link(dve.tensor_tensor(x.kk[:], x.kk[:], x.sc[:], ALU.mult))
            for c in range(HC):
                v.mark(dve.tensor_scalar(x.sc[:, c, :], x.a[:, c, :], col("rw_k_a", c), x.omka[:, c:c + 1], ALU.mult, ALU.add))
            v.wait()
            v.link(dve.tensor_tensor(K, K, x.sc[:], ALU.mult))
            for k in range(10, 14):
                shift(k)
            dve.wait_ge(ph.sem("mixed"), 14)
            for c in range(HC):
                dve.scalar_tensor_tensor(x.sc[:, c, :], R[:, c, :], col("rw_r_k", c), K[:, c, :], ALU.mult,
                                         ALU.mult).then_inc(ph.sem("rk"), 1)
            dve.wait_ge(ph.sem("decays"), 2 * HC)
            for c in range(HC):
                v.mark(dve.scalar_tensor_tensor(A4[:, c], t4(x.kk)[:, c], -1.0, A4[:, c], ALU.mult, ALU.mult))
                v.mark(dve.tensor_tensor(R4[:, c], t4(R)[:, c], R4[:, c], ALU.mult))
            v.wait()
            v.link(dve.tensor_tensor(x.kk[:], x.kk[:], x.a[:], ALU.mult))
            dve.wait_ge(ph.sem("inverse"), 1)
            v.mark(dve.tensor_tensor(x.kk[:], x.kk[:], x.w2[:], ALU.mult))
            dve.wait_ge(ph.sem("rk"), HC)
            v.mark(dve.tensor_tensor(K, K, x.w2[:], ALU.mult))
            for c in range(HC):
                dve.wait_ge(ph.sem("bonus"), c + 1)
                dve.tensor_tensor(x.bonus[:, c, 1:], m.banks[6 + c % 2][:], V[:, c, :], ALU.mult).then_inc(ph.sem("bonus_taken"), 1)

        @block.tensor
        def _(pe):
            norm_turn_pe(pe, ph, m, x.scaled)
            pe.wait_ge(ph.sem("normed"), NORMED)

            def item(n):
                project_pe(pe, ph, m, n, sum(w for _, w in items[n]), sizes[n], first[n], ring_counts[n], n == 5)

            item(0)
            item(1)
            pe.wait_ge(ph.sem("low"), 48)
            pe.wait_ge(ph.sem("low_in"), 1)
            for c in range(HC):
                for half in range(2):
                    if c:
                        pe.wait_ge(ph.sem("gates"), 2 * c - 1 + half)
                    o = 64 * half
                    pe.matmul(m.banks[6 + half][:], x.lw[o:o + 64, c * P:(c + 1) * P], x.x[o:o + 64, 0, 1:],
                              start=True, stop=True).then_inc(ph.sem("low_out"), 1)
            item(2)
            pe.wait_ge(ph.sem("gates"), 2 * HC)
            pe.wait_ge(ph.sem("kk_squares"), 1)
            for c in range(HC):
                if c >= 2:
                    pe.wait_ge(ph.sem("kk_bounded"), c - 1)
                pe.matmul(m.banks[6 + c % 2][:], m.same64[:], x.sc[:, c, :], start=True, stop=True).then_inc(ph.sem("kk_sums"), 1)
            item(3)
            pe.wait_ge(ph.sem("rk"), HC)
            for c in range(HC):
                if c >= 2:
                    pe.wait_ge(ph.sem("bonus_taken"), c - 1)
                pe.matmul(m.banks[6 + c % 2][:], m.same64[:], x.sc[:, c, :], start=True, stop=True).then_inc(ph.sem("bonus"), 1)
            item(4)
            item(5)
    ph.close()
Z_PLACE = [(0, 0), (1, 0), (2, 0), (1, 384)]
Z_FLAT = [0, 512, 1024, 896]
Z_BANKS = [(0, 512), (512, 512), (1024, 256)]


def phase_stick(nc, m, x):
    ph = Phase(nc, "sb")
    heads = 2 * HC
    at = x.free1
    sp2, at = m.view(at, 2, 1280)
    wt2, at = m.view(at, 2, 1280)
    sq, at = m.view(x.free1, HC, S)
    assert at <= x.sb

    def qk(t, h):
        return t[64 * (h % 2):64 * (h % 2) + 64, h // 2, :]

    def zbank(h, i):
        return m.banks[3 * (h % 2) + i]

    def z_region(h, c, t0=None):
        t0 = c if t0 is None else t0
        b, o = Z_PLACE[c]
        return zbank(h, b)[:, o + (t0 - c) * P:o + S - c * P]

    with nc.Block() as block:
        @block.tensor
        def _(pe):
            def scores(h):
                if h >= 2:
                    pe.wait_ge(ph.sem("weights"), 3 * (h - 1))
                for c in (0, 1, 2, 3):
                    last = pe.matmul(z_region(h, c), qk(x.kb, h)[:, c * P:(c + 1) * P], qk(x.q, h)[:, c * P:],
                                     start=(c != 3), stop=True, skip_group_check=True)
                last.then_inc(ph.sem("scores"), 1)

            def suffixes(h):
                pe.wait_ge(ph.sem("masked"), 2 * (h + 1))
                sp = sp2[:, h % 2, :]
                for c in range(NT):
                    for j in range(c, NT):
                        last = pe.matmul(z_region(h, c, j), (m.negtri if j == c else m.negones)[:],
                                         sp[:, Z_FLAT[j]:Z_FLAT[j] + S - j * P], start=False, stop=True,
                                         skip_group_check=True)
                last.then_inc(ph.sem("exponents"), 1)

            def values(h):
                pe.wait_ge(ph.sem("causal"), 2 * (h + 1))
                if h >= 4 and h % 2 == 0:
                    pe.wait_ge(ph.sem("output"), h // 2 - 1)
                o = 64 * (h % 2)
                w = wt2[:, h % 2, :]
                for c in range(NT):
                    last = pe.matmul(m.banks[6 + h // 2 % 2][o:o + 64, c * P:], x.vb[:, c, 64 * h:64 * h + 64],
                                     w[:, Z_FLAT[c]:Z_FLAT[c] + S - c * P], start=(c == 0), stop=(c == NT - 1),
                                     skip_group_check=True)
                last.then_inc(ph.sem("values"), 1)

            scores(0)
            for h in range(heads):
                if h + 1 < heads:
                    scores(h + 1)
                suffixes(h)
                if h >= 1:
                    values(h - 1)
            values(heads - 1)
            for p in range(HC):
                pe.wait_ge(ph.sem("squared"), p + 1)
                pe.matmul(m.banks[p][:], m.same64[:], sq[:, p, :], start=True, stop=True).then_inc(ph.sem("sums"), 1)

        @block.scalar
        def _(act):
            def softplus(h):
                act.wait_ge(ph.sem("scores"), h + 1)
                if h >= 2:
                    act.wait_ge(ph.sem("exponents"), h - 1)
                sp = sp2[:, h % 2, :]
                for i, (o, n) in enumerate(Z_BANKS):
                    act.activation(sp[:, o:o + n], zbank(h, i)[:, 0:n], ACT.Abs).then_inc(ph.sem("abs"), 1)
                act.wait_ge(ph.sem("abs"), 3 * (h + 1))
                act.activation(sp, sp, ACT.Exp, scale=-1.0).then_inc(ph.sem("exp"), 1)
                act.wait_ge(ph.sem("exp"), h + 1)
                act.activation(sp, sp, ACT.Ln, bias=1.0).then_inc(ph.sem("ln"), 1)

            def weights(h):
                act.wait_ge(ph.sem("exponents"), h + 1)
                if h >= 2:
                    act.wait_ge(ph.sem("values"), h - 1)
                for i, (o, n) in enumerate(Z_BANKS):
                    act.activation(wt2[:, h % 2, o:o + n], zbank(h, i)[:, 0:n], ACT.Exp).then_inc(ph.sem("weights"), 1)

            def output(p):
                act.wait_ge(ph.sem("values"), 2 * p + 2)
                act.activation(m.mixT[:, p, :], m.banks[6 + p % 2][:], ACT.Copy).then_inc(ph.sem("output"), 1)

            softplus(0)
            for h in range(heads):
                if h + 1 < heads:
                    softplus(h + 1)
                weights(h)
                if h >= 3 and h % 2 == 1:
                    output((h - 3) // 2)
            output(HC - 1)
            act.wait_ge(ph.sem("output"), HC)
            for p in range(HC):
                act.activation(sq[:, p, :], m.mixT[:, p, :], ACT.Square).then_inc(ph.sem("squared"), 1)
            act.wait_ge(ph.sem("mean"), HC)
            act.activation(sq[:], sq[:], ACT.Sqrt).then_inc(ph.sem("deviation"), 1)

        @block.vector
        def _(dve):
            v = Chain(dve, ph.sem("dve"))
            diagonal = m.after[:].unsqueeze(1).broadcast_to([P, 3, P])
            for h in range(heads):
                dve.wait_ge(ph.sem("ln"), h + 1)
                sp = sp2[:, h % 2, :]
                for i, (o, n) in enumerate(Z_BANKS):
                    v.mark(dve.scalar_tensor_tensor(sp[:, o:o + n], zbank(h, i)[:, 0:n], 0.0, sp[:, o:o + n], ALU.max, ALU.add))
                v.wait()
                d3 = sp.rearrange("p (a b) -> p a b", b=256)[:, 0:5:2, 0:P]
                dve.tensor_tensor(d3, d3, diagonal, ALU.mult).then_inc(ph.sem("masked"), 1)
                d1 = sp[:, Z_FLAT[3]:Z_FLAT[3] + P]
                dve.tensor_tensor(d1, d1, m.after[:], ALU.mult).then_inc(ph.sem("masked"), 1)
            for p in range(HC):
                dve.wait_ge(ph.sem("sums"), p + 1)
                dve.tensor_scalar(sq[:, p, :], m.banks[p][:], 1.0 / 64, EPS, ALU.mult, ALU.add).then_inc(ph.sem("mean"), 1)
            dve.wait_ge(ph.sem("deviation"), 1)
            v.link(dve.reciprocal(sq[:], sq[:]))
            g = COLUMN["sb_out_g"]
            for p in range(HC):
                v.mark(dve.scalar_tensor_tensor(m.mixT[:, p, :], m.mixT[:, p, :], m.params[:, g + p:g + p + 1], sq[:, p, :],
                                                ALU.mult, ALU.mult))
            v.wait()

        @block.gpsimd
        def _(pool):
            for h in range(heads):
                pool.wait_ge(ph.sem("weights"), 3 * (h + 1))
                w = wt2[:, h % 2, :]
                d3 = w.rearrange("p (a b) -> p a b", b=256)[:, 0:5:2, 0:P]
                pool.affine_select(out=d3, in_=d3, compare_op=ALU.is_gt, fill=0.0, base=0, pattern=[[0, 3], [1, P]],
                                   channel_multiplier=-1).then_inc(ph.sem("causal"), 1)
                d1 = w[:, Z_FLAT[3]:Z_FLAT[3] + P]
                pool.affine_select(out=d1, in_=d1, compare_op=ALU.is_gt, fill=0.0, base=0, pattern=[[1, P]],
                                   channel_multiplier=-1).then_inc(ph.sem("causal"), 1)
    ph.close()


def phase_rwkv(nc, m, x, g2s):
    ph = Phase(nc, "rw")
    at = x.free1
    brow, at = m.view(at, HC, NT, P)
    krow, at = m.view(at, HC, NT, P)
    vrow, at = m.view(at, HC, NT, P)
    rb, at = m.view(at, HC, 2, NT, P)
    st, at = m.view(at, NCH + 1, HC, 64)
    lt, at = m.view(at, 2, NT, P)
    lo, at = m.view(at, 2, NT, P)
    mk, at = m.view(at, 2, NT, 2, P)
    tt, at = m.view(at, 2, 2, NT, P)
    assert at <= m.arena_size - S, (at, m.arena_size)
    flat = x.v_at
    xp, flat = m.view(flat, 2, NT, P)
    arow, flat = m.view(flat, NT, P)
    w1, flat = m.view(flat, 2, NT, 64)
    sq, _ = m.view(x.free1, HC, S)
    oc, _ = m.view(x.free1 + HC * S, HC, S)
    A4, R4 = x.ar[:, :, :, 0, :], x.ar[:, :, :, 1, :]
    K = x.k[:, :, 1:]
    uw = x.kk
    uw4 = uw.rearrange("p a (t n) -> p a t n", n=P)
    ident4 = m.ident[:].unsqueeze(1).broadcast_to([P, NT, P])
    mask4 = lambda t: t.unsqueeze(1).broadcast_to([P, NT, P])
    bank4 = lambda i: m.banks[i][:].rearrange("p (t n) -> p t n", n=P)
    levels = len(LEVELS)

    with nc.Block() as block:
        @block.tensor
        def _(pe):
            i = 0
            for p in range(HC):
                for src in (x.kk[:, p, :], K[:, p, :], x.v[:, p, 1:]):
                    if i >= 6:
                        pe.wait_ge(ph.sem("rows"), i - 5)
                    for t in range(NT):
                        last = pe.transpose(m.banks[i % 6][:, t * P:(t + 1) * P], src[:, t * P:(t + 1) * P], m.ident[:])
                    last.then_inc(ph.sem("turned"), 1)
                    i += 1
            pe.wait_ge(ph.sem("rows"), 3 * HC)
            for p in range(HC):
                if p:
                    pe.wait_ge(ph.sem("post"), 4 * p)
                for t in range(NT):
                    last = pe.transpose(m.banks[6][:, t * P:(t + 1) * P], A4[:, p, t, :], m.ident[:])
                last.then_inc(ph.sem("arow"), 1)
                for q in range(2):
                    o = 64 * q
                    for t in range(NT):
                        u = NT * q + t
                        if u >= 2:
                            pe.wait_ge(ph.sem("products_taken"), 4 * (2 * NT * p + u - 1))
                        e0, e1 = m.banks[2 * (u % 2)], m.banks[2 * (u % 2) + 1]
                        b = x.kk[o:o + 64, p, t * P:(t + 1) * P]
                        k = K[o:o + 64, p, t * P:(t + 1) * P]
                        ar = x.ar[o:o + 64, p, t, :, :].rearrange("p a b -> p (a b)")
                        pe.matmul(e0[:, 0:2 * P], b, ar, start=True, stop=True)
                        pe.matmul(e0[:, 2 * P:3 * P], A4[o:o + 64, p, t, :], b, start=True, stop=True)
                        pe.matmul(e1[:, 0:2 * P], k, ar, start=True, stop=True).then_inc(ph.sem("products"), 1)
                pe.wait_ge(ph.sem("products_taken"), 4 * 2 * NT * (p + 1))
                for n in range(1, levels):
                    for q in range(2):
                        done = p * (levels - 1) + n - 1
                        pe.wait_ge(ph.sem(f"part{q}"), done + 1)
                        if n > 1:
                            pe.wait_ge(ph.sem(f"inverse{q}"), 2 * done - p)
                        else:
                            pe.wait_ge(ph.sem(f"first{q}"), 2 * (p + 1))
                        for t in range(NT):
                            last = pe.matmul(m.banks[4 + q][:, t * P:(t + 1) * P], lo[:, q, t, :], tt[:, q, 0, t, :],
                                             start=True, stop=True)
                        last.then_inc(ph.sem(f"lt{q}"), 1)
                    for q in range(2):
                        done = p * (levels - 1) + n - 1
                        pe.wait_ge(ph.sem(f"xp{q}"), done + 1)
                        if n < levels - 1:
                            for t in range(NT):
                                last = pe.matmul(m.banks[2 * q][:, t * P:(t + 1) * P], tt[:, q, 1, t, :], xp[:, q, t, :],
                                                 start=True, stop=True)
                            last.then_inc(ph.sem(f"merged{q}"), 1)
                        for t in range(NT):
                            last = pe.matmul(m.banks[2 * q + 1][:, t * P:(t + 1) * P], xp[:, q, t, :], tt[:, q, 1, t, :],
                                             start=True, stop=True)
                        last.then_inc(ph.sem(f"merged{q}"), 1)
                per_pair = 2 * (levels - 1) - 1
                pe.wait_ge(ph.sem("inverse0"), per_pair * (p + 1))
                pe.wait_ge(ph.sem("inverse1"), per_pair * (p + 1))
                pe.wait_ge(ph.sem("arow_taken"), p + 1)
                for q in range(2):
                    for t in range(NT):
                        last = pe.matmul(m.banks[6][:, (NT * q + t) * 64:(NT * q + t + 1) * 64], mk[:, q, t, 0, :],
                                         vrow[:, p, t, 64 * q:64 * q + 64], start=True, stop=True)
                last.then_inc(ph.sem("mv"), 1)
                for q in range(2):
                    for t in range(NT):
                        last = pe.matmul(m.banks[4][64 * q:64 * q + 64, t * P:(t + 1) * P], arow[:, t, 64 * q:64 * q + 64],
                                         tt[:, q, 1, t, :], start=True, stop=True)
                last.then_inc(ph.sem("ta"), 1)
                for q in range(2):
                    for t in range(NT):
                        last = pe.matmul(m.banks[5][64 * q:64 * q + 64, t * P:(t + 1) * P], vrow[:, p, t, 64 * q:64 * q + 64],
                                         mk[:, q, t, 1, :], start=True, stop=True)
                last.then_inc(ph.sem("rkv"), 1)
                pe.wait_ge(ph.sem("post"), 4 * p + 1)
                for q in range(2):
                    for t in range(NT):
                        last = pe.matmul(m.banks[7][:, (NT * q + t) * 64:(NT * q + t + 1) * 64], tt[:, q, 1, t, :],
                                         w1[:, q, t, :], start=True, stop=True)
                last.then_inc(ph.sem("tmv"), 1)
            pe.wait_ge(ph.sem("post"), 4 * HC)
            for c in range(NCH):
                b, t = 64 * (c % 2), c // 2
                sbank = m.banks[2 + c % 2]
                pe.wait_ge(ph.sem("state"), 2 * c + 1)
                for q in range(2):
                    for p in range(HC):
                        last = pe.matmul(m.banks[q][b:b + 64, p * 64:(p + 1) * 64],
                                         A4[64 * q:64 * q + 64, p, t, b:b + 64], st[64 * q:64 * q + 64, c, p, :],
                                         start=True, stop=True)
                last.then_inc(ph.sem("u"), 1)
                for q in range(2):
                    for p in range(HC):
                        pe.matmul(sbank[64 * q:64 * q + 64, p * 64:(p + 1) * 64], krow[b:b + 64, p, t, 64 * q:64 * q + 64],
                                  vrow[b:b + 64, p, t, 64 * q:64 * q + 64], start=(p == 0), stop=True, skip_group_check=True)
                pe.wait_ge(ph.sem("u_done"), 2 * c + 2)
                for q in range(2):
                    for p in range(HC):
                        last = pe.matmul(sbank[64 * q:64 * q + 64, p * 64:(p + 1) * 64], brow[b:b + 64, p, t, 64 * q:64 * q + 64],
                                         uw4[b:b + 64, p, t, 64 * q:64 * q + 64], start=False, stop=True, skip_group_check=True)
                last.then_inc(ph.sem("s"), 1)
            pe.wait_ge(ph.sem("state"), 2 * NCH)
            for p in range(HC):
                for q in range(2):
                    o = 64 * q
                    for t in range(NT):
                        out = m.banks[4 + p][o:o + 64, t * P:(t + 1) * P]
                        pe.matmul(out, uw4[:, p, t, o:o + 64], rb[:, p, q, t, :], start=True, stop=True, skip_group_check=True)
                        for half in range(2):
                            last = pe.matmul(out[:, 64 * half:64 * half + 64], st[o:o + 64, 2 * t + half, p, :],
                                             R4[o:o + 64, p, t, 64 * half:64 * half + 64], start=False, stop=True,
                                             skip_group_check=True)
                last.then_inc(ph.sem("o"), 1)
            for p in range(HC):
                pe.wait_ge(ph.sem("o_sum"), p + 1)
                pe.matmul(m.banks[p][:], m.centre[:], K[:, p, :], start=True, stop=True).then_inc(ph.sem("centred"), 1)
            for p in range(HC):
                pe.wait_ge(ph.sem("squared"), p + 1)
                pe.matmul(m.banks[4 + p][:], m.same64[:], sq[:, p, :], start=True, stop=True).then_inc(ph.sem("sums"), 1)
            for p in range(HC):
                pe.matmul(m.banks[p][:], g2s[:, p * P:(p + 1) * P], x.x[:, 1, 1:], start=True, stop=True).then_inc(ph.sem("gate"), 1)

        @block.vector
        def _(dve):
            v = Chain(dve, ph.sem("dve"))
            dve.memset(st[:, 0], 0.0).then_inc(ph.sem("state"), 1)
            tri = m.tri3
            for p in range(HC):
                for q in range(2):
                    for t in range(NT):
                        u = NT * q + t
                        dve.wait_ge(ph.sem("products"), 2 * NT * p + u + 1)
                        if p and u == 0:
                            dve.wait_ge(ph.sem("tmv"), p)
                            dve.wait_ge(ph.sem("part0"), (levels - 1) * p)
                            dve.wait_ge(ph.sem("part1"), (levels - 1) * p)
                        e0, e1 = m.banks[2 * (u % 2)], m.banks[2 * (u % 2) + 1]
                        for out, src, mask in ((lt[:, q, t, :], e0[:, 0:P], tri[:, 0, :]),
                                               (rb[:, p, q, t, :], e0[:, P:2 * P], tri[:, 1, :]),
                                               (lo[:, q, t, :], e0[:, 2 * P:3 * P], tri[:, 2, :]),
                                               (mk[:, q, t, :, :].rearrange("p a b -> p (a b)"), e1[:, 0:2 * P],
                                                tri[:, 0:2, :].rearrange("p a b -> p (a b)"))):
                            dve.tensor_tensor(out, src, mask, ALU.mult).then_inc(ph.sem("products_taken"), 1)
                for n in range(1, levels):
                    for q in range(2):
                        dve.wait_ge(ph.sem(f"lt{q}"), p * (levels - 1) + n)
                        dve.tensor_tensor(xp[:, q], bank4(4 + q), ident4, ALU.add).then_inc(ph.sem(f"xp{q}"), 1)
            for c in range(NCH):
                b, t = 64 * (c % 2), c // 2
                dve.wait_ge(ph.sem("u"), c + 1)
                for q in range(2):
                    uq = uw4[b:b + 64, :, t, 64 * q:64 * q + 64]
                    dve.tensor_tensor(uq, uq, m.banks[q][b:b + 64, 0:HC * 64].rearrange("p (a n) -> p a n", n=64),
                                      ALU.add).then_inc(ph.sem("u_done"), 1)
                dve.wait_ge(ph.sem("s"), c + 1)
                s_in = m.banks[2 + c % 2][:, 0:HC * 64].rearrange("p (a n) -> p a n", n=64)
                dve.tensor_tensor(st[:, c + 1], s_in, st[:, c], ALU.add).then_inc(ph.sem("state"), 1)
                dve.wait_ge(ph.sem("state"), 2 * c + 2)
                dve.tensor_tensor(st[:, c + 1], st[:, c + 1], x.dc[:, :, c:c + 1].broadcast_to([P, HC, 64]),
                                  ALU.mult).then_inc(ph.sem("state"), 1)
            for p in range(HC):
                dve.wait_ge(ph.sem("o"), p + 1)
                dve.tensor_tensor(K[:, p, :], K[:, p, :], m.banks[4 + p][:], ALU.add).then_inc(ph.sem("o_sum"), 1)
            for p in range(HC):
                dve.wait_ge(ph.sem("sums"), p + 1)
                dve.tensor_scalar(sq[:, p, :], m.banks[4 + p][:], 1.0 / 64, GN_EPS, ALU.mult, ALU.add).then_inc(ph.sem("var"), 1)
            dve.wait_ge(ph.sem("deviation"), 1)
            v.link(dve.reciprocal(sq[:], sq[:]))
            dve.wait_ge(ph.sem("centred_out"), HC)
            v.link(dve.tensor_tensor(oc[:], oc[:], sq[:], ALU.mult))
            for p in range(HC):
                lw, lb = COLUMN["rw_ln_w"] + p, COLUMN["rw_ln_b"] + p
                v.mark(dve.tensor_scalar(oc[:, p, :], oc[:, p, :], m.params[:, lw:lw + 1], m.params[:, lb:lb + 1], ALU.mult, ALU.add))
            v.wait()
            v.link(dve.tensor_tensor(oc[:], oc[:], x.bonus[:, :, 1:], ALU.add))
            for p in range(HC):
                dve.wait_ge(ph.sem("gate"), p + 1)
                v.mark(dve.tensor_tensor(m.mixT[:, HC + p, :], oc[:, p, :], m.banks[p][:], ALU.mult))
            v.wait()

        @block.scalar
        def _(act):
            i = 0
            for p in range(HC):
                for dst in (brow, krow, vrow):
                    act.wait_ge(ph.sem("turned"), i + 1)
                    act.activation(dst[:, p], bank4(i % 6), ACT.Copy).then_inc(ph.sem("rows"), 1)
                    i += 1
            act.wait_ge(ph.sem("rows"), 3 * HC)
            for p in range(HC):
                act.wait_ge(ph.sem("arow"), p + 1)
                act.activation(arow[:], bank4(6), ACT.Copy).then_inc(ph.sem("arow_taken"), 1)
                k = p * (2 * (levels - 1) - 1)
                for n in range(1, levels):
                    for q in range(2):
                        kk = k + 2 * (n - 1)
                        if n < levels - 1:
                            act.wait_ge(ph.sem(f"merged{q}"), kk + 1)
                            act.activation(tt[:, q, 0], bank4(2 * q), ACT.Copy).then_inc(ph.sem(f"inverse{q}"), 1)
                            kk += 1
                        act.wait_ge(ph.sem(f"merged{q}"), kk + 1)
                        act.activation(tt[:, q, 1], bank4(2 * q + 1), ACT.Copy).then_inc(ph.sem(f"inverse{q}"), 1)
                act.wait_ge(ph.sem("mv"), p + 1)
                act.activation(w1[:], m.banks[6][:].rearrange("p (q t n) -> p q t n", q=2, n=64), ACT.Copy).then_inc(ph.sem("post"), 1)
                act.wait_ge(ph.sem("ta"), p + 1)
                act.activation(A4[:, p], bank4(4), ACT.Copy).then_inc(ph.sem("post"), 1)
                act.wait_ge(ph.sem("rkv"), p + 1)
                act.activation(K[:, p, :], m.banks[5][:], ACT.Copy).then_inc(ph.sem("post"), 1)
                act.wait_ge(ph.sem("tmv"), p + 1)
                act.activation(uw[:, p, :].rearrange("p (t q n) -> p q t n", q=2, n=64),
                               m.banks[7][:].rearrange("p (q t n) -> p q t n", q=2, n=64), ACT.Copy).then_inc(ph.sem("post"), 1)
            for p in range(HC):
                act.wait_ge(ph.sem("centred"), p + 1)
                act.activation(oc[:, p, :], m.banks[p][:], ACT.Copy).then_inc(ph.sem("centred_out"), 1)
                act.activation(sq[:, p, :], m.banks[p][:], ACT.Square).then_inc(ph.sem("squared"), 1)
            act.wait_ge(ph.sem("var"), HC)
            act.activation(sq[:], sq[:], ACT.Sqrt).then_inc(ph.sem("deviation"), 1)

        @block.gpsimd
        def _(pool):
            g = Chain(pool, ph.sem("pool"))
            for p in range(HC):
                for q in range(2):
                    pool.wait_ge(ph.sem("products_taken"), 4 * (2 * NT * p + NT * (q + 1)))
                    if p:
                        pool.wait_ge(ph.sem("tmv"), p)
                    g.mark(pool.tensor_tensor(tt[:, q, 0], lo[:, q], mask4(m.m1low[:]), ALU.mult))
                    g.link(pool.tensor_tensor(tt[:, q, 1], lt[:, q], mask4(m.masks[:, 0, :]), ALU.mult))
                    pool.tensor_tensor(tt[:, q, 0], tt[:, q, 0], ident4, ALU.add).then_inc(ph.sem(f"first{q}"), 1)
                    pool.tensor_tensor(tt[:, q, 1], tt[:, q, 1], ident4, ALU.add).then_inc(ph.sem(f"first{q}"), 1)
                for n in range(1, levels):
                    for q in range(2):
                        if n > 1:
                            pool.wait_ge(ph.sem(f"lt{q}"), p * (levels - 1) + n - 1)
                        pool.tensor_tensor(lo[:, q], lt[:, q], mask4(m.masks[:, n, :]), ALU.mult).then_inc(ph.sem(f"part{q}"), 1)
    ph.close()
class Moe:

    def __init__(self, m, experts, per_group, halves, slots, block):
        self.E, self.per_group, self.halves, self.cap, self.block = experts, per_group, halves, slots, block
        self.groups = experts // per_group
        self.EB = 4 // halves
        self.bodies = experts // self.EB
        self.EC = self.EB // 2
        self.width = self.EC * slots
        at = 0
        self.h, at = m.view(at, NT, D)
        self.x, at = m.view(at, NT, D)
        self.q, at = m.view(at, NT, experts)
        self.cw, at = m.view(at, NT, experts)
        self.L, _ = m.view(at, NT, 36)
        s = at + NT * 36
        self.wr, s = m.view(s, DC, 36)
        self.bias, s = m.view(s, 36)
        self.tmp = [None] * 6
        for i in range(6):
            self.tmp[i], s = m.view(s, NT, experts)
        self.t4 = [None] * 8
        for i in range(8):
            self.t4[i], s = m.view(s, NT, 4)
        self.one = [None] * 8
        for i in range(8):
            self.one[i], s = m.view(s, NT)
        self.G, at = m.view(at, NT, 2, P)
        self.ST, at = m.view(at, 2, S)
        self.xe, at = m.view(at, 2, DC, P)
        self.cbc, at = m.view(at, 2, P)
        self.hid, at = m.view(at, 4, 2, P)
        self.sig, at = m.view(at, 2, 2, P)
        self.y, at = m.view(at, 2, D)
        self.cwx, at = m.view(at, NT, 4)
        self.ring23, end = m.view(m.arena_size - 2 * RING, 2, RING)
        assert max(at, s) <= m.arena_size - 2 * RING
        self.m = m

    def slot(self, s):
        r = self.m.ring01[:, s, :] if s < 2 else self.ring23[:, s - 2, :]
        half = DC * 256
        return (r[:, 0:half].rearrange("p (c n) -> p c n", n=256), r[:, half:2 * half].rearrange("p (c n) -> p c n", n=256),
                r[:, 2 * half:].rearrange("p (c n) -> p c n", n=D))

    def load(self, sp, io, s, body, sem):
        gate, up, down = self.slot(s)
        wg, wu, wd = (io[n][0] for n in self.weights)
        if self.halves == 1:
            e, f0 = body * 4 + s, 0
        else:
            e, f0 = body * 2 + s // 2, 256 * (s % 2)
        if isinstance(e, int):
            wg, wu, wd = wg[e], wu[e], wd[e]
        else:
            wg, wu, wd = (w[bass.ds(e, 1)].rearrange("e a b -> (e a) b") for w in (wg, wu, wd))
        sp.dma_start(gate, wg[:, f0:f0 + 256].rearrange("(c p) n -> p c n", p=P)).then_inc(sem, 16)
        sp.dma_start(up, wu[:, f0:f0 + 256].rearrange("(c p) n -> p c n", p=P)).then_inc(sem, 16)
        sp.dma_start(down, wd[f0:f0 + 256, :].rearrange("(c p) n -> p c n", p=P)).then_inc(sem, 16)


def phase_out(nc, m, io, z, name, residual, w_out, gain, router, ring_sems):
    ph = Phase(nc, name)
    w_out = io[w_out][0]
    wg, bg, we, be = (io[n] for n in router)
    E, G = z.E, z.groups
    L = z.L[:, :, 0:G + E]
    gl, el = L[:, :, 0:G], L[:, :, G:]
    t = z.tmp
    one = z.one
    down = lambda a, n: a.unsqueeze(2).broadcast_to([P, NT, n])
    ramp = lambda n: m.experts[:, 0:n].unsqueeze(1).broadcast_to([P, NT, n])
    rows = residual.rearrange("b (t p) d -> p (b t) d", p=P) if len(residual.shape) == 3 else residual
    with nc.Block() as block:
        @block.sync
        def _(sp):
            for n in range(2):
                v = item_view(m, n, HW)
                src = w_out[:, n * HW:(n + 1) * HW].rearrange("(c p) n -> p c n", p=P)
                for a, b in ((0, 4), (4, 8)):
                    sp.dma_start(v[:, a:b, :], src[:, a:b, :]).then_inc(ph.sem(f"ring{n}"), 16)
                if n == 0:
                    sp.dma_start(z.h[:], rows).then_inc(ph.sem("residual"), 16)
            sp.dma_start(z.wr[:, :, 0:G], wg[0].rearrange("(c p) n -> p c n", p=P)).then_inc(ph.sem("router"), 16)
            sp.dma_start(z.wr[:, :, G:G + E], we[0].rearrange("(c p) n -> p c n", p=P)).then_inc(ph.sem("router"), 16)
            sp.dma_start(z.bias[:, 0:G], bg.partition_broadcast(P) if len(bg.shape) == 1 else bg[0:1, :].broadcast_to([P, G])).then_inc(ph.sem("router"), 16)
            sp.dma_start(z.bias[:, G:G + E], be[0:1, :].broadcast_to([P, E])).then_inc(ph.sem("router"), 16)
            for s in (2, 3):
                z.load(sp, io, s, 0, ring_sems[s])
            for s in (0, 1):
                sp.wait_ge(ph.sem("projected"), NT * (s + 1))
                z.load(sp, io, s, 0, ring_sems[s])

        @block.tensor
        def _(pe):
            for n in range(2):
                project_pe(pe, ph, m, n, HW, NT, NT * n, 32, True)
            norm_turn_pe(pe, ph, m, z.x)
            pe.wait_ge(ph.sem("normed"), NORMED)
            pe.wait_ge(ph.sem("router"), 64)
            for i in range(NT):
                for c in range(DC):
                    last = pe.matmul(m.banks[i][:, 0:G + E], m.mixT[:, c, i * P:(i + 1) * P], z.wr[:, c, 0:G + E],
                                     start=(c == 0), stop=(c == DC - 1))
            last.then_inc(ph.sem("logits"), 1)
            pe.wait_ge(ph.sem("chosen"), 1)
            for i in range(NT):
                for j in range(i + 1):
                    pe.matmul(m.banks[4][:, i * E:(i + 1) * E], (m.after if j == i else m.ones)[:], t[2][:, j, :],
                              start=(j == 0), stop=(j == i))
            for j in range(NT):
                last = pe.matmul(m.banks[5][:, 0:E], m.ones[:], t[2][:, j, :], start=(j == 0), stop=(j == NT - 1))
            last.then_inc(ph.sem("counted"), 1)

        @block.scalar
        def _(act):
            norm_act(act, ph, m, z.h, z.x, lambda e, i: e.wait_ge(ph.sem("taken"), 2 * NT))
            act.wait_ge(ph.sem("group_less"), 1)
            act.activation(z.t4[0][:, :, 0:G], z.t4[0][:, :, 0:G], ACT.Exp).then_inc(ph.sem("group_exp"), 1)
            act.wait_ge(ph.sem("second_less"), 1)
            act.activation(one[4], one[4], ACT.Exp).then_inc(ph.sem("second_exp"), 1)

        @block.vector
        def _(dve):
            v = Chain(dve, ph.sem("dve"))
            dve.wait_ge(ph.sem("residual"), 16)
            for k in range(2 * NT):
                n, i = k // NT, k % NT
                dve.wait_ge(ph.sem("projected"), k + 1)
                h = z.h[:, i, n * HW:(n + 1) * HW]
                dve.tensor_tensor(h, h, m.banks[k % 6][:], ALU.add).then_inc(ph.sem("taken"), 1)
            norm_scale_dve(dve, ph, m, z.h, z.x, v)
            norm_gain_dve(dve, ph, m, COLUMN[gain])
            dve.wait_ge(ph.sem("logits"), 1)
            for i in range(NT):
                v.mark(dve.tensor_tensor(L[:, i, :], m.banks[i][:, 0:G + E], z.bias[:, 0:G + E], ALU.add))
            v.wait()

            def first_of(values, top, n, out, scratch):
                v.link(dve.tensor_reduce(top, values, AX_X, ALU.max))
                v.mark(dve.tensor_tensor(out, values, down(top, n), ALU.is_equal))
                v.link(dve.tensor_scalar(scratch, ramp(n), -1.0, float(n), ALU.mult, ALU.add))
                v.link(dve.tensor_tensor(out, out, scratch, ALU.mult))
                v.link(dve.tensor_reduce(one[7], out, AX_X, ALU.max))
                v.link(dve.tensor_tensor(out, scratch, down(one[7], n), ALU.is_equal))

            group, g_less, g_scratch = z.t4[1][:, :, 0:G], z.t4[0][:, :, 0:G], z.t4[2][:, :, 0:G]
            first_of(gl, one[0], G, group, g_scratch)
            dve.tensor_tensor(g_less, gl, down(one[0], G), ALU.subtract).then_inc(ph.sem("group_less"), 1)
            v.link(dve.tensor_scalar(group, group, 1e30, -1e30, ALU.mult, ALU.add))
            v.link(dve.tensor_tensor(t[3].rearrange("p t (g e) -> p t g e", g=G), el.rearrange("p t (g e) -> p t g e", g=G),
                                     group.unsqueeze(3).broadcast_to([P, NT, G, z.per_group]), ALU.add))
            first_of(t[3], one[1], E, t[0], t[5])
            v.link(dve.scalar_tensor_tensor(t[3], t[0], -2e30, t[3], ALU.mult, ALU.add))
            first_of(t[3], one[2], E, t[1], t[5])
            dve.tensor_tensor(t[2], t[0], t[1], ALU.add).then_inc(ph.sem("chosen"), 1)
            dve.tensor_tensor(one[4], one[2], one[1], ALU.subtract).then_inc(ph.sem("second_less"), 1)
            dve.wait_ge(ph.sem("group_exp"), 1)
            v.link(dve.tensor_reduce(one[3], g_less, AX_X, ALU.add))
            dve.wait_ge(ph.sem("second_exp"), 1)
            v.link(dve.tensor_scalar(one[5], one[4], 1.0, None, ALU.add))
            v.link(dve.tensor_tensor(one[5], one[5], one[3], ALU.mult))
            v.link(dve.reciprocal(one[5], one[5]))
            v.link(dve.tensor_tensor(one[6], one[5], one[4], ALU.mult))
            v.mark(dve.tensor_tensor(t[0], t[0], down(one[5], E), ALU.mult))
            v.link(dve.tensor_tensor(t[1], t[1], down(one[6], E), ALU.mult))
            v.link(dve.tensor_tensor(z.cw, t[0], t[1], ALU.add))
            dve.wait_ge(ph.sem("counted"), 1)
            v.link(dve.tensor_scalar(t[3], m.banks[4][:, 0:NT * E].rearrange("p (t e) -> p t e", e=E), 1.0, None, ALU.add))
            v.link(dve.tensor_tensor(t[3], t[3], t[2], ALU.mult))
            v.link(dve.tensor_scalar(z.q, t[3], -1.0, None, ALU.add))
            rounds = -(-S // z.cap)
            v.link(dve.tensor_reduce(one[0][:, 0:1], m.banks[5][:, 0:E], AX_X, ALU.max))
            v.link(dve.tensor_scalar(t[4][:, 0, 0:rounds], m.experts[:, 0:rounds], float(z.cap), one[0][:, 0:1], ALU.mult, ALU.is_lt))
            v.link(dve.tensor_reduce(one[1][:, 0:1], t[4][:, 0, 0:rounds], AX_X, ALU.add))
            v.link(dve.tensor_copy(m.rounds[:], one[1][:, 0:1]))
    ph.close()


def phase_moe(nc, m, io, z, name, gain, ring_sems):
    ph = Phase(nc, name)
    most = -(-S // z.cap)
    W, cap, NB = z.width, z.cap, z.bodies
    gath, hb, yb, sb_, cb = m.banks[0:2], m.banks[2:4], m.banks[4:6], m.banks[6], m.banks[7]
    own = lambda i: slice(64 * (i % 2), 64 * (i % 2) + cap) if z.halves == 1 else slice(0, cap)
    gains = lambda half: m.params[:, gain + 4 * half:gain + 4 * half + 4].unsqueeze(2).broadcast_to([P, 4, W])

    def loop(engine, body, after_round=None):
        n = engine.value_load(m.rounds[0:1, 0:1], min_val=1, max_val=most)
        with engine.Fori(0, n) as r:
            with engine.Fori(0, NB) as i:
                body(r * NB + i, i)
            if after_round:
                after_round(r)

    with nc.Block() as block:
        @block.sync
        def _(sp):
            def fill(g, i):
                for s in range(4):
                    sp.wait_ge(ph.sem("down"), g * 4 + (s - 3))
                    z.load(sp, io, s, i, ring_sems[s])

            n = sp.value_load(m.rounds[0:1, 0:1], min_val=1, max_val=most)
            with sp.Fori(1, NB) as i:
                fill(i, i)
            with sp.If(n > 1):
                with sp.Fori(1, n) as r:
                    with sp.Fori(0, NB) as i:
                        fill(r * NB + i, i)
            with sp.Else():
                sp.nop()

        @block.tensor
        def _(pe):
            def body(g, i):
                def gather(c):
                    pe.wait_ge(ph.sem("onehot"), g * 2 + c + 1)
                    if c == 0:
                        pe.wait_ge(ph.sem("summed"), g * 8 + 1)
                    else:
                        pe.wait_ge(ph.sem("gathered_taken"), g * 4 + 2)
                    for j in range(DC):
                        for t in range(NT):
                            last = pe.matmul(gath[j // 4][:, (j % 4) * W:(j % 4 + 1) * W], z.x[:, t, j * P:(j + 1) * P],
                                             z.G[:, t, c, 0:W], start=(t == 0), stop=(t == NT - 1))
                    last.then_inc(ph.sem("gathered"), 1)
                    if c == 1:
                        pe.wait_ge(ph.sem("turned_taken"), g * 2 + 2)
                    else:
                        pe.wait_ge(ph.sem("turned_taken"), g * 2 + 1)
                    for t in range(NT):
                        last = pe.transpose(sb_[0:W, t * P:(t + 1) * P], z.G[:, t, c, 0:W], m.ident[:])
                    last.then_inc(ph.sem("turned"), 1)
                    pe.wait_ge(ph.sem("cwx"), g + 1)
                    pe.wait_ge(ph.sem("cbc"), g * 2 + c + 1)
                    for k in range(z.EC):
                        for t in range(NT):
                            e = c * z.EC + k
                            last = pe.matmul(cb[:, k * cap:(k + 1) * cap], z.cwx[:, t, e:e + 1].broadcast_to([P, P]),
                                             z.G[:, t, c, k * cap:(k + 1) * cap], start=(t == 0), stop=(t == NT - 1))
                    last.then_inc(ph.sem("cweights"), 1)

                def gate_up(s):
                    c = s // 2
                    gate, up, _ = z.slot(s)
                    pe.wait_ge(ring_sems[s], (g + 1) * 48)
                    pe.wait_ge(ph.sem("gathered_taken"), g * 4 + 2 * c + 2)
                    if s >= 2:
                        pe.wait_ge(ph.sem("hidden_done"), g * 4 + s )
                    else:
                        pe.wait_ge(ph.sem("hidden_done"), g * 4 + 1)
                    for k, w in enumerate((gate, up)):
                        for f in range(2):
                            for j in range(DC):
                                last = pe.matmul(hb[s % 2][:, k * 256 + f * P:k * 256 + f * P + cap], w[:, j, f * P:(f + 1) * P],
                                                 z.xe[:, c, j, own(s)], start=(j == 0), stop=(j == DC - 1))
                    last.then_inc(ph.sem("hidden"), 1)

                def down(s):
                    c = s // 2
                    _, _, wd = z.slot(s)
                    pe.wait_ge(ph.sem("hidden_done"), g * 4 + s + 2)
                    if s % 2 == 0:
                        pe.wait_ge(ph.sem("y_taken"), g * 4 + 2 * c + 1)
                    for n in range(2):
                        for f in range(2):
                            first = f == 0 and (z.halves == 1 or s % 2 == 0)
                            final = f == 1 and (z.halves == 1 or s % 2 == 1)
                            last = pe.matmul(yb[n][own(s), :], z.hid[:, s, f, 0:cap], wd[:, f, n * 512:(n + 1) * 512],
                                             start=first, stop=final)
                    last.then_inc(ph.sem("down"), 1)

                gather(0)
                gather(1)
                gate_up(0)
                gate_up(1)
                down(0)
                gate_up(2)
                down(1)
                gate_up(3)
                down(2)
                down(3)
                pe.wait_ge(ph.sem("y_taken"), g * 4 + 4 + 1)
                pe.wait_ge(ph.sem("turned_taken"), g * 2 + 2 + 1)
                for k in range(8):
                    t, n = k // 2, k % 2
                    if k >= 2:
                        pe.wait_ge(ph.sem("summed"), g * 8 + k )
                    for c in range(2):
                        last = pe.matmul(gath[n][:], z.ST[0:W, c, t * P:(t + 1) * P], z.y[0:W, c, n * 512:(n + 1) * 512],
                                         start=(c == 0), stop=(c == 1))
                    last.then_inc(ph.sem("scattered"), 1)

            pe.sem_inc(ph.sem("scattered"), 1)
            loop(pe, body)

        @block.vector
        def _(dve):
            v = ph.sem("dve")

            def body(g, i):
                e0 = i * z.EB
                dve.tensor_copy(z.cwx[:, :, 0:z.EB], z.cw[:, :, bass.ds(e0, z.EB)]).then_inc(ph.sem("cwx"), 1)
                for c in range(2):
                    qe = z.q[:, :, bass.ds(e0 + c * z.EC, z.EC)]
                    if z.EC == 2:
                        dve.tensor_tensor(z.G[:, :, c, :].rearrange("p t (e n) -> p t e n", n=cap),
                                          m.slots[:, 0, :].rearrange("p (e n) -> p e n", n=cap).unsqueeze(1).broadcast_to([P, NT, 2, cap]),
                                          qe.unsqueeze(3).broadcast_to([P, NT, 2, cap]), ALU.is_equal).then_inc(ph.sem("onehot"), 1)
                    else:
                        dve.tensor_tensor(z.G[:, :, c, 0:cap], m.slots[:, 1:2, 0:cap].broadcast_to([P, NT, cap]),
                                          qe.broadcast_to([P, NT, cap]), ALU.is_equal).then_inc(ph.sem("onehot"), 1)
                for c in range(2):
                    dve.wait_ge(ph.sem("gathered"), g * 2 + c + 1)
                    for half in range(2):
                        dve.tensor_tensor(z.xe[:, c, 4 * half:4 * half + 4, 0:W],
                                          gath[half][:, 0:4 * W].rearrange("p (a n) -> p a n", n=W), gains(half),
                                          ALU.mult).then_inc(ph.sem("gathered_taken"), 1)
                for s in range(4):
                    c = s // 2
                    b = hb[s % 2][:].rearrange("p (k f n) -> p k f n", k=2, n=P)
                    h = z.hid[:, s, :, 0:cap]
                    dve.wait_ge(ph.sem("sigmoid"), g * 4 + s + 1)
                    dve.tensor_tensor(h, b[:, 0, :, 0:cap], z.sig[:, s % 2, :, 0:cap], ALU.mult).then_inc(v, 1)
                    dve.wait_ge(v, g * 8 + 2 * s + 1)
                    dve.tensor_tensor(h, h, b[:, 1, :, 0:cap], ALU.mult).then_inc(v, 1)
                    dve.wait_ge(v, g * 8 + 2 * s + 2)
                    if s % 2 == 0:
                        dve.wait_ge(ph.sem("cbc"), g * 2 + c + 2)
                    dve.tensor_tensor(h, h, z.cbc[:, c:c + 1, own(s)].broadcast_to([P, 2, cap]), ALU.mult).then_inc(ph.sem("hidden_done"), 1)
                for k in range(8):
                    t, n = k // 2, k % 2
                    dve.wait_ge(ph.sem("scattered"), g * 8 + k + 2)
                    hh = z.h[:, t, n * 512:(n + 1) * 512]
                    dve.tensor_tensor(hh, hh, gath[n][:], ALU.add).then_inc(ph.sem("summed"), 1)

            def next_round(r):
                dve.tensor_scalar(z.q, z.q, -float(cap), None, ALU.add).then_inc(ph.sem("round"), 1)
                dve.wait_ge(ph.sem("round"), r + 1)

            for name in ("hidden_done", "summed"):
                dve.sem_inc(ph.sem(name), 1)
            loop(dve, body, next_round)

        @block.scalar
        def _(act):
            def body(g, i):
                for c in range(2):
                    act.wait_ge(ph.sem("turned"), g * 2 + c + 1)
                    if c == 0:
                        act.wait_ge(ph.sem("scattered"), g * 8 + 1)
                    act.activation(z.ST[0:W, c, :], sb_[0:W, :], ACT.Copy).then_inc(ph.sem("turned_taken"), 1)
                    act.wait_ge(ph.sem("cweights"), g * 2 + c + 1)
                    act.wait_ge(ph.sem("hidden_done"), g * 4 + 1)
                    act.activation(z.cbc[:, c, 0:W], cb[:, 0:W], ACT.Copy).then_inc(ph.sem("cbc"), 1)

                def sigmoid(s):
                    act.wait_ge(ph.sem("hidden"), g * 4 + s + 1)
                    if s < 2:
                        act.wait_ge(ph.sem("hidden_done"), g * 4 + 1)
                    else:
                        act.wait_ge(ph.sem("hidden_done"), g * 4 + s )
                    b = hb[s % 2][:].rearrange("p (k f n) -> p k f n", k=2, n=P)
                    act.activation(z.sig[:, s % 2, :, 0:cap], b[:, 0, :, 0:cap], ACT.Sigmoid).then_inc(ph.sem("sigmoid"), 1)

                def rows(c):
                    act.wait_ge(ph.sem("down"), g * 4 + 2 * c + 2)
                    for n in range(2):
                        act.activation(z.y[0:W, c, n * 512:(n + 1) * 512], yb[n][0:W, :], ACT.Copy).then_inc(ph.sem("y_taken"), 1)

                for s in range(4):
                    sigmoid(s)
                    if s == 3:
                        rows(0)
                rows(1)

            for name in ("turned_taken", "cbc", "y_taken"):
                act.sem_inc(ph.sem(name), 1)
            loop(act, body)
    ph.close()


def phase_final(nc, m, z, name, gain_src, dst, out_view):
    ph = Phase(nc, name)
    gain = m.ring01[:, 0, 0:D]
    rows = dst.rearrange("b (t p) d -> p (b t) d", p=P) if len(dst.shape) == 3 else dst
    with nc.Block() as block:
        @block.sync
        def _(sp):
            sp.dma_start(gain, gain_src.rearrange("(a d) -> a d", a=1).broadcast_to([P, D])).then_inc(ph.sem("gain"), 16)
            for t in range(NT):
                sp.wait_ge(ph.sem("done"), t + 1)
                sp.dma_start(rows[:, t, :], out_view[:, t, :]).then_inc(ph.sem("stored"), 16)
            sp.wait_ge(ph.sem("stored"), 16 * NT)

        @block.scalar
        def _(act):
            norm_act(act, ph, m, z.h, z.x, lambda e, t: None)

        @block.vector
        def _(dve):
            v = Chain(dve, ph.sem("dve"))
            dve.wait_ge(ph.sem("squares"), NT)
            dve.tensor_scalar(m.small[:, 4:8], m.small[:, 0:4], 1.0 / D, EPS, ALU.mult, ALU.add).then_inc(ph.sem("mean"), 1)
            dve.wait_ge(ph.sem("deviation"), 1)
            v.link(dve.reciprocal(m.small[:, 12:16], m.small[:, 8:12]))
            dve.wait_ge(ph.sem("gain"), 16)
            for t in range(NT):
                dve.scalar_tensor_tensor(out_view[:, t, :], z.h[:, t, :], m.small[:, 12 + t:13 + t], gain, ALU.mult,
                                         ALU.mult).then_inc(ph.sem("done"), 1)
    ph.close()
HG = 4
FH = 8


class Mix2:

    def __init__(self, m):
        at = 0
        self.q, at = m.view(at, HG, S)
        self.k, at = m.view(at, HG, S)
        self.g, at = m.view(at, HG, S)
        self.i, at = m.view(at, NT, HW)
        self.b, at = m.view(at, HG, S)
        self.fq, at = m.view(at, HC, S)
        self.fk, at = m.view(at, HC, S)
        self.fv, at = m.view(at, NT, HW)
        self.ncum, at = m.view(at, S, partitions=8)
        self.lb, at = m.view(at, 3, HG)
        self.fbias, at = m.view(at, 1, partitions=8)
        self.free = at
        self.rows, end = m.view(at, NT, D)
        self.scaled, end = m.view(end, NT, D)
        self.f8, _ = m.view(end, 4, S, partitions=8)


def phase_project2(nc, m, io, x):
    ph = Phase(nc, "p2")
    w_in = io["w_in_2"].rearrange("l d n -> (l d) n")
    starts, sizes, widths = [HW, 0, 2 * HW, 3 * HW, 3 * HW + 768, 3 * HW + 1536], [4, 4, 4, 6, 6, 5], [HW, HW, HW, 768, 768, HW + FH]
    first = [sum(sizes[:i]) for i in range(6)]
    total = sum(sizes)
    lbc = COLUMN["hg_lb_logits_2"]

    with nc.Block() as block:
        @block.sync
        def _(sp):
            for n in range(6):
                if n >= 2:
                    sp.wait_ge(ph.sem("projected"), first[n - 1])
                v = item_view(m, n, widths[n])
                src = w_in[:, starts[n]:starts[n] + widths[n]].rearrange("(c p) n -> p c n", p=P)
                for a, b in ((0, 4), (4, 8)):
                    sp.dma_start(v[:, a:b, :], src[:, a:b, :]).then_inc(ph.sem(f"ring{n % 2}"), 16)
                if n == 0:
                    sp.dma_start(x.fbias[:], io["fox_f_bias_2"].rearrange("l h -> h l")).then_inc(ph.sem("fbias"), 16)
            sp.wait_ge(ph.sem("fbias"), 16)

        @block.tensor
        def _(pe):
            norm_turn_pe(pe, ph, m, x.scaled)
            pe.wait_ge(ph.sem("normed"), NORMED)
            for n in range(6):
                project_pe(pe, ph, m, n, widths[n], sizes[n] if n < 5 else 4, first[n], 32 * (n // 2 + 1), n in (2, 5))
            w = item_view(m, 5, widths[5])
            k = total - 1
            pe.wait_ge(ph.sem("taken"), k - 5)
            for c in range(DC):
                last = pe.matmul(m.banks[k % 6][0:FH, :], w[:, c, HW:HW + FH], m.mixT[:, c, :], start=(c == 0), stop=(c == DC - 1))
            last.then_inc(ph.sem("projected"), 1)

        @block.scalar
        def _(act):
            a = Chain(act, ph.sem("act"))
            norm_act(act, ph, m, x.rows, x.scaled, lambda e, t: None)
            act.wait_ge(ph.sem("lb_less"), 1)
            act.activation(x.lb[:, 0, :], x.lb[:, 2, :], ACT.Sigmoid).then_inc(ph.sem("lb"), 1)
            outs = [(x.k[:, c, :], ACT.Sigmoid, 1.0) for c in range(4)] + [(x.q[:, c, :], ACT.Silu, 1.0) for c in range(4)] \
                + [(x.i[:, c, :], ACT.Copy, 1.0) for c in range(4)] + [(x.g[:, c, :], ACT.Silu, 1.0) for c in range(4)] \
                + [(x.fq[:, c, :], ACT.Copy, 0.125) for c in range(4)] + [(x.fk[:, c, :], ACT.Copy, 1.0) for c in range(4)] \
                + [(x.fv[:, c, :], ACT.Copy, 1.0) for c in range(4)]

            for k in range(total):
                act.wait_ge(ph.sem("projected"), k + 1)
                bank = m.banks[k % 6]
                if k < total - 1:
                    out, func, scale = outs[k]
                    act.activation(out, bank[:], func, scale=scale).then_inc(ph.sem("taken"), 1)
                else:
                    act.activation(x.f8[:, 0], bank[0:FH, :], ACT.Identity, bias=x.fbias[:, 0:1]).then_inc(ph.sem("taken"), 1)
                if k == 8:
                    act.wait_ge(ph.sem("f"), 1)
                    act.activation(x.b[:], x.b[:], ACT.Ln).then_inc(ph.sem("logf"), 1)
            act.wait_ge(ph.sem("taken"), total)
            a.link(act.activation(x.f8[:, 1], x.f8[:, 0], ACT.Abs))
            a.link(act.activation(x.f8[:, 1], x.f8[:, 1], ACT.Exp, scale=-1.0))
            act.activation(x.f8[:, 1], x.f8[:, 1], ACT.Ln, bias=1.0).then_inc(ph.sem("f8"), 1)

        @block.vector
        def _(dve):
            v = Chain(dve, ph.sem("dve"))
            dve.tensor_tensor(x.lb[:, 2, :], m.params[:, lbc:lbc + 4], m.params[:, lbc + 4:lbc + 8], ALU.subtract).then_inc(ph.sem("lb_less"), 1)
            norm_scale_dve(dve, ph, m, x.rows, x.scaled, v)
            norm_gain_dve(dve, ph, m, COLUMN["attn_norm_2"])
            dve.wait_ge(ph.sem("lb"), 1)
            v.link(dve.tensor_scalar(x.lb[:, 1, :], x.lb[:, 0, :], -1.0, 1.0, ALU.mult, ALU.add))
            for c in range(HG):
                dve.wait_ge(ph.sem("taken"), c + 1)
                v.mark(dve.tensor_scalar(x.b[:, c, :], x.k[:, c, :], x.lb[:, 1, c:c + 1], x.lb[:, 0, c:c + 1], ALU.mult, ALU.add))
            v.wait()
            dve.tensor_scalar(x.k[:], x.b[:], -1.0, 1.0, ALU.mult, ALU.add).then_inc(ph.sem("f"), 1)
            dve.wait_ge(ph.sem("logf"), 1)
            for c in range(HG):
                v.mark(dve.tensor_tensor_scan(x.b[:, c, :], m.restart[:], x.b[:, c, :], 0.0, ALU.mult, ALU.add))
            v.mark(dve.memset(x.f8[:, 3], 1.0))
            dve.wait_ge(ph.sem("f8"), 1)
            v.link(dve.scalar_tensor_tensor(x.f8[:, 2], x.f8[:, 0], 0.0, x.f8[:, 1], ALU.min, ALU.subtract))
            v.link(dve.tensor_tensor_scan(x.f8[:, 1], x.f8[:, 3], x.f8[:, 2], 0.0, ALU.mult, ALU.add))
            v.link(dve.tensor_scalar(x.ncum[:], x.f8[:, 1], -1.0, None, ALU.mult))
    ph.close()


def phase_hgrn(nc, m, x):
    ph = Phase(nc, "hg")
    at = x.free
    e2, at = m.view(at, 2, S)
    q2, at = m.view(at, 2, S)
    k2, at = m.view(at, 2, S)
    sc, at = m.view(at, HG, NT, P)
    kd, at = m.view(at, HG, S)
    krow, at = m.view(at, NT, HG, P)
    st, at = m.view(at, NCH + 1, HG, P)
    dl, at = m.view(at, HG, NCH)
    qb = x.q
    sq = kd
    units = [(h, l) for h in range(HG) for l in range(len(LEVELS))]
    chunked = lambda ap: ap.rearrange("p h (c n) -> p h c n", n=CH)
    bank4 = lambda i: m.banks[i][:].rearrange("p (t n) -> p t n", n=P)

    with nc.Block() as block:
        @block.vector
        def _(dve):
            v = Chain(dve, ph.sem("dve"))
            v.mark(dve.memset(st[:, 0], 0.0))
            last = chunked(x.b)[:, :, :, CH - 1:CH].broadcast_to([P, HG, NCH, CH])
            dve.tensor_tensor(chunked(kd), last, chunked(x.b), ALU.subtract).then_inc(ph.sem("to_end"), 1)

            def difference(u):
                h, l = units[u]
                n = LEVELS[l]
                if u >= 2:
                    dve.wait_ge(ph.sem("queries"), u - 1)
                    dve.wait_ge(ph.sem("keys"), u - 1)
                b = x.b[:, h, :].rearrange("p (a n) -> p a n", n=2 * n)
                dve.tensor_tensor(e2[:, u % 2, :].rearrange("p (a n) -> p a n", n=2 * n), b,
                                  b[:, :, n - 1:n].broadcast_to([P, S // (2 * n), 2 * n]), ALU.subtract).then_inc(ph.sem("difference"), 1)

            def keys(u):
                h, _ = units[u]
                dve.wait_ge(ph.sem("decay"), u + 1)
                if u >= 2:
                    dve.wait_ge(ph.sem("products"), HG + u - 1)
                dve.tensor_tensor(k2[:, u % 2, :], x.k[:, h, :], e2[:, u % 2, :], ALU.mult).then_inc(ph.sem("keys"), 1)

            def select(u):
                h, l = units[u]
                dve.wait_ge(ph.sem("products"), HG + u + 1)
                mask = m.masks[:, l:l + 1, :].bitcast(I32).broadcast_to([P, NT, P])
                dve.copy_predicated(sc[:, h], mask, bank4(4 + u % 4)).then_inc(ph.sem("selected"), 1)

            for h in range(HG):
                dve.wait_ge(ph.sem("products"), h + 1)
                v.mark(dve.tensor_tensor(sc[:, h], bank4(h), m.ident[:].unsqueeze(1).broadcast_to([P, NT, P]), ALU.mult))
            v.wait()
            dve.wait_ge(ph.sem("end_decay"), 1)
            dve.tensor_tensor(kd[:], kd[:], x.k[:], ALU.mult).then_inc(ph.sem("kd"), 1)
            difference(0)
            for u in range(len(units)):
                if u + 1 < len(units):
                    difference(u + 1)
                keys(u)
                if u >= 1:
                    if u >= 2:
                        dve.wait_ge(ph.sem("selected"), u - 1)
                    select(u - 1)
            dve.wait_ge(ph.sem("selected"), len(units) - 1)
            select(len(units) - 1)
            for c in range(NCH):
                dve.wait_ge(ph.sem("outer"), c + 1)
                if c:
                    dve.wait_ge(ph.sem("state"), HG * c)
                for h in range(HG):
                    dve.scalar_tensor_tensor(st[:, c + 1, h, :], st[:, c, h, :], dl[:, h, c:c + 1],
                                             m.banks[c % 4][:, h * P:(h + 1) * P], ALU.mult, ALU.add).then_inc(ph.sem("state"), 1)
            for h in range(HG):
                dve.wait_ge(ph.sem("sums"), h + 1)
                dve.tensor_scalar(sq[:, h, :], m.banks[h][:], 1.0 / P, EPS, ALU.mult, ALU.add).then_inc(ph.sem("mean"), 1)
            dve.wait_ge(ph.sem("deviation"), 1)
            v.link(dve.reciprocal(sq[:], sq[:]))
            v.link(dve.tensor_tensor(sq[:], sq[:], x.g[:], ALU.mult))
            g = COLUMN["hg_norm_2"]
            v.link(dve.scalar_tensor_tensor(m.mixT[:, 0:HG, :], m.mixT[:, 0:HG, :], m.params[:, g:g + 1], sq[:], ALU.mult, ALU.mult))

        @block.scalar
        def _(act):
            a = Chain(act, ph.sem("act"))
            act.wait_ge(ph.sem("to_end"), 1)
            act.activation(kd[:], kd[:], ACT.Exp).then_inc(ph.sem("end_decay"), 1)
            a.link(act.activation(dl[:], chunked(x.b)[:, :, :, CH - 1], ACT.Exp))
            for u in range(len(units)):
                act.wait_ge(ph.sem("difference"), u + 1)
                a.link(act.activation(e2[:, u % 2, :], e2[:, u % 2, :], ACT.Abs))
                act.activation(e2[:, u % 2, :], e2[:, u % 2, :], ACT.Exp, scale=-1.0).then_inc(ph.sem("decay"), 1)
                if u == 3:
                    act.wait_ge(ph.sem("kd_turned"), 1)
                    for t in range(NT):
                        act.wait_ge(ph.sem("kd_turned"), t + 1)
                        act.activation(krow[:, t], bank4(t), ACT.Copy).then_inc(ph.sem("krow"), 1)
            act.wait_ge(ph.sem("difference"), len(units))
            act.activation(x.b[:], x.b[:], ACT.Exp).then_inc(ph.sem("start_decay"), 1)
            for h in range(HG):
                act.wait_ge(ph.sem("out"), h + 1)
                act.activation(m.mixT[:, h, :], m.banks[4 + h][:], ACT.Copy).then_inc(ph.sem("out_taken"), 1)
                act.activation(sq[:, h, :], m.banks[4 + h][:], ACT.Square).then_inc(ph.sem("squared"), 1)
            act.wait_ge(ph.sem("mean"), HG)
            act.activation(sq[:], sq[:], ACT.Sqrt).then_inc(ph.sem("deviation"), 1)

        @block.gpsimd
        def _(pool):
            for u in range(len(units)):
                h, _ = units[u]
                pool.wait_ge(ph.sem("decay"), u + 1)
                if u >= 2:
                    pool.wait_ge(ph.sem("products"), HG + u - 1)
                pool.tensor_tensor(q2[:, u % 2, :], x.q[:, h, :], e2[:, u % 2, :], ALU.mult).then_inc(ph.sem("queries"), 1)
            pool.wait_ge(ph.sem("queries"), len(units))
            pool.wait_ge(ph.sem("start_decay"), 1)
            pool.tensor_tensor(qb[:], x.q[:], x.b[:], ALU.mult).then_inc(ph.sem("qb"), 1)

        @block.tensor
        def _(pe):
            for h in range(HG):
                for t in range(NT):
                    last = pe.matmul(m.banks[h][:, t * P:(t + 1) * P], x.k[:, h, t * P:(t + 1) * P], x.q[:, h, t * P:(t + 1) * P],
                                     start=True, stop=True)
                last.then_inc(ph.sem("products"), 1)
            pe.wait_ge(ph.sem("kd"), 1)
            for t in range(NT):
                for h in range(HG):
                    last = pe.transpose(m.banks[t][:, h * P:(h + 1) * P], kd[:, h, t * P:(t + 1) * P], m.ident[:])
                last.then_inc(ph.sem("kd_turned"), 1)
            for u in range(len(units)):
                pe.wait_ge(ph.sem("queries"), u + 1)
                pe.wait_ge(ph.sem("keys"), u + 1)
                if u >= 4:
                    pe.wait_ge(ph.sem("selected"), u - 3)
                for t in range(NT):
                    last = pe.matmul(m.banks[4 + u % 4][:, t * P:(t + 1) * P], k2[:, u % 2, t * P:(t + 1) * P],
                                     q2[:, u % 2, t * P:(t + 1) * P], start=True, stop=True)
                last.then_inc(ph.sem("products"), 1)
            pe.wait_ge(ph.sem("krow"), NT)
            for c in range(NCH):
                if c >= 4:
                    pe.wait_ge(ph.sem("state"), HG * (c - 3))
                b, t = 64 * (c % 2), c // 2
                for h in range(HG):
                    last = pe.matmul(m.banks[c % 4][:, h * P:(h + 1) * P], krow[b:b + 64, t, h, :], x.i[b:b + 64, t, h * P:(h + 1) * P],
                                     start=True, stop=True)
                last.then_inc(ph.sem("outer"), 1)
            pe.wait_ge(ph.sem("state"), HG * NCH)
            pe.wait_ge(ph.sem("selected"), len(units))
            pe.wait_ge(ph.sem("qb"), 1)
            for h in range(HG):
                for t in range(NT):
                    out = m.banks[4 + h][:, t * P:(t + 1) * P]
                    pe.matmul(out, x.i[:, t, h * P:(h + 1) * P], sc[:, h, t, :], start=True, stop=True, skip_group_check=True)
                    for half in range(2):
                        last = pe.matmul(out[:, 64 * half:64 * half + 64], st[:, 2 * t + half, h, :],
                                         qb[:, h, t * P + 64 * half:t * P + 64 * half + 64], start=False, stop=True, skip_group_check=True)
                last.then_inc(ph.sem("out"), 1)
            for h in range(HG):
                pe.wait_ge(ph.sem("squared"), h + 1)
                pe.matmul(m.banks[h][:], m.ones[:], sq[:, h, :], start=True, stop=True).then_inc(ph.sem("sums"), 1)
    ph.close()


F_PLACE = [(1, 384), (2, 0), (1, 0), (0, 0)]
F_FLAT = [896, 1024, 512, 0]


def phase_fox(nc, m, x):
    ph = Phase(nc, "fox")
    at = x.free
    p2, at = m.view(at, 2, 1280)
    pt, at = m.view(at, 2, 10, P)
    o, at = m.view(at, NT, FH, 64)
    sq, at = m.view(at, NT, FH, 64)
    far, at = m.view(at, P)
    mx, at = m.view(at, FH, NT)
    total, at = m.view(at, FH, NT)
    rms, at = m.view(at, NT, FH)
    blocks = [(t, s) for t in range(NT) for s in range(t + 1)]
    parts = [(0, 4), (4, 8), (8, 10)]
    zbank = lambda h, i: m.banks[3 * (h % 2) + i]

    def region(h, t):
        b, c = F_PLACE[t]
        return zbank(h, b)[:, c:c + (t + 1) * P]

    with nc.Block() as block:
        @block.tensor
        def _(pe):
            def logits(h):
                if h >= 2:
                    pe.wait_ge(ph.sem("exp"), NT * (h - 1))
                r = 64 * (h % 2)
                for t in (3, 2, 1, 0):
                    last = pe.matmul(region(h, t), x.fq[r:r + 64, h // 2, t * P:(t + 1) * P], x.fk[r:r + 64, h // 2, 0:(t + 1) * P],
                                     start=(t != 0), stop=False, skip_group_check=True)
                last.then_inc(ph.sem("qk"), 1)
                pe.wait_ge(ph.sem("qk"), h + 1)
                for t in (3, 2, 1, 0):
                    last = pe.matmul(region(h, t), m.sel8[0:8, h, :], x.ncum[0:8, 0:(t + 1) * P],
                                     start=False, stop=True, skip_group_check=True)
                last.then_inc(ph.sem("logits"), 1)

            def turn(h):
                pe.wait_ge(ph.sem("exp"), NT * (h + 1))
                for i, (a, b) in enumerate(parts):
                    k = 3 * h + i
                    if k >= 1:
                        pe.wait_ge(ph.sem("pt"), k)
                    for j in range(a, b):
                        t, s = blocks[j]
                        last = pe.transpose(m.banks[6][:, (j - a) * P:(j - a + 1) * P],
                                            p2[:, h % 2, F_FLAT[t] + s * P:F_FLAT[t] + (s + 1) * P], m.ident[:])
                    last.then_inc(ph.sem("turned"), 1)

            def values(h):
                pe.wait_ge(ph.sem("pt"), 3 * (h + 1))
                if h >= 1:
                    pe.wait_ge(ph.sem("o"), h)
                for j, (t, s) in enumerate(blocks):
                    c = 256 * (h % 2) + 64 * t
                    last = pe.matmul(m.banks[7][:, c:c + 64], pt[:, h % 2, j, :], x.fv[:, s, 64 * h:64 * h + 64],
                                     start=(s == 0), stop=(s == t))
                last.then_inc(ph.sem("values"), 1)

            logits(0)
            for h in range(FH):
                if h + 1 < FH:
                    logits(h + 1)
                if h >= 1:
                    values(h - 1)
                turn(h)
            values(FH - 1)
            pe.wait_ge(ph.sem("normed"), 1)
            for t in range(NT):
                for c in range(HC):
                    last = pe.transpose(m.banks[c][:, t * P:(t + 1) * P], o[:, t, 2 * c:2 * c + 2, :].rearrange("p a b -> p (a b)"), m.ident[:])
            last.then_inc(ph.sem("o_turned"), 1)

        @block.vector
        def _(dve):
            v = Chain(dve, ph.sem("dve"))
            v.link(dve.tensor_scalar(far[:], m.after[:], -1e30, None, ALU.mult))

            def masked(h):
                dve.wait_ge(ph.sem("logits"), h + 1)
                for t in range(NT):
                    d = region(h, t)[:, t * P:]
                    v.mark(dve.tensor_tensor(d, d, far[:], ALU.add))
                v.wait()
                for t in range(NT):
                    v.mark(dve.tensor_reduce(mx[:, h, t:t + 1], region(h, t), AX_X, ALU.max))
                v.wait()
                dve.tensor_scalar(mx[:, h], mx[:, h], -1.0, None, ALU.mult).then_inc(ph.sem("max"), 1)

            def output(h):
                dve.wait_ge(ph.sem("exp"), NT * (h + 1))
                v.link(dve.reciprocal(total[:, h], total[:, h]))
                dve.wait_ge(ph.sem("values"), h + 1)
                c = 256 * (h % 2)
                dve.tensor_tensor(o[:, :, h, :], m.banks[7][:, c:c + 256].rearrange("p (t n) -> p t n", n=64),
                                  total[:, h].unsqueeze(2).broadcast_to([P, NT, 64]), ALU.mult).then_inc(ph.sem("o"), 1)

            masked(0)
            for h in range(FH):
                if h + 1 < FH:
                    masked(h + 1)
                if h >= 1:
                    output(h - 1)
            output(FH - 1)
            dve.wait_ge(ph.sem("o"), FH)
            v.link(dve.tensor_tensor(sq[:], o[:], o[:], ALU.mult))
            v.link(dve.tensor_reduce(rms[:], sq[:], AX_X, ALU.add))
            dve.tensor_scalar(rms[:], rms[:], 1.0 / 64, EPS, ALU.mult, ALU.add).then_inc(ph.sem("mean"), 1)
            dve.wait_ge(ph.sem("deviation"), 1)
            v.link(dve.reciprocal(rms[:], rms[:]))
            dve.tensor_tensor(o[:], o[:], rms.unsqueeze(3).broadcast_to([P, NT, FH, 64]), ALU.mult).then_inc(ph.sem("normed"), 1)
            dve.wait_ge(ph.sem("o_turned"), 1)
            g = COLUMN["fox_norm_2"]
            for c in range(HC):
                v.mark(dve.tensor_scalar(m.mixT[:, HC + c, :], m.banks[c][:], m.params[:, g:g + 1], None, ALU.mult))
            v.wait()

        @block.scalar
        def _(act):
            def exps(h):
                act.wait_ge(ph.sem("max"), h + 1)
                if h >= 2:
                    act.wait_ge(ph.sem("turned"), 3 * (h - 1))
                for t in range(NT):
                    act.activation(p2[:, h % 2, F_FLAT[t]:F_FLAT[t] + (t + 1) * P], region(h, t), ACT.Exp, bias=mx[:, h, t:t + 1],
                                   accum_out=total[:, h, t:t + 1]).then_inc(ph.sem("exp"), 1)

            def probabilities(h):
                for i, (a, b) in enumerate(parts):
                    act.wait_ge(ph.sem("turned"), 3 * h + i + 1)
                    if h >= 2:
                        act.wait_ge(ph.sem("values"), h - 1)
                    act.activation(pt[:, h % 2, a:b, :], m.banks[6][:, 0:(b - a) * P].rearrange("p (a b) -> p a b", b=P),
                                   ACT.Copy).then_inc(ph.sem("pt"), 1)

            for h in range(FH):
                exps(h)
                probabilities(h)
            act.wait_ge(ph.sem("mean"), 1)
            act.activation(rms[:], rms[:], ACT.Sqrt).then_inc(ph.sem("deviation"), 1)
    ph.close()
INPUTS = [
    "x", "norm_mix_g", "w_in", "shift_mu", "sb_out_g", "rw_w0", "rw_w2", "rw_a0", "rw_a2", "rw_g2", "rw_k_k", "rw_k_a",
    "rw_r_k", "rw_ln_w", "rw_ln_b", "w_out", "norm_ffn_g", "router_grp_w", "router_grp_b", "router_exp_w",
    "router_exp_b", "exp_w_gate", "exp_w_up", "exp_w_down", "final_norm_g", "attn_norm_2", "w_in_2",
    "hg_lb_logits_2", "hg_norm_2", "fox_f_bias_2", "fox_norm_2", "w_out_2", "ffn_norm_2", "w_group_2",
    "b_group_2", "w_expert_2", "b_expert_2", "w_gate_2", "w_up_2", "w_down_2", "final_norm_2",
]


def two_blocks_kernel(nc, io, out):
    with ExitStack() as ctx:
        m = Memory(nc, ctx)
        ring = [[nc.alloc_semaphore(f"experts{b}_ring{s}") for s in range(4)] for b in range(2)]
        between = nc.dram_tensor("between_blocks", (1, S, D), F32, kind="Internal").ap()

        setup_phase(nc, m, io)

        x = Mix1(m)
        g2s, _ = m.view(m.arena_size - HW, HW)
        phase_project1(nc, m, io, g2s)
        phase_stick(nc, m, x)
        phase_rwkv(nc, m, x, g2s)
        z = Moe(m, 32, 8, 1, 64, 1)
        z.weights = ("exp_w_gate", "exp_w_up", "exp_w_down")
        phase_out(nc, m, io, z, "out1", io["x"], "w_out", "norm_ffn_g",
                  ("router_grp_w", "router_grp_b", "router_exp_w", "router_exp_b"), ring[0])
        phase_moe(nc, m, io, z, "moe1", COLUMN["norm_ffn_g"], ring[0])

        y = Mix2(m)
        phase_final(nc, m, z, "end1", io["final_norm_g"], between, y.rows)
        phase_project2(nc, m, io, y)
        phase_hgrn(nc, m, y)
        phase_fox(nc, m, y)
        z = Moe(m, 16, 4, 2, 96, 2)
        z.weights = ("w_gate_2", "w_up_2", "w_down_2")
        phase_out(nc, m, io, z, "out2", between, "w_out_2", "ffn_norm_2",
                  ("w_group_2", "b_group_2", "w_expert_2", "b_expert_2"), ring[1])
        phase_moe(nc, m, io, z, "moe2", COLUMN["ffn_norm_2"], ring[1])
        phase_final(nc, m, z, "end2", io["final_norm_2"], out, z.x)


def kernel(**inputs):
    import concourse.bacc as bacc
    from concourse.bass_utils import run_bass_kernel_spmd

    nc = bacc.Bacc("TRN2", target_bir_lowering=False, num_devices=1)
    arrays, io = {}, {}
    for name in INPUTS:
        a = np.ascontiguousarray(inputs[name])
        arrays[f"in_{name}"] = a
        io[name] = nc.dram_tensor(f"in_{name}", a.shape, mybir.dt.from_np(a.dtype), kind="ExternalInput").ap()
    out = nc.dram_tensor("out_0", (1, S, D), F32, kind="ExternalOutput").ap()
    two_blocks_kernel(nc, io, out)
    r = run_bass_kernel_spmd(nc, [arrays], core_ids=[0])
    return r.results[0]["out_0"]
```

```python
from contextlib import ExitStack

import numpy as np

import concourse.bass as bass
from concourse import mybir

ALU = mybir.AluOpType
ACT = mybir.ActivationFunctionType
F32 = mybir.dt.float32
F32R = mybir.dt.float32r
I32 = mybir.dt.int32
U32 = mybir.dt.uint32
AX_X = mybir.AxisListType.X

P = 128
S = 512
NT = S // P
D = 1024
DC = D // P
EPS = 1e-6
GN_EPS = 64e-5
HW = 512
HC = HW // P
CH = 64
NCH = S // CH
DECAY = float(np.exp(-0.5))
RING = 6144
LEVELS = (1, 2, 4, 8, 16, 32)


class Phase:

    def __init__(self, nc, name, ahead=None):
        self.nc, self.name, self.sems = nc, name, dict(ahead or {})

    def sem(self, name):
        if name not in self.sems:
            self.sems[name] = self.nc.alloc_semaphore(f"{self.name}_{name}")
        return self.sems[name]

    def close(self):
        self.nc.clear_and_free_semaphores(list(self.sems.values()))
        self.nc.all_engine_barrier()


class Chain:

    def __init__(self, engine, sem):
        self.engine, self.sem, self.n = engine, sem, 0

    def mark(self, instruction):
        self.n += 1
        instruction.then_inc(self.sem, 1)
        return self.n

    def wait(self, n=None):
        self.engine.wait_ge(self.sem, self.n if n is None else n)

    def link(self, instruction):
        self.mark(instruction)
        self.wait()


class Memory:

    def __init__(self, nc, ctx):
        self.nc = nc

        def sb(name, shape, dt=F32):
            return ctx.enter_context(nc.sbuf_tensor(name, shape, dt))

        self.ring01 = sb("ring01", [P, 2, RING])
        self.mixT = sb("mixT", [P, DC, S])
        self.rows = self.mixT[:].rearrange("p a s -> p (a s)").rearrange("p (t d) -> p t d", d=D)
        self.params = sb("params", [P, 96])
        self.ident = sb("ident", [P, P])
        self.masks = sb("masks", [P, len(LEVELS), P])
        self.m1low = sb("m1low", [P, P])
        self.tri3 = sb("tri3", [P, 3, P])
        self.after = sb("after", [P, P])
        self.negtri = sb("negtri", [P, P])
        self.negones = sb("negones", [P, P])
        self.ones = sb("ones", [P, P])
        self.same64 = sb("same64", [P, P])
        self.centre = sb("centre", [P, P])
        self.sel8 = sb("sel8", [8, 8, P])
        self.restart = sb("restart", [P, S])
        self.slots = sb("slots", [P, 2, P])
        self.experts = sb("experts", [P, 32])
        self.small = sb("small", [P, 64])
        self.rounds = sb("rounds", [P, 1], I32)
        self.banks = [ctx.enter_context(nc.psum_tensor(f"bank{i}", [P, 512], F32)) for i in range(8)]
        self.free = (229368 - 64 - nc.sbuf_base) // 4
        self.stretch = ExitStack()
        ctx.callback(lambda: self.stretch.close())
        self.open("mix1")

    def open(self, name, parts=()):
        self.stretch.close()
        self.stretch = ExitStack()
        rounded = dict(parts)
        self.arena_size = self.free - sum(int(np.prod(shape)) for shape in rounded.values())
        self.arena = self.stretch.enter_context(self.nc.sbuf_tensor(f"arena_{name}", [P, self.arena_size], F32))
        return {n: self.stretch.enter_context(self.nc.sbuf_tensor(f"{n}_{name}", [P, *shape], F32R))
                for n, shape in rounded.items()}

    def view(self, at, *shape, partitions=P, dt=None):
        n = int(np.prod(shape))
        assert at + n <= self.arena_size, (at, shape, self.arena_size)
        v = self.arena[0:partitions, at:at + n]
        if dt is not None:
            v = v.bitcast(dt)
        if len(shape) > 1:
            names = "abcdef"[:len(shape)]
            v = v.rearrange(f"p ({' '.join(names)}) -> p {' '.join(names)}", **dict(zip(names[1:], shape[1:])))
        return v, at + n


def bcast(ap, *shape):
    return ap.broadcast_to([ap.shape[0], *shape])


VECTORS = [("norm_mix_g", 8), ("shift_mu", 14), ("sb_out_g", 4), ("rw_w0", 4), ("rw_a0", 4), ("rw_k_k", 4),
           ("rw_k_a", 4), ("rw_r_k", 4), ("rw_ln_w", 4), ("rw_ln_b", 4), ("norm_ffn_g", 8),
           ("attn_norm_2", 8), ("hg_lb_logits_2", 8), ("hg_norm_2", 1), ("fox_norm_2", 1), ("ffn_norm_2", 8)]
COLUMN = {}
_at = 0
for _name, _n in VECTORS:
    COLUMN[_name] = _at
    _at += _n
NVEC = _at


def setup_phase(nc, m, io, load_ahead):
    ph = Phase(nc, "setup")
    raw, at = m.view(0, P)
    count, at = m.view(at, 2 * P, dt=I32)
    count2, at = m.view(at, 32, dt=I32)
    with nc.Block() as block:
        @block.sync
        def _(sp):
            load_ahead(sp)

        @block.scalar
        def _(act):
            for name, n in VECTORS:
                src = io[name]
                c = COLUMN[name]
                if name == "fox_norm_2":
                    for half in range(2):
                        act.dma_start(raw[c:c + 1, 64 * half:64 * half + 64], src).then_inc(ph.sem("vectors"), 16)
                    continue
                if len(src.shape) == 3:
                    src = src.rearrange("l h d -> l (h d)")
                act.dma_start(raw[c:c + n, :], src.rearrange("l (c p) -> (l c) p", p=P)).then_inc(ph.sem("vectors"), 16)

        @block.gpsimd
        def _(pool):
            g = Chain(pool, ph.sem("made"))

            def select(view, pattern, base, mult, op=ALU.is_ge, fill=0.0):
                g.link(pool.affine_select(out=view, in_=view, compare_op=op, fill=fill, base=base,
                                          pattern=pattern, channel_multiplier=mult))

            def same_block(t, n):
                v = t.rearrange("p (b c) -> p b c", c=n)
                select(v, [[-n, P // n], [0, n]], 0, 1)
                select(v, [[n, P // n], [0, n]], n - 1, -1)

            for t in (m.ident, m.masks, m.m1low, m.sel8):
                g.mark(pool.memset(t[:], 0.0))
            for t in (m.ones, m.same64, m.tri3, m.after, m.restart):
                g.mark(pool.memset(t[:], 1.0))
            g.mark(pool.memset(m.negones[:], -1.0))
            g.mark(pool.memset(m.negtri[:], -1.0))
            g.mark(pool.iota(count.rearrange("p (a b c) -> p a b c", a=2, b=2)[:, 0], [[0, 2], [1, 64]], base=0,
                             channel_multiplier=0))
            g.mark(pool.iota(count[:, P:2 * P], [[1, P]], base=0, channel_multiplier=0))
            g.link(pool.iota(count2, [[1, 32]], base=0, channel_multiplier=0))
            g.mark(pool.tensor_copy(m.slots[:].rearrange("p a b -> p (a b)"), count))
            g.mark(pool.tensor_copy(m.experts[:], count2))
            select(m.ident[:], [[-1, P]], 0, 1, ALU.not_equal, 1.0)
            select(m.sel8[:], [[-1, 8], [0, P]], 0, 1, ALU.not_equal, 1.0)
            for i, n in enumerate(LEVELS):
                v = m.masks[:, i, :].rearrange("p (b c) -> p b c", c=2 * n)
                g.link(pool.memset(v[:, :, n:2 * n], 1.0))
                select(v, [[-2 * n, P // (2 * n)], [0, 2 * n]], 0, 1)
                select(v, [[2 * n, P // (2 * n)], [0, 2 * n]], n - 1, -1)
            v = m.m1low[:].rearrange("p (b c) -> p b c", c=2)
            g.link(pool.memset(v[:, :, 0:1], 1.0))
            select(v, [[-2, P // 2], [0, 2]], -1, 1)
            select(v, [[2, P // 2], [0, 2]], 1, -1)
            same_block(m.same64[:], 64)
            for i in range(3):
                same_block(m.tri3[:, i, :], CH)
            select(m.tri3[:, 0, :], [[1, P]], -1, -1)
            select(m.tri3[:, 1, :], [[1, P]], 0, -1)
            select(m.tri3[:, 2, :], [[-1, P]], -1, 1)
            select(m.after[:], [[1, P]], -1, -1)
            select(m.negtri[:], [[-1, P]], 0, 1)
            v = m.restart[:].rearrange("p (b c) -> p b c", c=CH)
            g.link(pool.memset(v[:, :, 0:1], 0.0))
            pool.memset(m.small[:], 0.0).then_inc(ph.sem("constants"), 1)

        @block.vector
        def _(dve):
            v = Chain(dve, ph.sem("dve"))
            dve.wait_ge(ph.sem("constants"), 1)
            v.link(dve.tensor_scalar(m.centre[:], m.same64[:], -1.0 / 64, None, ALU.mult))
            v.link(dve.tensor_tensor(m.centre[:], m.centre[:], m.ident[:], ALU.add))
            dve.wait_ge(ph.sem("turned"), 1)
            v.link(dve.tensor_copy(m.params[:, 0:NVEC], m.banks[0][:, 0:NVEC]))

        @block.tensor
        def _(pe):
            pe.wait_ge(ph.sem("constants"), 1)
            pe.wait_ge(ph.sem("vectors"), 16 * (len(VECTORS) + 1))
            pe.transpose(m.banks[0][:, 0:NVEC], raw[0:NVEC, :], m.ident[0:NVEC, 0:NVEC]).then_inc(ph.sem("turned"), 1)
    ph.close()


def weight_item(sp, m, ring_sem, n, src, cols):
    v = m.ring01[:, n % 2, 0:DC * cols].rearrange("p (c n) -> p c n", n=cols)
    s = src.rearrange("(c p) n -> p c n", p=P)
    for a, b in ((0, 3), (3, 6), (6, 8)):
        sp.dma_start(v[:, a:b, :], s[:, a:b, :]).then_inc(ring_sem(n % 2), 16)


def item_view(m, n, cols):
    return m.ring01[:, n % 2, 0:DC * cols].rearrange("p (c n) -> p c n", n=cols)
def norm_act(act, ph, m, rows, scaled, arrived):
    for t in range(NT):
        arrived(act, t)
        act.activation(scaled[:, t, :], rows[:, t, :], ACT.Square, accum_out=m.small[:, t:t + 1]).then_inc(ph.sem("squares"), 1)
        act.wait_ge(ph.sem("mean"), t + 1)
        act.activation(m.small[:, 8 + t:9 + t], m.small[:, 4 + t:5 + t], ACT.Sqrt).then_inc(ph.sem("deviation"), 1)


def inverse_rms_dve(dve, ph, m, t, v):
    dve.wait_ge(ph.sem("squares"), t + 1)
    dve.tensor_scalar(m.small[:, 4 + t:5 + t], m.small[:, t:t + 1], 1.0 / D, EPS, ALU.mult, ALU.add).then_inc(ph.sem("mean"), 1)
    dve.wait_ge(ph.sem("deviation"), t + 1)
    v.link(dve.reciprocal(m.small[:, 12 + t:13 + t], m.small[:, 8 + t:9 + t]))


def norm_scale_dve(dve, ph, m, rows, scaled, v):
    for t in range(NT):
        inverse_rms_dve(dve, ph, m, t, v)
        dve.tensor_scalar(scaled[:, t, :], rows[:, t, :], m.small[:, 12 + t:13 + t], None, ALU.mult).then_inc(ph.sem("scaled"), 1)
    dve.wait_ge(ph.sem("scaled"), NT)


def norm_turn_pe(pe, ph, m, scaled):
    for t in range(NT):
        pe.wait_ge(ph.sem("scaled"), t + 1)
        for half in range(2):
            for j in range(4):
                c = 4 * half + j
                last = pe.transpose(m.banks[2 * t + half][:, j * P:(j + 1) * P], scaled[:, t, c * P:(c + 1) * P], m.ident[:])
            last.then_inc(ph.sem("turned"), 1)


def norm_gain_dve(dve, ph, m, gain):
    for t in range(NT):
        for half in range(2):
            dve.wait_ge(ph.sem("turned"), 2 * t + half + 1)
            g = m.params[:, gain + 4 * half:gain + 4 * half + 4].unsqueeze(2).broadcast_to([P, 4, P])
            dve.tensor_tensor(m.mixT[:, 4 * half:4 * half + 4, t * P:(t + 1) * P],
                              m.banks[2 * t + half][:].rearrange("p (a b) -> p a b", b=P), g,
                              ALU.mult).then_inc(ph.sem("normed"), 1)


NORMED = 2 * NT


def project_pe(pe, ph, m, n, cols, chunks, first, ring_count, rows_form):
    w = item_view(m, n, cols)
    pe.wait_ge(ph.sem(f"ring{n % 2}"), ring_count)
    for i in range(chunks):
        k = first + i
        bank = m.banks[k % 6]
        if k >= 6:
            pe.wait_ge(ph.sem("taken"), k - 5)
        for c in range(DC):
            if rows_form:
                last = pe.matmul(bank[:, 0:4 * P], m.mixT[:, c, i * P:(i + 1) * P], w[:, c, 0:4 * P],
                                 start=(c == 0), stop=(c == DC - 1))
            else:
                last = pe.matmul(bank[:], w[:, c, i * P:(i + 1) * P], m.mixT[:, c, :],
                                 start=(c == 0), stop=(c == DC - 1))
        last.then_inc(ph.sem("projected"), 1)


class Mix1:

    def __init__(self, m):
        at = 0
        self.k, at = m.view(at, HC, S + 1)
        self.r, at = m.view(at, HC, S + 1)
        self.v_at = at
        self.v, at = m.view(at, HC, S + 1)
        self.x, at = m.view(at, 2, S + 1)
        self.ar, at = m.view(at, HC, NT, 2, P)
        self.ar_flat = self.ar.rearrange("p a b c d -> p (a b c d)")
        self.kk, at = m.view(at, HC, S)
        self.bonus = self.r
        self.dc, at = m.view(at, HC, NCH)
        self.free1 = at
        self.w1, at = m.view(at, HC, S)
        self.w2, at = m.view(at, HC, S)
        self.a, at = m.view(at, HC, S)
        self.sc, at = m.view(at, HC, S)
        self.tmp, at = m.view(at, 2, S)
        self.lw, at = m.view(at, S)
        self.omka, at = m.view(at, HC)
        self.sb = at
        self.q, at = m.view(at, HC, S)
        self.kb, at = m.view(at, HC, S)
        self.vb, at = m.view(at, NT, HW)
        self.end = at
        self.rows, end = m.view(self.free1, NT, D)
        self.scaled, end = m.view(end, NT, D)


ITEMS1 = [[(6 * HW, 256), (5 * HW, HW)], [(4 * HW, HW)], [(3 * HW, HW)], [(0, HW)], [(HW, HW)], [(2 * HW, HW)]]


def load_item1(sp, m, io, n, sem):
    w_in = io["w_in"].rearrange("l d n -> (l d) n")
    at = 0
    v = item_view(m, n, sum(w for _, w in ITEMS1[n]))
    for c0, w in ITEMS1[n]:
        src = w_in[:, c0:c0 + w].rearrange("(c p) n -> p c n", p=P)
        for a, b in ((0, 4), (4, 8)):
            sp.dma_start(v[:, a:b, at:at + w], src[:, a:b, :]).then_inc(sem, 16)
        at += w


def load_first(sp, m, io, x, ahead):
    xin = io["x"].rearrange("b (t p) d -> p (b t) d", p=P)
    for t in range(NT):
        sp.dma_start(x.rows[:, t, :], xin[:, t, :]).then_inc(ahead["rows"], 16)
    for n in range(2):
        load_item1(sp, m, io, n, ahead[f"ring{n}"])


def phase_project1(nc, m, io, g2s, ahead):
    ph = Phase(nc, "p1", ahead)
    x = Mix1(m)
    items = ITEMS1
    sizes = [6, 4, 4, 4, 4, 4]
    first = [sum(sizes[:i]) for i in range(6)]
    mu = COLUMN["shift_mu"]
    dest = [(x.x, 0, mu + 12), (x.x, 1, mu + 13)] + [(x.v, c, mu + 8 + c) for c in range(4)] \
        + [(x.k, c, mu + 4 + c) for c in range(4)] + [(x.r, c, mu + c) for c in range(4)]
    col = lambda name, c: m.params[:, COLUMN[name] + c:COLUMN[name] + c + 1]
    cols4 = lambda name: m.params[:, COLUMN[name]:COLUMN[name] + 4].unsqueeze(2).broadcast_to([P, 4, S])
    K, R, V = x.k[:, :, 1:], x.r[:, :, 1:], x.v[:, :, 1:]
    A4 = x.ar[:, :, :, 0, :]
    R4 = x.ar[:, :, :, 1, :]
    t4 = lambda ap: ap.rearrange("p a (t n) -> p a t n", n=P)

    with nc.Block() as block:
        @block.sync
        def _(sp):
            sp.dma_start(x.lw[0:64, :], io["rw_w2"][0]).then_inc(ph.sem("low"), 16)
            sp.dma_start(x.lw[64:128, :], io["rw_a2"][0]).then_inc(ph.sem("low"), 16)
            sp.dma_start(g2s, io["rw_g2"][0]).then_inc(ph.sem("low"), 16)
            for n in range(2, len(items)):
                sp.wait_ge(ph.sem("projected"), first[n - 1])
                load_item1(sp, m, io, n, ph.sem(f"ring{n % 2}"))
            sp.wait_ge(ph.sem("low"), 48)

        ring_counts = [64, 32, 96, 64, 128, 96]

        @block.scalar
        def _(act):
            a = Chain(act, ph.sem("act"))
            norm_act(act, ph, m, x.rows, x.scaled, lambda e, t: e.wait_ge(ph.sem("rows"), 64))

            def take(k):
                act.wait_ge(ph.sem("projected"), k + 1)
                bank = m.banks[k % 6][:]
                if k < 14:
                    out, scale = dest[k][0][:, dest[k][1], 1:], 1.0
                elif k < 18:
                    out, scale = x.q[:, k - 14, :], 0.125
                elif k < 22:
                    out, scale = x.kb[:, k - 18, :], 1.0
                else:
                    out, scale = x.vb[:, k - 22, :], 1.0
                act.activation(out, bank, ACT.Copy, scale=scale).then_inc(ph.sem("taken"), 1)

            for k in range(10):
                take(k)
            act.wait_ge(ph.sem("mixed"), 1)
            act.activation(x.x[0:64, 0, 1:], x.x[0:64, 0, 1:], ACT.Tanh).then_inc(ph.sem("low_in"), 1)
            act.wait_ge(ph.sem("mixed"), 2)
            a.mark(act.activation(x.x[:, 1, 1:], x.x[:, 1, 1:], ACT.Sigmoid))
            for c in range(HC):
                act.wait_ge(ph.sem("low_out"), 2 * c + 1)
                act.activation(x.w1[:, c, :], m.banks[6][:], ACT.Sigmoid, bias=col("rw_w0", c)).then_inc(ph.sem("gates"), 1)
                act.wait_ge(ph.sem("low_out"), 2 * c + 2)
                act.activation(x.a[:, c, :], m.banks[7][:], ACT.Sigmoid, bias=col("rw_a0", c)).then_inc(ph.sem("gates"), 1)
            for k in range(10, 14):
                take(k)
            act.wait_ge(ph.sem("kk"), 1)
            act.activation(x.sc[:], x.kk[:], ACT.Square).then_inc(ph.sem("kk_squares"), 1)
            act.wait_ge(ph.sem("kk_bounded"), HC)
            a.link(act.activation(x.sc[:], x.sc[:], ACT.Ln))
            act.activation(x.sc[:], x.sc[:], ACT.Exp, scale=-0.5).then_inc(ph.sem("kk_inverse"), 1)
            act.wait_ge(ph.sem("cumulated"), 1)
            for c in range(HC):
                act.activation(A4[:, c], t4(x.w1)[:, c], ACT.Exp).then_inc(ph.sem("decays"), 1)
                act.activation(R4[:, c], t4(x.w2)[:, c], ACT.Exp).then_inc(ph.sem("decays"), 1)
            ends = x.w2.rearrange("p a (c n) -> p a c n", n=CH)[:, :, :, CH - 1]
            a.link(act.activation(x.dc[:], ends, ACT.Exp))
            act.activation(x.w2[:], x.w2[:], ACT.Exp, scale=-1.0).then_inc(ph.sem("inverse"), 1)
            for k in range(14, 26):
                take(k)

        @block.vector
        def _(dve):
            v = Chain(dve, ph.sem("dve"))
            for t in (x.k, x.r, x.v, x.x):
                v.mark(dve.memset(t[:, :, 0:1], 0.0))
            norm_scale_dve(dve, ph, m, x.rows, x.scaled, v)
            norm_gain_dve(dve, ph, m, COLUMN["norm_mix_g"])

            def shift(k):
                buf, c, mu_col = dest[k]
                dve.wait_ge(ph.sem("taken"), k + 1)
                if k >= 2:
                    dve.wait_ge(ph.sem("mixed"), k - 1)
                v.link(dve.tensor_tensor(x.tmp[:, k % 2, :], buf[:, c, 0:S], buf[:, c, 1:], ALU.subtract))
                dve.scalar_tensor_tensor(buf[:, c, 1:], x.tmp[:, k % 2, :], m.params[:, mu_col:mu_col + 1],
                                         buf[:, c, 1:], ALU.mult, ALU.add).then_inc(ph.sem("mixed"), 1)

            v.wait()
            for k in range(10):
                shift(k)
            dve.wait_ge(ph.sem("mixed"), 10)
            dve.tensor_tensor(x.kk[:], K, cols4("rw_k_k"), ALU.mult).then_inc(ph.sem("kk"), 1)
            v.link(dve.tensor_scalar(x.omka[:], m.params[:, COLUMN["rw_k_a"]:COLUMN["rw_k_a"] + 4], -1.0, 1.0, ALU.mult, ALU.add))
            dve.wait_ge(ph.sem("gates"), 2 * HC)
            v.link(dve.tensor_scalar(x.w1[:], x.w1[:], -DECAY, None, ALU.mult))
            for c in range(HC):
                v.mark(dve.tensor_tensor_scan(x.w2[:, c, :], m.restart[:], x.w1[:, c, :], 0.0, ALU.mult, ALU.add))
            v.wait()
            dve.tensor_tensor(x.w1[:], x.w2[:], x.w1[:], ALU.subtract).then_inc(ph.sem("cumulated"), 1)
            for c in range(HC):
                dve.wait_ge(ph.sem("kk_sums"), c + 1)
                dve.tensor_scalar(x.sc[:, c, :], m.banks[6 + c % 2][:], 1e-24, None, ALU.max).then_inc(ph.sem("kk_bounded"), 1)
            dve.wait_ge(ph.sem("kk_inverse"), 1)
            v.link(dve.tensor_tensor(x.kk[:], x.kk[:], x.sc[:], ALU.mult))
            for c in range(HC):
                v.mark(dve.tensor_scalar(x.sc[:, c, :], x.a[:, c, :], col("rw_k_a", c), x.omka[:, c:c + 1], ALU.mult, ALU.add))
            v.wait()
            v.link(dve.tensor_tensor(K, K, x.sc[:], ALU.mult))
            for k in range(10, 14):
                shift(k)
            dve.wait_ge(ph.sem("mixed"), 14)
            for c in range(HC):
                dve.scalar_tensor_tensor(x.sc[:, c, :], R[:, c, :], col("rw_r_k", c), K[:, c, :], ALU.mult,
                                         ALU.mult).then_inc(ph.sem("rk"), 1)
            dve.wait_ge(ph.sem("decays"), 2 * HC)
            for c in range(HC):
                v.mark(dve.scalar_tensor_tensor(A4[:, c], t4(x.kk)[:, c], -1.0, A4[:, c], ALU.mult, ALU.mult))
                v.mark(dve.tensor_tensor(R4[:, c], t4(R)[:, c], R4[:, c], ALU.mult))
            v.wait()
            v.link(dve.tensor_tensor(x.kk[:], x.kk[:], x.a[:], ALU.mult))
            dve.wait_ge(ph.sem("inverse"), 1)
            v.mark(dve.tensor_tensor(x.kk[:], x.kk[:], x.w2[:], ALU.mult))
            dve.wait_ge(ph.sem("rk"), HC)
            v.mark(dve.tensor_tensor(K, K, x.w2[:], ALU.mult))
            for c in range(HC):
                dve.wait_ge(ph.sem("bonus"), c + 1)
                dve.tensor_tensor(x.bonus[:, c, 1:], m.banks[6 + c % 2][:], V[:, c, :], ALU.mult).then_inc(ph.sem("bonus_taken"), 1)

        @block.tensor
        def _(pe):
            norm_turn_pe(pe, ph, m, x.scaled)
            pe.wait_ge(ph.sem("normed"), NORMED)

            def item(n):
                project_pe(pe, ph, m, n, sum(w for _, w in items[n]), sizes[n], first[n], ring_counts[n], n == 5)

            item(0)
            item(1)
            pe.wait_ge(ph.sem("low"), 48)
            pe.wait_ge(ph.sem("low_in"), 1)
            for c in range(HC):
                for half in range(2):
                    if c:
                        pe.wait_ge(ph.sem("gates"), 2 * c - 1 + half)
                    o = 64 * half
                    pe.matmul(m.banks[6 + half][:], x.lw[o:o + 64, c * P:(c + 1) * P], x.x[o:o + 64, 0, 1:],
                              start=True, stop=True).then_inc(ph.sem("low_out"), 1)
            item(2)
            pe.wait_ge(ph.sem("gates"), 2 * HC)
            pe.wait_ge(ph.sem("kk_squares"), 1)
            for c in range(HC):
                if c >= 2:
                    pe.wait_ge(ph.sem("kk_bounded"), c - 1)
                pe.matmul(m.banks[6 + c % 2][:], m.same64[:], x.sc[:, c, :], start=True, stop=True).then_inc(ph.sem("kk_sums"), 1)
            item(3)
            pe.wait_ge(ph.sem("rk"), HC)
            for c in range(HC):
                if c >= 2:
                    pe.wait_ge(ph.sem("bonus_taken"), c - 1)
                pe.matmul(m.banks[6 + c % 2][:], m.same64[:], x.sc[:, c, :], start=True, stop=True).then_inc(ph.sem("bonus"), 1)
            item(4)
            item(5)
    ph.close()
Z_PLACE = [(0, 0), (1, 0), (2, 0), (1, 384)]
Z_FLAT = [0, 512, 1024, 896]
Z_BANKS = [(0, 512), (512, 512), (1024, 256)]


def inverse_root_act(act, ph, sq, n):
    for p in range(n):
        act.wait_ge(ph.sem("mean"), p + 1)
        act.activation(sq[:, p, :], sq[:, p, :], ACT.Ln).then_inc(ph.sem("logs"), 1)
    for p in range(n):
        act.wait_ge(ph.sem("logs"), p + 1)
        act.activation(sq[:, p, :], sq[:, p, :], ACT.Exp, scale=-0.5).then_inc(ph.sem("inverse_root"), 1)


def phase_stick(nc, m, x):
    ph = Phase(nc, "sb")
    heads = 2 * HC
    at = x.free1
    sp2, at = m.view(at, 2, 1280)
    wt2, at = m.view(at, 2, 1280)
    sq, at = m.view(x.free1, HC, S)
    assert at <= x.sb

    def qk(t, h):
        return t[64 * (h % 2):64 * (h % 2) + 64, h // 2, :]

    def zbank(h, i):
        return m.banks[3 * (h % 2) + i]

    def z_region(h, c, t0=None):
        t0 = c if t0 is None else t0
        b, o = Z_PLACE[c]
        return zbank(h, b)[:, o + (t0 - c) * P:o + S - c * P]

    with nc.Block() as block:
        @block.tensor
        def _(pe):
            def scores(h):
                if h >= 2:
                    pe.wait_ge(ph.sem("weights"), 3 * (h - 1))
                for c in (0, 1, 2, 3):
                    last = pe.matmul(z_region(h, c), qk(x.kb, h)[:, c * P:(c + 1) * P], qk(x.q, h)[:, c * P:],
                                     start=(c != 3), stop=True, skip_group_check=True)
                last.then_inc(ph.sem("scores"), 1)

            def suffixes(h):
                pe.wait_ge(ph.sem("masked"), 2 * (h + 1))
                sp = sp2[:, h % 2, :]
                for c in range(NT):
                    for j in range(c, NT):
                        last = pe.matmul(z_region(h, c, j), (m.negtri if j == c else m.negones)[:],
                                         sp[:, Z_FLAT[j]:Z_FLAT[j] + S - j * P], start=False, stop=True,
                                         skip_group_check=True)
                last.then_inc(ph.sem("exponents"), 1)

            def values(h):
                pe.wait_ge(ph.sem("causal"), 2 * (h + 1))
                if h >= 4 and h % 2 == 0:
                    pe.wait_ge(ph.sem("output"), h // 2 - 1)
                o = 64 * (h % 2)
                w = wt2[:, h % 2, :]
                for c in range(NT):
                    last = pe.matmul(m.banks[6 + h // 2 % 2][o:o + 64, c * P:], x.vb[:, c, 64 * h:64 * h + 64],
                                     w[:, Z_FLAT[c]:Z_FLAT[c] + S - c * P], start=(c == 0), stop=(c == NT - 1),
                                     skip_group_check=True)
                last.then_inc(ph.sem("values"), 1)

            scores(0)
            for h in range(heads):
                if h + 1 < heads:
                    scores(h + 1)
                suffixes(h)
                if h >= 1:
                    values(h - 1)
            values(heads - 1)
            for p in range(HC):
                pe.wait_ge(ph.sem("squared"), p + 1)
                pe.matmul(m.banks[p][:], m.same64[:], sq[:, p, :], start=True, stop=True).then_inc(ph.sem("sums"), 1)

        @block.scalar
        def _(act):
            def softplus(h):
                act.wait_ge(ph.sem("scores"), h + 1)
                if h >= 2:
                    act.wait_ge(ph.sem("exponents"), h - 1)
                sp = sp2[:, h % 2, :]
                for i, (o, n) in enumerate(Z_BANKS):
                    act.activation(sp[:, o:o + n], zbank(h, i)[:, 0:n], ACT.Abs).then_inc(ph.sem("abs"), 1)
                act.wait_ge(ph.sem("abs"), 3 * (h + 1))
                act.activation(sp, sp, ACT.Exp, scale=-1.0).then_inc(ph.sem("exp"), 1)
                act.wait_ge(ph.sem("exp"), h + 1)
                act.activation(sp, sp, ACT.Ln, bias=1.0).then_inc(ph.sem("ln"), 1)

            def weights(h):
                act.wait_ge(ph.sem("exponents"), h + 1)
                if h >= 2:
                    act.wait_ge(ph.sem("values"), h - 1)
                for i, (o, n) in enumerate(Z_BANKS):
                    act.activation(wt2[:, h % 2, o:o + n], zbank(h, i)[:, 0:n], ACT.Exp).then_inc(ph.sem("weights"), 1)

            def output(p):
                act.wait_ge(ph.sem("values"), 2 * p + 2)
                act.activation(m.mixT[:, p, :], m.banks[6 + p % 2][:], ACT.Copy).then_inc(ph.sem("output"), 1)

            softplus(0)
            for h in range(heads):
                if h + 1 < heads:
                    softplus(h + 1)
                weights(h)
                if h >= 3 and h % 2 == 1:
                    output((h - 3) // 2)
            output(HC - 1)
            act.wait_ge(ph.sem("output"), HC)
            for p in range(HC):
                act.activation(sq[:, p, :], m.mixT[:, p, :], ACT.Square).then_inc(ph.sem("squared"), 1)
            inverse_root_act(act, ph, sq, HC)

        @block.vector
        def _(dve):
            v = Chain(dve, ph.sem("dve"))
            diagonal = m.after[:].unsqueeze(1).broadcast_to([P, 3, P])
            for h in range(heads):
                dve.wait_ge(ph.sem("ln"), h + 1)
                sp = sp2[:, h % 2, :]
                for i, (o, n) in enumerate(Z_BANKS):
                    v.mark(dve.scalar_tensor_tensor(sp[:, o:o + n], zbank(h, i)[:, 0:n], 0.0, sp[:, o:o + n], ALU.max, ALU.add))
                v.wait()
                d3 = sp.rearrange("p (a b) -> p a b", b=256)[:, 0:5:2, 0:P]
                dve.tensor_tensor(d3, d3, diagonal, ALU.mult).then_inc(ph.sem("masked"), 1)
                d1 = sp[:, Z_FLAT[3]:Z_FLAT[3] + P]
                dve.tensor_tensor(d1, d1, m.after[:], ALU.mult).then_inc(ph.sem("masked"), 1)
            for p in range(HC):
                dve.wait_ge(ph.sem("sums"), p + 1)
                dve.tensor_scalar(sq[:, p, :], m.banks[p][:], 1.0 / 64, EPS, ALU.mult, ALU.add).then_inc(ph.sem("mean"), 1)
            g = COLUMN["sb_out_g"]
            for p in range(HC):
                dve.wait_ge(ph.sem("inverse_root"), p + 1)
                v.mark(dve.scalar_tensor_tensor(m.mixT[:, p, :], m.mixT[:, p, :], m.params[:, g + p:g + p + 1], sq[:, p, :],
                                                ALU.mult, ALU.mult))
            v.wait()

        @block.gpsimd
        def _(pool):
            for h in range(heads):
                pool.wait_ge(ph.sem("weights"), 3 * (h + 1))
                w = wt2[:, h % 2, :]
                d3 = w.rearrange("p (a b) -> p a b", b=256)[:, 0:5:2, 0:P]
                pool.affine_select(out=d3, in_=d3, compare_op=ALU.is_gt, fill=0.0, base=0, pattern=[[0, 3], [1, P]],
                                   channel_multiplier=-1).then_inc(ph.sem("causal"), 1)
                d1 = w[:, Z_FLAT[3]:Z_FLAT[3] + P]
                pool.affine_select(out=d1, in_=d1, compare_op=ALU.is_gt, fill=0.0, base=0, pattern=[[1, P]],
                                   channel_multiplier=-1).then_inc(ph.sem("causal"), 1)
    ph.close()


def phase_rwkv(nc, m, x, g2s, load_ahead):
    ph = Phase(nc, "rw")
    at = x.free1
    brow, at = m.view(at, HC, NT, P)
    krow, at = m.view(at, HC, NT, P)
    vrow, at = m.view(at, HC, NT, P)
    rb, at = m.view(at, HC, 2, NT, P)
    st, at = m.view(at, NCH + 1, HC, 64)
    lt, at = m.view(at, 2, NT, P)
    lo, at = m.view(at, 2, NT, P)
    mk, at = m.view(at, 2, NT, 2, P)
    tt, at = m.view(at, 2, 2, NT, P)
    assert at <= m.arena_size - S, (at, m.arena_size)
    flat = x.v_at
    xp, flat = m.view(flat, 2, NT, P)
    arow, flat = m.view(flat, NT, P)
    w1, flat = m.view(flat, 2, NT, 64)
    sq, _ = m.view(x.free1, HC, S)
    oc, _ = m.view(x.free1 + HC * S, HC, S)
    A4, R4 = x.ar[:, :, :, 0, :], x.ar[:, :, :, 1, :]
    K = x.k[:, :, 1:]
    uw = x.kk
    uw4 = uw.rearrange("p a (t n) -> p a t n", n=P)
    ident4 = m.ident[:].unsqueeze(1).broadcast_to([P, NT, P])
    mask4 = lambda t: t.unsqueeze(1).broadcast_to([P, NT, P])
    bank4 = lambda i: m.banks[i][:].rearrange("p (t n) -> p t n", n=P)
    levels = len(LEVELS)

    def first_inverse(engine, chain, q):
        chain.mark(engine.tensor_tensor(tt[:, q, 0], lo[:, q], mask4(m.m1low[:]), ALU.mult))
        chain.link(engine.tensor_tensor(tt[:, q, 1], lt[:, q], mask4(m.masks[:, 0, :]), ALU.mult))
        engine.tensor_tensor(tt[:, q, 0], tt[:, q, 0], ident4, ALU.add).then_inc(ph.sem(f"first{q}"), 1)
        engine.tensor_tensor(tt[:, q, 1], tt[:, q, 1], ident4, ALU.add).then_inc(ph.sem(f"first{q}"), 1)

    with nc.Block() as block:
        @block.sync
        def _(sp):
            load_ahead(sp)

        @block.tensor
        def _(pe):
            i = 0
            for p in range(HC):
                for src in (x.kk[:, p, :], K[:, p, :], x.v[:, p, 1:]):
                    if i >= 6:
                        pe.wait_ge(ph.sem("rows"), i - 5)
                    for t in range(NT):
                        last = pe.transpose(m.banks[i % 6][:, t * P:(t + 1) * P], src[:, t * P:(t + 1) * P], m.ident[:])
                    last.then_inc(ph.sem("turned"), 1)
                    i += 1
            pe.wait_ge(ph.sem("rows"), 3 * HC)
            for p in range(HC):
                if p:
                    pe.wait_ge(ph.sem("post"), 4 * p)
                for t in range(NT):
                    last = pe.transpose(m.banks[6][:, t * P:(t + 1) * P], A4[:, p, t, :], m.ident[:])
                last.then_inc(ph.sem("arow"), 1)
                for q in range(2):
                    o = 64 * q
                    for t in range(NT):
                        u = NT * q + t
                        if u >= 2:
                            pe.wait_ge(ph.sem("products_taken"), 4 * (2 * NT * p + u - 1))
                        e0, e1 = m.banks[2 * (u % 2)], m.banks[2 * (u % 2) + 1]
                        b = x.kk[o:o + 64, p, t * P:(t + 1) * P]
                        k = K[o:o + 64, p, t * P:(t + 1) * P]
                        ar = x.ar[o:o + 64, p, t, :, :].rearrange("p a b -> p (a b)")
                        pe.matmul(e0[:, 0:2 * P], b, ar, start=True, stop=True)
                        pe.matmul(e0[:, 2 * P:3 * P], A4[o:o + 64, p, t, :], b, start=True, stop=True)
                        pe.matmul(e1[:, 0:2 * P], k, ar, start=True, stop=True).then_inc(ph.sem("products"), 1)
                pe.wait_ge(ph.sem("products_taken"), 4 * 2 * NT * (p + 1))
                for n in range(1, levels):
                    for q in range(2):
                        done = p * (levels - 1) + n - 1
                        pe.wait_ge(ph.sem(f"part{q}"), done + 1)
                        if n > 1:
                            pe.wait_ge(ph.sem(f"inverse{q}"), 2 * done - p)
                        else:
                            pe.wait_ge(ph.sem(f"first{q}"), 2 * (p + 1))
                        for t in range(NT):
                            last = pe.matmul(m.banks[4 + q][:, t * P:(t + 1) * P], lo[:, q, t, :], tt[:, q, 0, t, :],
                                             start=True, stop=True)
                        last.then_inc(ph.sem(f"lt{q}"), 1)
                    for q in range(2):
                        done = p * (levels - 1) + n - 1
                        pe.wait_ge(ph.sem(f"xp{q}"), done + 1)
                        if n < levels - 1:
                            for t in range(NT):
                                last = pe.matmul(m.banks[2 * q][:, t * P:(t + 1) * P], tt[:, q, 1, t, :], xp[:, q, t, :],
                                                 start=True, stop=True)
                            last.then_inc(ph.sem(f"merged{q}"), 1)
                        for t in range(NT):
                            last = pe.matmul(m.banks[2 * q + 1][:, t * P:(t + 1) * P], xp[:, q, t, :], tt[:, q, 1, t, :],
                                             start=True, stop=True)
                        last.then_inc(ph.sem(f"merged{q}"), 1)
                per_pair = 2 * (levels - 1) - 1
                pe.wait_ge(ph.sem("inverse0"), per_pair * (p + 1))
                pe.wait_ge(ph.sem("inverse1"), per_pair * (p + 1))
                pe.wait_ge(ph.sem("arow_taken"), p + 1)
                for q in range(2):
                    for t in range(NT):
                        last = pe.matmul(m.banks[6][:, (NT * q + t) * 64:(NT * q + t + 1) * 64], mk[:, q, t, 0, :],
                                         vrow[:, p, t, 64 * q:64 * q + 64], start=True, stop=True)
                last.then_inc(ph.sem("mv"), 1)
                for q in range(2):
                    for t in range(NT):
                        last = pe.matmul(m.banks[4][64 * q:64 * q + 64, t * P:(t + 1) * P], arow[:, t, 64 * q:64 * q + 64],
                                         tt[:, q, 1, t, :], start=True, stop=True)
                last.then_inc(ph.sem("ta"), 1)
                for q in range(2):
                    for t in range(NT):
                        last = pe.matmul(m.banks[5][64 * q:64 * q + 64, t * P:(t + 1) * P], vrow[:, p, t, 64 * q:64 * q + 64],
                                         mk[:, q, t, 1, :], start=True, stop=True)
                last.then_inc(ph.sem("rkv"), 1)
                pe.wait_ge(ph.sem("post"), 4 * p + 1)
                for q in range(2):
                    for t in range(NT):
                        last = pe.matmul(m.banks[7][:, (NT * q + t) * 64:(NT * q + t + 1) * 64], tt[:, q, 1, t, :],
                                         w1[:, q, t, :], start=True, stop=True)
                last.then_inc(ph.sem("tmv"), 1)
            pe.wait_ge(ph.sem("post"), 4 * HC)
            for c in range(NCH):
                b, t = 64 * (c % 2), c // 2
                sbank = m.banks[2 + c % 2]
                pe.wait_ge(ph.sem("state"), 2 * c + 1)
                for q in range(2):
                    for p in range(HC):
                        last = pe.matmul(m.banks[q][b:b + 64, p * 64:(p + 1) * 64],
                                         A4[64 * q:64 * q + 64, p, t, b:b + 64], st[64 * q:64 * q + 64, c, p, :],
                                         start=True, stop=True)
                last.then_inc(ph.sem("u"), 1)
                for q in range(2):
                    for p in range(HC):
                        pe.matmul(sbank[64 * q:64 * q + 64, p * 64:(p + 1) * 64], krow[b:b + 64, p, t, 64 * q:64 * q + 64],
                                  vrow[b:b + 64, p, t, 64 * q:64 * q + 64], start=(p == 0), stop=True, skip_group_check=True)
                pe.wait_ge(ph.sem("u_done"), 2 * c + 2)
                for q in range(2):
                    for p in range(HC):
                        last = pe.matmul(sbank[64 * q:64 * q + 64, p * 64:(p + 1) * 64], brow[b:b + 64, p, t, 64 * q:64 * q + 64],
                                         uw4[b:b + 64, p, t, 64 * q:64 * q + 64], start=False, stop=True, skip_group_check=True)
                last.then_inc(ph.sem("s"), 1)
            pe.wait_ge(ph.sem("state"), 2 * NCH)
            for p in range(HC):
                for q in range(2):
                    o = 64 * q
                    for t in range(NT):
                        out = m.banks[4 + p][o:o + 64, t * P:(t + 1) * P]
                        pe.matmul(out, uw4[:, p, t, o:o + 64], rb[:, p, q, t, :], start=True, stop=True, skip_group_check=True)
                        for half in range(2):
                            last = pe.matmul(out[:, 64 * half:64 * half + 64], st[o:o + 64, 2 * t + half, p, :],
                                             R4[o:o + 64, p, t, 64 * half:64 * half + 64], start=False, stop=True,
                                             skip_group_check=True)
                last.then_inc(ph.sem("o"), 1)
            for p in range(HC):
                pe.wait_ge(ph.sem("o_sum"), p + 1)
                pe.matmul(m.banks[p][:], m.centre[:], K[:, p, :], start=True, stop=True).then_inc(ph.sem("centred"), 1)
            for p in range(HC):
                pe.wait_ge(ph.sem("squared"), p + 1)
                pe.matmul(m.banks[4 + p][:], m.same64[:], sq[:, p, :], start=True, stop=True).then_inc(ph.sem("sums"), 1)
            for p in range(HC):
                pe.matmul(m.banks[p][:], g2s[:, p * P:(p + 1) * P], x.x[:, 1, 1:], start=True, stop=True).then_inc(ph.sem("gate"), 1)

        @block.vector
        def _(dve):
            v = Chain(dve, ph.sem("dve"))
            dve.memset(st[:, 0], 0.0).then_inc(ph.sem("state"), 1)
            tri = m.tri3
            for p in range(HC):
                for q in range(2):
                    for t in range(NT):
                        u = NT * q + t
                        dve.wait_ge(ph.sem("products"), 2 * NT * p + u + 1)
                        if p and u == 0:
                            dve.wait_ge(ph.sem("tmv"), p)
                            dve.wait_ge(ph.sem("part0"), (levels - 1) * p)
                            dve.wait_ge(ph.sem("part1"), (levels - 1) * p)
                        e0, e1 = m.banks[2 * (u % 2)], m.banks[2 * (u % 2) + 1]
                        for out, src, mask in ((lt[:, q, t, :], e0[:, 0:P], tri[:, 0, :]),
                                               (rb[:, p, q, t, :], e0[:, P:2 * P], tri[:, 1, :]),
                                               (lo[:, q, t, :], e0[:, 2 * P:3 * P], tri[:, 2, :]),
                                               (mk[:, q, t, :, :].rearrange("p a b -> p (a b)"), e1[:, 0:2 * P],
                                                tri[:, 0:2, :].rearrange("p a b -> p (a b)"))):
                            dve.tensor_tensor(out, src, mask, ALU.mult).then_inc(ph.sem("products_taken"), 1)
                dve.wait_ge(ph.sem("products_taken"), 4 * (2 * NT * (p + 1)))
                first_inverse(dve, v, 1)
                for n in range(1, levels):
                    for q in range(2):
                        dve.wait_ge(ph.sem(f"lt{q}"), p * (levels - 1) + n)
                        dve.tensor_tensor(xp[:, q], bank4(4 + q), ident4, ALU.add).then_inc(ph.sem(f"xp{q}"), 1)
            for c in range(NCH):
                b, t = 64 * (c % 2), c // 2
                dve.wait_ge(ph.sem("u"), c + 1)
                for q in range(2):
                    uq = uw4[b:b + 64, :, t, 64 * q:64 * q + 64]
                    dve.tensor_tensor(uq, uq, m.banks[q][b:b + 64, 0:HC * 64].rearrange("p (a n) -> p a n", n=64),
                                      ALU.add).then_inc(ph.sem("u_done"), 1)
                dve.wait_ge(ph.sem("s"), c + 1)
                s_in = m.banks[2 + c % 2][:, 0:HC * 64].rearrange("p (a n) -> p a n", n=64)
                dve.tensor_tensor(st[:, c + 1], s_in, st[:, c], ALU.add).then_inc(ph.sem("state"), 1)
                dve.wait_ge(ph.sem("state"), 2 * c + 2)
                dve.tensor_tensor(st[:, c + 1], st[:, c + 1], x.dc[:, :, c:c + 1].broadcast_to([P, HC, 64]),
                                  ALU.mult).then_inc(ph.sem("state"), 1)
            for p in range(HC):
                dve.wait_ge(ph.sem("o"), p + 1)
                dve.tensor_tensor(K[:, p, :], K[:, p, :], m.banks[4 + p][:], ALU.add).then_inc(ph.sem("o_sum"), 1)
            for p in range(HC):
                dve.wait_ge(ph.sem("sums"), p + 1)
                dve.tensor_scalar(sq[:, p, :], m.banks[4 + p][:], 1.0 / 64, GN_EPS, ALU.mult, ALU.add).then_inc(ph.sem("mean"), 1)
            dve.wait_ge(ph.sem("centred_out"), HC)
            steps = [lambda p: dve.tensor_tensor(oc[:, p, :], oc[:, p, :], sq[:, p, :], ALU.mult),
                     lambda p: dve.tensor_scalar(oc[:, p, :], oc[:, p, :], m.params[:, COLUMN["rw_ln_w"] + p:COLUMN["rw_ln_w"] + p + 1],
                                                 m.params[:, COLUMN["rw_ln_b"] + p:COLUMN["rw_ln_b"] + p + 1], ALU.mult, ALU.add),
                     lambda p: dve.tensor_tensor(oc[:, p, :], oc[:, p, :], x.bonus[:, p, 1:], ALU.add),
                     lambda p: dve.tensor_tensor(m.mixT[:, HC + p, :], oc[:, p, :], m.banks[p][:], ALU.mult)]
            at = {}
            for k in range(HC + len(steps) - 1):
                for s in reversed(range(len(steps))):
                    p = k - s
                    if 0 <= p < HC:
                        if s == 0:
                            dve.wait_ge(ph.sem("inverse_root"), p + 1)
                        else:
                            v.wait(at[p])
                        if s == 3:
                            dve.wait_ge(ph.sem("gate"), p + 1)
                        at[p] = v.mark(steps[s](p))
            v.wait()

        @block.scalar
        def _(act):
            i = 0
            for p in range(HC):
                for dst in (brow, krow, vrow):
                    act.wait_ge(ph.sem("turned"), i + 1)
                    act.activation(dst[:, p], bank4(i % 6), ACT.Copy).then_inc(ph.sem("rows"), 1)
                    i += 1
            act.wait_ge(ph.sem("rows"), 3 * HC)
            for p in range(HC):
                act.wait_ge(ph.sem("arow"), p + 1)
                act.activation(arow[:], bank4(6), ACT.Copy).then_inc(ph.sem("arow_taken"), 1)
                k = p * (2 * (levels - 1) - 1)
                for n in range(1, levels):
                    for q in range(2):
                        kk = k + 2 * (n - 1)
                        if n < levels - 1:
                            act.wait_ge(ph.sem(f"merged{q}"), kk + 1)
                            act.activation(tt[:, q, 0], bank4(2 * q), ACT.Copy).then_inc(ph.sem(f"inverse{q}"), 1)
                            kk += 1
                        act.wait_ge(ph.sem(f"merged{q}"), kk + 1)
                        act.activation(tt[:, q, 1], bank4(2 * q + 1), ACT.Copy).then_inc(ph.sem(f"inverse{q}"), 1)
                act.wait_ge(ph.sem("mv"), p + 1)
                act.activation(w1[:], m.banks[6][:].rearrange("p (q t n) -> p q t n", q=2, n=64), ACT.Copy).then_inc(ph.sem("post"), 1)
                act.wait_ge(ph.sem("ta"), p + 1)
                act.activation(A4[:, p], bank4(4), ACT.Copy).then_inc(ph.sem("post"), 1)
                act.wait_ge(ph.sem("rkv"), p + 1)
                act.activation(K[:, p, :], m.banks[5][:], ACT.Copy).then_inc(ph.sem("post"), 1)
                act.wait_ge(ph.sem("tmv"), p + 1)
                act.activation(uw[:, p, :].rearrange("p (t q n) -> p q t n", q=2, n=64),
                               m.banks[7][:].rearrange("p (q t n) -> p q t n", q=2, n=64), ACT.Copy).then_inc(ph.sem("post"), 1)
            for p in range(HC):
                act.wait_ge(ph.sem("centred"), p + 1)
                act.activation(oc[:, p, :], m.banks[p][:], ACT.Copy).then_inc(ph.sem("centred_out"), 1)
                act.activation(sq[:, p, :], m.banks[p][:], ACT.Square).then_inc(ph.sem("squared"), 1)
            inverse_root_act(act, ph, sq, HC)

        @block.gpsimd
        def _(pool):
            g = Chain(pool, ph.sem("pool"))
            for p in range(HC):
                pool.wait_ge(ph.sem("products_taken"), 4 * (2 * NT * p + NT))
                if p:
                    pool.wait_ge(ph.sem("tmv"), p)
                first_inverse(pool, g, 0)
                for n in range(1, levels):
                    for q in range(2):
                        if n == 1:
                            pool.wait_ge(ph.sem("products_taken"), 4 * (2 * NT * p + NT * (q + 1)))
                            pool.wait_ge(ph.sem(f"first{q}"), 2 * p + 2)
                        if n > 1:
                            pool.wait_ge(ph.sem(f"lt{q}"), p * (levels - 1) + n - 1)
                        pool.tensor_tensor(lo[:, q], lt[:, q], mask4(m.masks[:, n, :]), ALU.mult).then_inc(ph.sem(f"part{q}"), 1)
    ph.close()
class Moe:

    def __init__(self, m, experts, per_group, halves, slots, block):
        self.E, self.per_group, self.halves, self.cap, self.block = experts, per_group, halves, slots, block
        self.groups = experts // per_group
        self.EB = 4 // halves
        self.bodies = experts // self.EB
        self.EC = self.EB // 2
        self.width = self.EC * slots
        parts = m.open(f"moe{block}", {
            "x_hi": (NT, D), "x_lo": (NT, D),
            "y_hi": (2, D), "y_lo": (2, D),
            "G": (NT, 2, P),
            "ST": (2, S),
            "ident_r": (P,)})
        self.x_hi, self.x_lo, self.y_hi, self.y_lo, self.G, self.ST, self.ident = (
            parts[n] for n in ("x_hi", "x_lo", "y_hi", "y_lo", "G", "ST", "ident_r"))
        at = 0
        self.h, at = m.view(at, NT, D)
        self.q, at = m.view(at, NT, experts)
        self.cw, at = m.view(at, NT, experts)
        self.L, _ = m.view(at, NT, 36)
        s = at + NT * 36
        self.wr, s = m.view(s, DC, 36)
        self.bias, s = m.view(s, 36)
        self.tmp = [None] * 6
        for i in range(6):
            self.tmp[i], s = m.view(s, NT, experts)
        self.t4 = [None] * 8
        for i in range(8):
            self.t4[i], s = m.view(s, NT, 4)
        self.one = [None] * 8
        for i in range(8):
            self.one[i], s = m.view(s, NT)
        self.cwx, at = m.view(at, NT, 4)
        self.ws, at = m.view(at, 2)
        self.ring23, end = m.view(m.arena_size - 2 * RING, 2, RING)
        assert max(at, s) <= m.arena_size - 2 * RING
        self.xe = m.mixT[:, 0:4, :].rearrange("p a s -> p (a s)").rearrange("p (c j n) -> p c j n", c=2, n=P)
        self.hid = m.mixT[:, 4:6, :].rearrange("p a s -> p (a s)").rearrange("p (s f n) -> p s f n", s=4, n=P)
        self.sig = m.mixT[:, 6, :].rearrange("p (b f n) -> p b f n", b=2, n=P)
        self.m = m

    def slot(self, s):
        r = self.m.ring01[:, s, :] if s < 2 else self.ring23[:, s - 2, :]
        half = DC * 256
        return (r[:, 0:half].rearrange("p (c n) -> p c n", n=256), r[:, half:2 * half].rearrange("p (c n) -> p c n", n=256),
                r[:, 2 * half:].rearrange("p (c n) -> p c n", n=D))

    def load(self, sp, io, s, body, sem):
        gate, up, down = self.slot(s)
        wg, wu, wd = (io[n][0] for n in self.weights)
        if self.halves == 1:
            e, f0 = body * 4 + s, 0
        else:
            e, f0 = body * 2 + s // 2, 256 * (s % 2)
        if isinstance(e, int):
            wg, wu, wd = wg[e], wu[e], wd[e]
        else:
            wg, wu, wd = (w[bass.ds(e, 1)].rearrange("e a b -> (e a) b") for w in (wg, wu, wd))
        sp.dma_start(gate, wg[:, f0:f0 + 256].rearrange("(c p) n -> p c n", p=P)).then_inc(sem, 16)
        sp.dma_start(up, wu[:, f0:f0 + 256].rearrange("(c p) n -> p c n", p=P)).then_inc(sem, 16)
        sp.dma_start(down, wd[f0:f0 + 256, :].rearrange("(c p) n -> p c n", p=P)).then_inc(sem, 16)


def load_w_out(sp, m, w_out, sem):
    for n in range(2):
        v = item_view(m, n, HW)
        src = w_out[0][:, n * HW:(n + 1) * HW].rearrange("(c p) n -> p c n", p=P)
        for a, b in ((0, 4), (4, 8)):
            sp.dma_start(v[:, a:b, :], src[:, a:b, :]).then_inc(sem, 16)


def phase_out(nc, m, io, z, name, residual, w_out_sem, gain, router, ring_sems):
    ph = Phase(nc, name)
    wg, bg, we, be = (io[n] for n in router)
    E, G = z.E, z.groups
    L = z.L[:, :, 0:G + E]
    gl, el = L[:, :, 0:G], L[:, :, G:]
    t = z.tmp
    one = z.one
    down = lambda a, n: a.unsqueeze(2).broadcast_to([P, NT, n])
    ramp = lambda n: m.experts[:, 0:n].unsqueeze(1).broadcast_to([P, NT, n])
    rows = residual.rearrange("b (t p) d -> p (b t) d", p=P) if len(residual.shape) == 3 else residual
    with nc.Block() as block:
        @block.sync
        def _(sp):
            sp.dma_start(z.h[:], rows).then_inc(ph.sem("residual"), 16)
            sp.dma_start(z.wr[:, :, 0:G], wg[0].rearrange("(c p) n -> p c n", p=P)).then_inc(ph.sem("router"), 16)
            sp.dma_start(z.wr[:, :, G:G + E], we[0].rearrange("(c p) n -> p c n", p=P)).then_inc(ph.sem("router"), 16)
            sp.dma_start(z.bias[:, 0:G], bg.partition_broadcast(P) if len(bg.shape) == 1 else bg[0:1, :].broadcast_to([P, G])).then_inc(ph.sem("router"), 16)
            sp.dma_start(z.bias[:, G:G + E], be[0:1, :].broadcast_to([P, E])).then_inc(ph.sem("router"), 16)
            for s in (2, 3):
                z.load(sp, io, s, 0, ring_sems[s])
            sp.wait_ge(ph.sem("projected"), 2 * NT)
            for s in (0, 1):
                z.load(sp, io, s, 0, ring_sems[s])

        @block.tensor
        def _(pe):
            def project(i):
                for n in range(2):
                    k = 2 * i + n
                    if k >= 4:
                        pe.wait_ge(ph.sem("taken"), k - 3)
                    w = item_view(m, n, HW)
                    for c in range(DC):
                        last = pe.matmul(m.banks[k % 4][:], m.mixT[:, c, i * P:(i + 1) * P], w[:, c, :],
                                         start=(c == 0), stop=(c == DC - 1))
                    last.then_inc(ph.sem("projected"), 1)

            def turn(t_):
                pe.wait_ge(ph.sem("split"), t_ + 1)
                for half in range(2):
                    if t_ >= 2:
                        pe.wait_ge(ph.sem("normed"), 2 * (t_ - 2) + half + 1)
                    for j in range(4):
                        c = 4 * half + j
                        for part in (z.x_hi, z.x_lo):
                            last = pe.matmul(m.banks[4 + (2 * t_ + half) % 4][:, j * P:(j + 1) * P],
                                             part[:, t_, c * P:(c + 1) * P], z.ident[:],
                                             start=(part is z.x_hi), stop=(part is z.x_lo))
                    last.then_inc(ph.sem("turned"), 1)

            pe.wait_ge(w_out_sem, 64)
            project(0)
            pe.wait_ge(ph.sem("ident"), 1)
            for i in range(1, NT):
                project(i)
                turn(i - 1)
            turn(NT - 1)
            pe.wait_ge(ph.sem("normed"), NORMED)
            pe.wait_ge(ph.sem("router"), 64)
            for i in range(NT):
                for c in range(DC):
                    last = pe.matmul(m.banks[i][:, 0:G + E], m.mixT[:, c, i * P:(i + 1) * P], z.wr[:, c, 0:G + E],
                                     start=(c == 0), stop=(c == DC - 1))
            last.then_inc(ph.sem("logits"), 1)
            pe.wait_ge(ph.sem("chosen"), 1)
            for i in range(NT):
                for j in range(i + 1):
                    pe.matmul(m.banks[4][:, i * E:(i + 1) * E], (m.after if j == i else m.ones)[:], t[2][:, j, :],
                              start=(j == 0), stop=(j == i))
            for j in range(NT):
                last = pe.matmul(m.banks[5][:, 0:E], m.ones[:], t[2][:, j, :], start=(j == 0), stop=(j == NT - 1))
            last.then_inc(ph.sem("counted"), 1)

        @block.scalar
        def _(act):
            for i in range(NT):
                act.wait_ge(ph.sem("taken"), 2 * (i + 1))
                act.activation(z.x_lo[:, i, :], z.h[:, i, :], ACT.Square, accum_out=m.small[:, i:i + 1]).then_inc(ph.sem("squares"), 1)
                act.wait_ge(ph.sem("mean"), i + 1)
                act.activation(m.small[:, 8 + i:9 + i], m.small[:, 4 + i:5 + i], ACT.Sqrt).then_inc(ph.sem("deviation"), 1)
                act.wait_ge(ph.sem("inverse_rms"), i + 1)
                act.activation(z.x_hi[:, i, :], z.h[:, i, :], ACT.Copy, scale=m.small[:, 12 + i:13 + i]).then_inc(ph.sem("high"), 1)
            act.wait_ge(ph.sem("group_less"), 1)
            act.activation(z.t4[0][:, :, 0:G], z.t4[0][:, :, 0:G], ACT.Exp).then_inc(ph.sem("group_exp"), 1)
            act.wait_ge(ph.sem("second_less"), 1)
            act.activation(one[4], one[4], ACT.Exp).then_inc(ph.sem("second_exp"), 1)

        @block.vector
        def _(dve):
            v = Chain(dve, ph.sem("dve"))
            dve.wait_ge(ph.sem("residual"), 16)
            dve.tensor_copy(z.ident[:], m.ident[:]).then_inc(ph.sem("ident"), 1)

            def norm(i):
                for n in range(2):
                    k = 2 * i + n
                    dve.wait_ge(ph.sem("projected"), k + 1)
                    h = z.h[:, i, n * HW:(n + 1) * HW]
                    dve.tensor_tensor(h, h, m.banks[k % 4][:], ALU.add).then_inc(ph.sem("taken"), 1)
                dve.wait_ge(ph.sem("squares"), i + 1)
                dve.tensor_scalar(m.small[:, 4 + i:5 + i], m.small[:, i:i + 1], 1.0 / D, EPS, ALU.mult, ALU.add).then_inc(ph.sem("mean"), 1)
                dve.wait_ge(ph.sem("deviation"), i + 1)
                dve.reciprocal(m.small[:, 12 + i:13 + i], m.small[:, 8 + i:9 + i]).then_inc(ph.sem("inverse_rms"), 1)
                dve.wait_ge(ph.sem("inverse_rms"), i + 1)
                dve.wait_ge(ph.sem("high"), i + 1)
                dve.scalar_tensor_tensor(z.x_lo[:, i, :], z.h[:, i, :], m.small[:, 12 + i:13 + i],
                                         z.x_hi[:, i, :].bitcast(F32), ALU.mult, ALU.subtract).then_inc(ph.sem("split"), 1)

            def scale(t_):
                for half in range(2):
                    dve.wait_ge(ph.sem("turned"), 2 * t_ + half + 1)
                    c = COLUMN[gain] + 4 * half
                    dve.tensor_tensor(m.mixT[:, 4 * half:4 * half + 4, t_ * P:(t_ + 1) * P],
                                      m.banks[4 + (2 * t_ + half) % 4][:].rearrange("p (a b) -> p a b", b=P),
                                      m.params[:, c:c + 4].unsqueeze(2).broadcast_to([P, 4, P]),
                                      ALU.mult).then_inc(ph.sem("normed"), 1)

            norm(0)
            for i in range(1, NT):
                norm(i)
                scale(i - 1)
            scale(NT - 1)
            dve.wait_ge(ph.sem("logits"), 1)
            for i in range(NT):
                v.mark(dve.tensor_tensor(L[:, i, :], m.banks[i][:, 0:G + E], z.bias[:, 0:G + E], ALU.add))
            v.wait()

            def first_of(values, top, n, out, scratch):
                v.link(dve.tensor_reduce(top, values, AX_X, ALU.max))
                v.mark(dve.tensor_tensor(out, values, down(top, n), ALU.is_equal))
                v.link(dve.tensor_scalar(scratch, ramp(n), -1.0, float(n), ALU.mult, ALU.add))
                v.link(dve.tensor_tensor(out, out, scratch, ALU.mult))
                v.link(dve.tensor_reduce(one[7], out, AX_X, ALU.max))
                v.link(dve.tensor_tensor(out, scratch, down(one[7], n), ALU.is_equal))

            group, g_less, g_scratch = z.t4[1][:, :, 0:G], z.t4[0][:, :, 0:G], z.t4[2][:, :, 0:G]
            first_of(gl, one[0], G, group, g_scratch)
            dve.tensor_tensor(g_less, gl, down(one[0], G), ALU.subtract).then_inc(ph.sem("group_less"), 1)
            v.link(dve.tensor_scalar(group, group, 1e30, -1e30, ALU.mult, ALU.add))
            v.link(dve.tensor_tensor(t[3].rearrange("p t (g e) -> p t g e", g=G), el.rearrange("p t (g e) -> p t g e", g=G),
                                     group.unsqueeze(3).broadcast_to([P, NT, G, z.per_group]), ALU.add))
            first_of(t[3], one[1], E, t[0], t[5])
            v.link(dve.scalar_tensor_tensor(t[3], t[0], -2e30, t[3], ALU.mult, ALU.add))
            first_of(t[3], one[2], E, t[1], t[5])
            dve.tensor_tensor(t[2], t[0], t[1], ALU.add).then_inc(ph.sem("chosen"), 1)
            dve.tensor_tensor(one[4], one[2], one[1], ALU.subtract).then_inc(ph.sem("second_less"), 1)
            dve.wait_ge(ph.sem("group_exp"), 1)
            v.link(dve.tensor_reduce(one[3], g_less, AX_X, ALU.add))
            dve.wait_ge(ph.sem("second_exp"), 1)
            v.link(dve.tensor_scalar(one[5], one[4], 1.0, None, ALU.add))
            v.link(dve.tensor_tensor(one[5], one[5], one[3], ALU.mult))
            v.link(dve.reciprocal(one[5], one[5]))
            v.link(dve.tensor_tensor(one[6], one[5], one[4], ALU.mult))
            v.mark(dve.tensor_tensor(t[0], t[0], down(one[5], E), ALU.mult))
            v.link(dve.tensor_tensor(t[1], t[1], down(one[6], E), ALU.mult))
            v.link(dve.tensor_tensor(z.cw, t[0], t[1], ALU.add))
            dve.wait_ge(ph.sem("counted"), 1)
            v.link(dve.tensor_scalar(t[3], m.banks[4][:, 0:NT * E].rearrange("p (t e) -> p t e", e=E), 1.0, None, ALU.add))
            v.link(dve.tensor_tensor(t[3], t[3], t[2], ALU.mult))
            v.link(dve.tensor_scalar(z.q, t[3], -1.0, None, ALU.add))
            rounds = -(-S // z.cap)
            v.link(dve.tensor_reduce(one[0][:, 0:1], m.banks[5][:, 0:E], AX_X, ALU.max))
            v.link(dve.tensor_scalar(t[4][:, 0, 0:rounds], m.experts[:, 0:rounds], float(z.cap), one[0][:, 0:1], ALU.mult, ALU.is_lt))
            v.link(dve.tensor_reduce(one[1][:, 0:1], t[4][:, 0, 0:rounds], AX_X, ALU.add))
            v.link(dve.tensor_copy(m.rounds[:], one[1][:, 0:1]))
    ph.close()


def phase_moe(nc, m, io, z, name, gain, ring_sems):
    ph = Phase(nc, name)
    most = -(-S // z.cap)
    W, cap, NB = z.width, z.cap, z.bodies
    gath, hb, yb, turns = m.banks[0:2], m.banks[2:4], m.banks[4:6], m.banks[6:8]
    own = lambda i: slice(64 * (i % 2), 64 * (i % 2) + cap) if z.halves == 1 else slice(0, cap)

    def loop(engine, prologue, body, after_round=None):
        n = engine.value_load(m.rounds[0:1, 0:1], min_val=1, max_val=most)
        with engine.Fori(0, n) as r:
            prologue(r * NB, 0)
            with engine.Fori(0, NB - 1) as i:
                body(r * NB + i, (i + 1) * z.EB)
            body(r * NB + (NB - 1), None)
            if after_round:
                after_round(r)

    with nc.Block() as block:
        @block.sync
        def _(sp):
            def fill(g, i):
                for s in range(4):
                    sp.wait_ge(ph.sem("down"), g * 4 + (s - 3))
                    z.load(sp, io, s, i, ring_sems[s])

            n = sp.value_load(m.rounds[0:1, 0:1], min_val=1, max_val=most)
            with sp.Fori(1, NB) as i:
                fill(i, i)
            with sp.If(n > 1):
                with sp.Fori(1, n) as r:
                    with sp.Fori(0, NB) as i:
                        fill(r * NB + i, i)
            with sp.Else():
                sp.nop()

        @block.tensor
        def _(pe):
            def gather(g, half, scattered):
                if half == 0:
                    pe.wait_ge(ph.sem("onehot"), g * 2 + 2)
                    pe.wait_ge(ph.sem("summed"), scattered)
                for a in range(2):
                    if half == 1:
                        pe.wait_ge(ph.sem("gathered_taken"), g * 4 + a + 1)
                    for b in range(2):
                        j = 4 * half + 2 * a + b
                        for t in range(NT):
                            for part in (z.x_hi, z.x_lo):
                                last = pe.matmul(gath[a][:, b * 2 * W:(b + 1) * 2 * W], part[:, t, j * P:(j + 1) * P],
                                                 z.G[:, t, :, 0:W], start=(t == 0 and part is z.x_hi),
                                                 stop=(t == NT - 1 and part is z.x_lo))
                    last.then_inc(ph.sem("gathered"), 1)

            def weigh(g):
                pe.wait_ge(ph.sem("y_taken"), g * 8 + 1)
                for c in range(2):
                    for k in range(z.EC):
                        e = c * z.EC + k
                        for t in range(NT):
                            last = pe.matmul(yb[0][k * cap:(k + 1) * cap, c:c + 1],
                                             z.G[:, t, c, k * cap:(k + 1) * cap].bitcast(F32),
                                             z.cwx[:, t, e:e + 1], start=(t == 0), stop=(t == NT - 1))
                last.then_inc(ph.sem("weighed"), 1)

            def turn(g):
                pe.wait_ge(ph.sem("onehot"), g * 2 + 2)
                pe.wait_ge(ph.sem("turned_taken"), g * 2 + 1)
                for c in range(2):
                    for t in range(NT):
                        last = pe.matmul(turns[c][0:W, t * P:(t + 1) * P], z.G[:, t, c, 0:W], z.ident[:], start=True, stop=True)
                    last.then_inc(ph.sem("turned"), 1)

            def gate_up(g, s):
                c = s // 2
                gate, up, _ = z.slot(s)
                pe.wait_ge(ring_sems[s], (g + 1) * 48)
                pe.wait_ge(ph.sem("gathered_taken"), g * 4 + 4)
                pe.wait_ge(ph.sem("hidden_done"), g * 4 + max(s, 1))
                for k, w in enumerate((gate, up)):
                    for f in range(2):
                        for j in range(DC):
                            last = pe.matmul(hb[s % 2][:, k * 256 + f * P:k * 256 + f * P + W], w[:, j, f * P:(f + 1) * P],
                                             z.xe[:, c, j, 0:W], start=(j == 0), stop=(j == DC - 1))
                last.then_inc(ph.sem("hidden"), 1)

            def down(g, s):
                c = s // 2
                _, _, wd = z.slot(s)
                pe.wait_ge(ph.sem("hidden_done"), g * 4 + s + 2)
                if s == 0:
                    pe.wait_ge(ph.sem("weights_taken"), g + 1)
                if s == 2:
                    pe.wait_ge(ph.sem("y_taken"), g * 8 + 4 + 1)
                for n in range(2):
                    for f in range(2):
                        first = f == 0 and (z.halves == 1 or s % 2 == 0)
                        final = f == 1 and (z.halves == 1 or s % 2 == 1)
                        last = pe.matmul(yb[n][own(s), :], z.hid[:, s, f, 0:cap], wd[:, f, n * 512:(n + 1) * 512],
                                         start=first, stop=final)
                    if n == 0 and s % 2 == 1:
                        last.then_inc(ph.sem("half_down"), 1)
                last.then_inc(ph.sem("down"), 1)

            def scatter(g):
                pe.wait_ge(ph.sem("turned_taken"), g * 2 + 2 + 1)

                def rows(k, c):
                    t, n = k // 2, k % 2
                    for part in (z.y_hi, z.y_lo):
                        last = pe.matmul(gath[n][:], z.ST[0:W, c, t * P:(t + 1) * P], part[0:W, c, n * 512:(n + 1) * 512],
                                         start=(c == 0 and part is z.y_hi), stop=(c == 1 and part is z.y_lo))
                    return last

                rows(0, 0)
                rows(1, 0)
                for k in range(2):
                    pe.wait_ge(ph.sem("y_taken"), g * 8 + 6 + 2 * k + 1)
                    rows(k, 1).then_inc(ph.sem("scattered"), 1)
                for k in range(2, 8):
                    pe.wait_ge(ph.sem("summed"), g * 8 + k)
                    rows(k, 0)
                    rows(k, 1).then_inc(ph.sem("scattered"), 1)

            def prologue(g, e0):
                gather(g, 0, g * 8 + 1)
                gather(g, 1, None)
                turn(g)
                pe.wait_ge(ph.sem("cwx"), g + 1)
                weigh(g)

            def body(g, ahead):
                gate_up(g, 0)
                gate_up(g, 1)
                down(g, 0)
                gate_up(g, 2)
                down(g, 1)
                gate_up(g, 3)
                if ahead is not None:
                    gather(g + 1, 0, g * 8 + 1)
                down(g, 2)
                if ahead is not None:
                    gather(g + 1, 1, None)
                down(g, 3)
                if ahead is not None:
                    turn(g + 1)
                pe.wait_ge(ph.sem("gathered_taken"), g * 4 + (4 if ahead is None else 8))
                scatter(g)
                if ahead is not None:
                    pe.wait_ge(ph.sem("cwx"), g + 2)
                    weigh(g + 1)

            for name in ("weighed", "scattered"):
                pe.sem_inc(ph.sem(name), 1)
            loop(pe, prologue, body)

        @block.vector
        def _(dve):
            v = ph.sem("dve")

            def onehot(g, e0):
                dve.wait_ge(ph.sem("weighed"), g + 1)
                dve.tensor_copy(z.cwx[:, :, 0:z.EB], z.cw[:, :, bass.ds(e0, z.EB)]).then_inc(ph.sem("cwx"), 1)
                for c in range(2):
                    qe = z.q[:, :, bass.ds(e0 + c * z.EC, z.EC)]
                    if z.EC == 2:
                        dve.tensor_tensor(z.G[:, :, c, :].rearrange("p t (e n) -> p t e n", n=cap),
                                          m.slots[:, 0, :].rearrange("p (e n) -> p e n", n=cap).unsqueeze(1).broadcast_to([P, NT, 2, cap]),
                                          qe.unsqueeze(3).broadcast_to([P, NT, 2, cap]), ALU.is_equal).then_inc(ph.sem("onehot"), 1)
                    else:
                        dve.tensor_tensor(z.G[:, :, c, 0:cap], m.slots[:, 1:2, 0:cap].broadcast_to([P, NT, cap]),
                                          qe.broadcast_to([P, NT, cap]), ALU.is_equal).then_inc(ph.sem("onehot"), 1)

            def gathered(g, half):
                for a in range(2):
                    dve.wait_ge(ph.sem("gathered"), g * 4 + 2 * half + a + 1)
                    j = 4 * half + 2 * a
                    dve.tensor_tensor(z.xe[:, :, j:j + 2, 0:W].rearrange("p c j n -> p j c n"),
                                      gath[a][:, 0:4 * W].rearrange("p (j c n) -> p j c n", j=2, n=W),
                                      m.params[:, gain + j:gain + j + 2].unsqueeze(2).unsqueeze(3).broadcast_to([P, 2, 2, W]),
                                      ALU.mult).then_inc(ph.sem("gathered_taken"), 1)

            def hidden(g, s):
                b = hb[s % 2][:].rearrange("p (k f n) -> p k f n", k=2, n=P)
                h = z.hid[:, s, :, 0:cap]
                dve.wait_ge(ph.sem("sigmoid"), g * 4 + s + 1)
                dve.tensor_tensor(h, b[:, 0, :, own(s)], z.sig[:, s % 2, :, 0:cap], ALU.mult).then_inc(v, 1)
                dve.wait_ge(v, g * 4 + s + 1)
                dve.tensor_tensor(h, h, b[:, 1, :, own(s)], ALU.mult).then_inc(ph.sem("hidden_done"), 1)

            def rows_low(g, c):
                for n in range(2):
                    dve.wait_ge(ph.sem("y_taken"), g * 8 + 4 * c + 2 * n + 1 + 1)
                    dve.scalar_tensor_tensor(z.y_lo[0:W, c, n * 512:(n + 1) * 512], yb[n][0:W, :], z.ws[0:W, c:c + 1],
                                             z.y_hi[0:W, c, n * 512:(n + 1) * 512].bitcast(F32), ALU.mult,
                                             ALU.subtract).then_inc(ph.sem("y_taken"), 1)

            def prologue(g, e0):
                onehot(g, e0)
                gathered(g, 0)
                gathered(g, 1)

            def body(g, ahead):
                if ahead is not None:
                    onehot(g + 1, ahead)
                hidden(g, 0)
                hidden(g, 1)
                hidden(g, 2)
                rows_low(g, 0)
                hidden(g, 3)
                if ahead is not None:
                    gathered(g + 1, 0)
                    gathered(g + 1, 1)
                rows_low(g, 1)
                for k in range(8):
                    t, n = k // 2, k % 2
                    dve.wait_ge(ph.sem("scattered"), g * 8 + k + 2)
                    hh = z.h[:, t, n * 512:(n + 1) * 512]
                    dve.tensor_tensor(hh, hh, gath[n][:], ALU.add).then_inc(ph.sem("summed"), 1)

            def next_round(r):
                dve.tensor_scalar(z.q, z.q, -float(cap), None, ALU.add).then_inc(ph.sem("round"), 1)
                dve.wait_ge(ph.sem("round"), r + 1)

            for name in ("hidden_done", "summed"):
                dve.sem_inc(ph.sem(name), 1)
            loop(dve, prologue, body, next_round)

        @block.scalar
        def _(act):
            def turned(g):
                act.wait_ge(ph.sem("scattered"), g * 8 + 1)
                for c in range(2):
                    act.wait_ge(ph.sem("turned"), g * 2 + c + 1)
                    act.activation(z.ST[0:W, c, :], turns[c][0:W, :], ACT.Copy).then_inc(ph.sem("turned_taken"), 1)
                act.wait_ge(ph.sem("weighed"), g + 1 + 1)
                act.activation(z.ws[0:W, :], yb[0][0:W, 0:2], ACT.Copy).then_inc(ph.sem("weights_taken"), 1)

            def sigmoid(g, s):
                act.wait_ge(ph.sem("hidden"), g * 4 + s + 1)
                act.wait_ge(ph.sem("hidden_done"), g * 4 + max(s, 1))
                b = hb[s % 2][:].rearrange("p (k f n) -> p k f n", k=2, n=P)
                act.activation(z.sig[:, s % 2, :, 0:cap], b[:, 0, :, own(s)], ACT.Sigmoid).then_inc(ph.sem("sigmoid"), 1)

            def rows_high(g, c):
                act.wait_ge(ph.sem("weights_taken"), g + 1)
                for n in range(2):
                    if n == 0:
                        act.wait_ge(ph.sem("half_down"), g * 2 + c + 1)
                    else:
                        act.wait_ge(ph.sem("down"), g * 4 + 2 * c + 2)
                    act.wait_ge(ph.sem("y_taken"), g * 8 + 4 * c + 2 * n + 1)
                    act.activation(z.y_hi[0:W, c, n * 512:(n + 1) * 512], yb[n][0:W, :], ACT.Copy,
                                   scale=z.ws[0:W, c:c + 1]).then_inc(ph.sem("y_taken"), 1)

            def body(g, ahead):
                sigmoid(g, 0)
                sigmoid(g, 1)
                sigmoid(g, 2)
                rows_high(g, 0)
                sigmoid(g, 3)
                rows_high(g, 1)
                if ahead is not None:
                    turned(g + 1)

            for name in ("turned_taken", "y_taken"):
                act.sem_inc(ph.sem(name), 1)
            loop(act, lambda g, e0: turned(g), body)
    ph.close()


def phase_final(nc, m, z, name, gain_src, dst):
    out_view = m.rows
    ph = Phase(nc, name)
    gain = m.ring01[:, 0, 0:D]
    rows = dst.rearrange("b (t p) d -> p (b t) d", p=P) if len(dst.shape) == 3 else dst
    with nc.Block() as block:
        @block.sync
        def _(sp):
            sp.dma_start(gain, gain_src.rearrange("(a d) -> a d", a=1).broadcast_to([P, D])).then_inc(ph.sem("gain"), 16)
            for t in range(NT):
                sp.wait_ge(ph.sem("done"), t + 1)
                sp.dma_start(rows[:, t, :], out_view[:, t, :]).then_inc(ph.sem("stored"), 16)
            sp.wait_ge(ph.sem("stored"), 16 * NT)

        @block.scalar
        def _(act):
            norm_act(act, ph, m, z.h, z.x_lo, lambda e, t: None)

        @block.vector
        def _(dve):
            v = Chain(dve, ph.sem("dve"))
            for t in range(NT):
                inverse_rms_dve(dve, ph, m, t, v)
                dve.wait_ge(ph.sem("gain"), 16)
                dve.scalar_tensor_tensor(out_view[:, t, :], z.h[:, t, :], m.small[:, 12 + t:13 + t], gain, ALU.mult,
                                         ALU.mult).then_inc(ph.sem("done"), 1)
    ph.close()
HG = 4
FH = 8


class Mix2:

    def __init__(self, m):
        at = 0
        self.q, at = m.view(at, HG, S)
        self.k, at = m.view(at, HG, S)
        self.g, at = m.view(at, HG, S)
        self.i, at = m.view(at, NT, HW)
        self.b, at = m.view(at, HG, S)
        self.fq, at = m.view(at, HC, S)
        self.fk, at = m.view(at, HC, S)
        self.fv, at = m.view(at, NT, HW)
        self.ncum, at = m.view(at, S, partitions=8)
        self.lb, at = m.view(at, 3, HG)
        self.fbias, at = m.view(at, 1, partitions=8)
        self.free = at
        self.rows = m.rows
        self.scaled, end = m.view(at, NT, D)
        self.f8, _ = m.view(end, 4, S, partitions=8)


def phase_project2(nc, m, io, x):
    ph = Phase(nc, "p2")
    w_in = io["w_in_2"].rearrange("l d n -> (l d) n")
    starts, sizes, widths = [HW, 0, 2 * HW, 3 * HW, 3 * HW + 768, 3 * HW + 1536], [4, 4, 4, 6, 6, 5], [HW, HW, HW, 768, 768, HW + FH]
    first = [sum(sizes[:i]) for i in range(6)]
    total = sum(sizes)
    lbc = COLUMN["hg_lb_logits_2"]

    with nc.Block() as block:
        @block.sync
        def _(sp):
            for n in range(6):
                if n >= 2:
                    sp.wait_ge(ph.sem("projected"), first[n - 1])
                v = item_view(m, n, widths[n])
                src = w_in[:, starts[n]:starts[n] + widths[n]].rearrange("(c p) n -> p c n", p=P)
                for a, b in ((0, 4), (4, 8)):
                    sp.dma_start(v[:, a:b, :], src[:, a:b, :]).then_inc(ph.sem(f"ring{n % 2}"), 16)
                if n == 0:
                    sp.dma_start(x.fbias[:], io["fox_f_bias_2"].rearrange("l h -> h l")).then_inc(ph.sem("fbias"), 16)
            sp.wait_ge(ph.sem("fbias"), 16)

        @block.tensor
        def _(pe):
            norm_turn_pe(pe, ph, m, x.scaled)
            pe.wait_ge(ph.sem("normed"), NORMED)
            for n in range(6):
                project_pe(pe, ph, m, n, widths[n], sizes[n] if n < 5 else 4, first[n], 32 * (n // 2 + 1), n in (2, 5))
            w = item_view(m, 5, widths[5])
            k = total - 1
            pe.wait_ge(ph.sem("taken"), k - 5)
            for c in range(DC):
                last = pe.matmul(m.banks[k % 6][0:FH, :], w[:, c, HW:HW + FH], m.mixT[:, c, :], start=(c == 0), stop=(c == DC - 1))
            last.then_inc(ph.sem("projected"), 1)

        @block.scalar
        def _(act):
            a = Chain(act, ph.sem("act"))
            norm_act(act, ph, m, x.rows, x.scaled, lambda e, t: None)
            act.wait_ge(ph.sem("lb_less"), 1)
            act.activation(x.lb[:, 0, :], x.lb[:, 2, :], ACT.Sigmoid).then_inc(ph.sem("lb"), 1)
            outs = [(x.k[:, c, :], ACT.Sigmoid, 1.0) for c in range(4)] + [(x.q[:, c, :], ACT.Silu, 1.0) for c in range(4)] \
                + [(x.i[:, c, :], ACT.Copy, 1.0) for c in range(4)] + [(x.g[:, c, :], ACT.Silu, 1.0) for c in range(4)] \
                + [(x.fq[:, c, :], ACT.Copy, 0.125) for c in range(4)] + [(x.fk[:, c, :], ACT.Copy, 1.0) for c in range(4)] \
                + [(x.fv[:, c, :], ACT.Copy, 1.0) for c in range(4)]

            for k in range(total):
                act.wait_ge(ph.sem("projected"), k + 1)
                bank = m.banks[k % 6]
                if k < total - 1:
                    out, func, scale = outs[k]
                    act.activation(out, bank[:], func, scale=scale).then_inc(ph.sem("taken"), 1)
                else:
                    act.activation(x.f8[:, 0], bank[0:FH, :], ACT.Identity, bias=x.fbias[:, 0:1]).then_inc(ph.sem("taken"), 1)
                if k == 8:
                    act.wait_ge(ph.sem("f"), 1)
                    act.activation(x.b[:], x.b[:], ACT.Ln).then_inc(ph.sem("logf"), 1)
            act.wait_ge(ph.sem("taken"), total)
            a.link(act.activation(x.f8[:, 1], x.f8[:, 0], ACT.Abs))
            a.link(act.activation(x.f8[:, 1], x.f8[:, 1], ACT.Exp, scale=-1.0))
            act.activation(x.f8[:, 1], x.f8[:, 1], ACT.Ln, bias=1.0).then_inc(ph.sem("f8"), 1)

        @block.vector
        def _(dve):
            v = Chain(dve, ph.sem("dve"))
            dve.tensor_tensor(x.lb[:, 2, :], m.params[:, lbc:lbc + 4], m.params[:, lbc + 4:lbc + 8], ALU.subtract).then_inc(ph.sem("lb_less"), 1)
            norm_scale_dve(dve, ph, m, x.rows, x.scaled, v)
            norm_gain_dve(dve, ph, m, COLUMN["attn_norm_2"])
            dve.wait_ge(ph.sem("lb"), 1)
            v.link(dve.tensor_scalar(x.lb[:, 1, :], x.lb[:, 0, :], -1.0, 1.0, ALU.mult, ALU.add))
            for c in range(HG):
                dve.wait_ge(ph.sem("taken"), c + 1)
                v.mark(dve.tensor_scalar(x.b[:, c, :], x.k[:, c, :], x.lb[:, 1, c:c + 1], x.lb[:, 0, c:c + 1], ALU.mult, ALU.add))
            v.wait()
            dve.tensor_scalar(x.k[:], x.b[:], -1.0, 1.0, ALU.mult, ALU.add).then_inc(ph.sem("f"), 1)
            dve.wait_ge(ph.sem("logf"), 1)
            for c in range(HG):
                v.mark(dve.tensor_tensor_scan(x.b[:, c, :], m.restart[:], x.b[:, c, :], 0.0, ALU.mult, ALU.add))
            v.mark(dve.memset(x.f8[:, 3], 1.0))
            dve.wait_ge(ph.sem("f8"), 1)
            v.link(dve.scalar_tensor_tensor(x.f8[:, 2], x.f8[:, 0], 0.0, x.f8[:, 1], ALU.min, ALU.subtract))
            v.link(dve.tensor_tensor_scan(x.f8[:, 1], x.f8[:, 3], x.f8[:, 2], 0.0, ALU.mult, ALU.add))
            v.link(dve.tensor_scalar(x.ncum[:], x.f8[:, 1], -1.0, None, ALU.mult))
    ph.close()


def phase_hgrn(nc, m, x):
    ph = Phase(nc, "hg")
    at = x.free
    e2, at = m.view(at, 2, S)
    q2, at = m.view(at, 2, S)
    k2, at = m.view(at, 2, S)
    sc, at = m.view(at, HG, NT, P)
    kd, at = m.view(at, HG, S)
    krow, at = m.view(at, NT, HG, P)
    st, at = m.view(at, NCH + 1, HG, P)
    dl, at = m.view(at, HG, NCH)
    qb = x.q
    sq = kd
    units = [(h, l) for h in range(HG) for l in range(len(LEVELS))]
    chunked = lambda ap: ap.rearrange("p h (c n) -> p h c n", n=CH)
    bank4 = lambda i: m.banks[i][:].rearrange("p (t n) -> p t n", n=P)

    with nc.Block() as block:
        @block.vector
        def _(dve):
            v = Chain(dve, ph.sem("dve"))
            v.mark(dve.memset(st[:, 0], 0.0))
            last = chunked(x.b)[:, :, :, CH - 1:CH].broadcast_to([P, HG, NCH, CH])
            dve.tensor_tensor(chunked(kd), last, chunked(x.b), ALU.subtract).then_inc(ph.sem("to_end"), 1)

            def difference(u):
                h, l = units[u]
                n = LEVELS[l]
                if u >= 2:
                    dve.wait_ge(ph.sem("queries"), u - 1)
                    dve.wait_ge(ph.sem("keys"), u - 1)
                b = x.b[:, h, :].rearrange("p (a n) -> p a n", n=2 * n)
                dve.tensor_tensor(e2[:, u % 2, :].rearrange("p (a n) -> p a n", n=2 * n), b,
                                  b[:, :, n - 1:n].broadcast_to([P, S // (2 * n), 2 * n]), ALU.subtract).then_inc(ph.sem("difference"), 1)

            def keys(u):
                h, _ = units[u]
                dve.wait_ge(ph.sem("decay"), u + 1)
                if u >= 2:
                    dve.wait_ge(ph.sem("products"), HG + u - 1)
                dve.tensor_tensor(k2[:, u % 2, :], x.k[:, h, :], e2[:, u % 2, :], ALU.mult).then_inc(ph.sem("keys"), 1)

            def select(u):
                h, l = units[u]
                dve.wait_ge(ph.sem("products"), HG + u + 1)
                mask = m.masks[:, l:l + 1, :].bitcast(I32).broadcast_to([P, NT, P])
                dve.copy_predicated(sc[:, h], mask, bank4(4 + u % 4)).then_inc(ph.sem("selected"), 1)

            for h in range(HG):
                dve.wait_ge(ph.sem("products"), h + 1)
                v.mark(dve.tensor_tensor(sc[:, h], bank4(h), m.ident[:].unsqueeze(1).broadcast_to([P, NT, P]), ALU.mult))
            v.wait()
            dve.wait_ge(ph.sem("end_decay"), 1)
            dve.tensor_tensor(kd[:], kd[:], x.k[:], ALU.mult).then_inc(ph.sem("kd"), 1)
            difference(0)
            for u in range(len(units)):
                if u + 1 < len(units):
                    difference(u + 1)
                keys(u)
                if u >= 1:
                    if u >= 2:
                        dve.wait_ge(ph.sem("selected"), u - 1)
                    select(u - 1)
            dve.wait_ge(ph.sem("selected"), len(units) - 1)
            select(len(units) - 1)
            for c in range(NCH):
                dve.wait_ge(ph.sem("outer"), c + 1)
                if c:
                    dve.wait_ge(ph.sem("state"), HG * c)
                for h in range(HG):
                    dve.scalar_tensor_tensor(st[:, c + 1, h, :], st[:, c, h, :], dl[:, h, c:c + 1],
                                             m.banks[c % 4][:, h * P:(h + 1) * P], ALU.mult, ALU.add).then_inc(ph.sem("state"), 1)
            for h in range(HG):
                dve.wait_ge(ph.sem("sums"), h + 1)
                dve.tensor_scalar(sq[:, h, :], m.banks[h][:], 1.0 / P, EPS, ALU.mult, ALU.add).then_inc(ph.sem("mean"), 1)
            g = COLUMN["hg_norm_2"]
            dve.wait_ge(ph.sem("out_taken"), HG)
            for h in range(HG):
                dve.wait_ge(ph.sem("inverse_root"), h + 1)
                v.mark(dve.scalar_tensor_tensor(m.mixT[:, h, :], m.mixT[:, h, :], m.params[:, g:g + 1], sq[:, h, :], ALU.mult, ALU.mult))
            for h in range(HG):
                v.wait(v.n - HG + 1)
                v.mark(dve.tensor_tensor(m.mixT[:, h, :], m.mixT[:, h, :], x.g[:, h, :], ALU.mult))
            v.wait()

        @block.scalar
        def _(act):
            a = Chain(act, ph.sem("act"))
            act.wait_ge(ph.sem("to_end"), 1)
            act.activation(kd[:], kd[:], ACT.Exp).then_inc(ph.sem("end_decay"), 1)
            a.link(act.activation(dl[:], chunked(x.b)[:, :, :, CH - 1], ACT.Exp))
            for u in range(len(units)):
                act.wait_ge(ph.sem("difference"), u + 1)
                a.link(act.activation(e2[:, u % 2, :], e2[:, u % 2, :], ACT.Abs))
                act.activation(e2[:, u % 2, :], e2[:, u % 2, :], ACT.Exp, scale=-1.0).then_inc(ph.sem("decay"), 1)
                if u == 3:
                    act.wait_ge(ph.sem("kd_turned"), 1)
                    for t in range(NT):
                        act.wait_ge(ph.sem("kd_turned"), t + 1)
                        act.activation(krow[:, t], bank4(t), ACT.Copy).then_inc(ph.sem("krow"), 1)
            act.wait_ge(ph.sem("difference"), len(units))
            act.activation(x.b[:], x.b[:], ACT.Exp).then_inc(ph.sem("start_decay"), 1)
            for h in range(HG):
                act.wait_ge(ph.sem("out"), h + 1)
                act.activation(m.mixT[:, h, :], m.banks[4 + h][:], ACT.Copy).then_inc(ph.sem("out_taken"), 1)
                act.activation(sq[:, h, :], m.banks[4 + h][:], ACT.Square).then_inc(ph.sem("squared"), 1)
            inverse_root_act(act, ph, sq, HG)

        @block.gpsimd
        def _(pool):
            for u in range(len(units)):
                h, _ = units[u]
                pool.wait_ge(ph.sem("decay"), u + 1)
                if u >= 2:
                    pool.wait_ge(ph.sem("products"), HG + u - 1)
                pool.tensor_tensor(q2[:, u % 2, :], x.q[:, h, :], e2[:, u % 2, :], ALU.mult).then_inc(ph.sem("queries"), 1)
            pool.wait_ge(ph.sem("queries"), len(units))
            pool.wait_ge(ph.sem("start_decay"), 1)
            pool.tensor_tensor(qb[:], x.q[:], x.b[:], ALU.mult).then_inc(ph.sem("qb"), 1)

        @block.tensor
        def _(pe):
            for h in range(HG):
                for t in range(NT):
                    last = pe.matmul(m.banks[h][:, t * P:(t + 1) * P], x.k[:, h, t * P:(t + 1) * P], x.q[:, h, t * P:(t + 1) * P],
                                     start=True, stop=True)
                last.then_inc(ph.sem("products"), 1)
            pe.wait_ge(ph.sem("kd"), 1)
            for t in range(NT):
                for h in range(HG):
                    last = pe.transpose(m.banks[t][:, h * P:(h + 1) * P], kd[:, h, t * P:(t + 1) * P], m.ident[:])
                last.then_inc(ph.sem("kd_turned"), 1)
            for u in range(len(units)):
                pe.wait_ge(ph.sem("queries"), u + 1)
                pe.wait_ge(ph.sem("keys"), u + 1)
                if u >= 4:
                    pe.wait_ge(ph.sem("selected"), u - 3)
                for t in range(NT):
                    last = pe.matmul(m.banks[4 + u % 4][:, t * P:(t + 1) * P], k2[:, u % 2, t * P:(t + 1) * P],
                                     q2[:, u % 2, t * P:(t + 1) * P], start=True, stop=True)
                last.then_inc(ph.sem("products"), 1)
            pe.wait_ge(ph.sem("krow"), NT)
            for c in range(NCH):
                if c >= 4:
                    pe.wait_ge(ph.sem("state"), HG * (c - 3))
                b, t = 64 * (c % 2), c // 2
                for h in range(HG):
                    last = pe.matmul(m.banks[c % 4][:, h * P:(h + 1) * P], krow[b:b + 64, t, h, :], x.i[b:b + 64, t, h * P:(h + 1) * P],
                                     start=True, stop=True)
                last.then_inc(ph.sem("outer"), 1)
            pe.wait_ge(ph.sem("state"), HG * NCH)
            pe.wait_ge(ph.sem("selected"), len(units))
            pe.wait_ge(ph.sem("qb"), 1)
            for h in range(HG):
                for t in range(NT):
                    out = m.banks[4 + h][:, t * P:(t + 1) * P]
                    pe.matmul(out, x.i[:, t, h * P:(h + 1) * P], sc[:, h, t, :], start=True, stop=True, skip_group_check=True)
                    for half in range(2):
                        last = pe.matmul(out[:, 64 * half:64 * half + 64], st[:, 2 * t + half, h, :],
                                         qb[:, h, t * P + 64 * half:t * P + 64 * half + 64], start=False, stop=True, skip_group_check=True)
                last.then_inc(ph.sem("out"), 1)
            for h in range(HG):
                pe.wait_ge(ph.sem("squared"), h + 1)
                pe.matmul(m.banks[h][:], m.ones[:], sq[:, h, :], start=True, stop=True).then_inc(ph.sem("sums"), 1)
    ph.close()


F_PLACE = [(1, 384), (2, 0), (1, 0), (0, 0)]
F_FLAT = [896, 1024, 512, 0]


def phase_fox(nc, m, x, load_ahead):
    ph = Phase(nc, "fox")
    at = x.free
    p2, at = m.view(at, 2, 1280)
    pt, at = m.view(at, 2, 10, P)
    o, at = m.view(at, NT, FH, 64)
    sq, at = m.view(at, NT, FH, 64)
    far, at = m.view(at, P)
    mx, at = m.view(at, FH, NT)
    total, at = m.view(at, FH, NT)
    rms, at = m.view(at, NT, FH)
    blocks = [(t, s) for t in range(NT) for s in range(t + 1)]
    parts = [(0, 4), (4, 8), (8, 10)]
    zbank = lambda h, i: m.banks[3 * (h % 2) + i]

    def region(h, t):
        b, c = F_PLACE[t]
        return zbank(h, b)[:, c:c + (t + 1) * P]

    with nc.Block() as block:
        @block.sync
        def _(sp):
            load_ahead(sp)

        @block.tensor
        def _(pe):
            def logits(h):
                if h >= 2:
                    pe.wait_ge(ph.sem("exp"), NT * (h - 1))
                r = 64 * (h % 2)
                for t in (3, 2, 1, 0):
                    last = pe.matmul(region(h, t), x.fq[r:r + 64, h // 2, t * P:(t + 1) * P], x.fk[r:r + 64, h // 2, 0:(t + 1) * P],
                                     start=(t != 0), stop=False, skip_group_check=True)
                last.then_inc(ph.sem("qk"), 1)
                pe.wait_ge(ph.sem("qk"), h + 1)
                for t in (3, 2, 1, 0):
                    last = pe.matmul(region(h, t), m.sel8[0:8, h, :], x.ncum[0:8, 0:(t + 1) * P],
                                     start=False, stop=True, skip_group_check=True)
                last.then_inc(ph.sem("logits"), 1)

            def turn(h):
                pe.wait_ge(ph.sem("exp"), NT * (h + 1))
                for i, (a, b) in enumerate(parts):
                    k = 3 * h + i
                    if k >= 1:
                        pe.wait_ge(ph.sem("pt"), k)
                    for j in range(a, b):
                        t, s = blocks[j]
                        last = pe.transpose(m.banks[6][:, (j - a) * P:(j - a + 1) * P],
                                            p2[:, h % 2, F_FLAT[t] + s * P:F_FLAT[t] + (s + 1) * P], m.ident[:])
                    last.then_inc(ph.sem("turned"), 1)

            def values(h):
                pe.wait_ge(ph.sem("pt"), 3 * (h + 1))
                if h >= 1:
                    pe.wait_ge(ph.sem("o"), h)
                for j, (t, s) in enumerate(blocks):
                    c = 256 * (h % 2) + 64 * t
                    last = pe.matmul(m.banks[7][:, c:c + 64], pt[:, h % 2, j, :], x.fv[:, s, 64 * h:64 * h + 64],
                                     start=(s == 0), stop=(s == t))
                last.then_inc(ph.sem("values"), 1)

            logits(0)
            for h in range(FH):
                if h + 1 < FH:
                    logits(h + 1)
                if h >= 1:
                    values(h - 1)
                turn(h)
            values(FH - 1)
            pe.wait_ge(ph.sem("normed"), 1)
            for t in range(NT):
                for c in range(HC):
                    last = pe.transpose(m.banks[c][:, t * P:(t + 1) * P], o[:, t, 2 * c:2 * c + 2, :].rearrange("p a b -> p (a b)"), m.ident[:])
            last.then_inc(ph.sem("o_turned"), 1)

        @block.vector
        def _(dve):
            v = Chain(dve, ph.sem("dve"))
            v.link(dve.tensor_scalar(far[:], m.after[:], -1e30, None, ALU.mult))

            def masked(h):
                dve.wait_ge(ph.sem("logits"), h + 1)
                for t in range(NT):
                    d = region(h, t)[:, t * P:]
                    v.mark(dve.tensor_tensor(d, d, far[:], ALU.add))
                v.wait()
                for t in range(NT):
                    v.mark(dve.tensor_reduce(mx[:, h, t:t + 1], region(h, t), AX_X, ALU.max))
                v.wait()
                dve.tensor_scalar(mx[:, h], mx[:, h], -1.0, None, ALU.mult).then_inc(ph.sem("max"), 1)

            def output(h):
                dve.wait_ge(ph.sem("exp"), NT * (h + 1))
                v.link(dve.reciprocal(total[:, h], total[:, h]))
                dve.wait_ge(ph.sem("values"), h + 1)
                c = 256 * (h % 2)
                dve.tensor_tensor(o[:, :, h, :], m.banks[7][:, c:c + 256].rearrange("p (t n) -> p t n", n=64),
                                  total[:, h].unsqueeze(2).broadcast_to([P, NT, 64]), ALU.mult).then_inc(ph.sem("o"), 1)

            masked(0)
            for h in range(FH):
                if h + 1 < FH:
                    masked(h + 1)
                if h >= 1:
                    output(h - 1)
            output(FH - 1)
            dve.wait_ge(ph.sem("o"), FH)
            v.link(dve.tensor_tensor(sq[:], o[:], o[:], ALU.mult))
            v.link(dve.tensor_reduce(rms[:], sq[:], AX_X, ALU.add))
            dve.tensor_scalar(rms[:], rms[:], 1.0 / 64, EPS, ALU.mult, ALU.add).then_inc(ph.sem("mean"), 1)
            dve.wait_ge(ph.sem("deviation"), 1)
            v.link(dve.reciprocal(rms[:], rms[:]))
            dve.tensor_tensor(o[:], o[:], rms.unsqueeze(3).broadcast_to([P, NT, FH, 64]), ALU.mult).then_inc(ph.sem("normed"), 1)
            dve.wait_ge(ph.sem("o_turned"), 1)
            g = COLUMN["fox_norm_2"]
            for c in range(HC):
                v.mark(dve.tensor_scalar(m.mixT[:, HC + c, :], m.banks[c][:], m.params[:, g:g + 1], None, ALU.mult))
            v.wait()

        @block.scalar
        def _(act):
            def exps(h):
                act.wait_ge(ph.sem("max"), h + 1)
                if h >= 2:
                    act.wait_ge(ph.sem("turned"), 3 * (h - 1))
                for t in range(NT):
                    act.activation(p2[:, h % 2, F_FLAT[t]:F_FLAT[t] + (t + 1) * P], region(h, t), ACT.Exp, bias=mx[:, h, t:t + 1],
                                   accum_out=total[:, h, t:t + 1]).then_inc(ph.sem("exp"), 1)

            def probabilities(h):
                for i, (a, b) in enumerate(parts):
                    act.wait_ge(ph.sem("turned"), 3 * h + i + 1)
                    if h >= 2:
                        act.wait_ge(ph.sem("values"), h - 1)
                    act.activation(pt[:, h % 2, a:b, :], m.banks[6][:, 0:(b - a) * P].rearrange("p (a b) -> p a b", b=P),
                                   ACT.Copy).then_inc(ph.sem("pt"), 1)

            for h in range(FH):
                exps(h)
                probabilities(h)
            act.wait_ge(ph.sem("mean"), 1)
            act.activation(rms[:], rms[:], ACT.Sqrt).then_inc(ph.sem("deviation"), 1)
    ph.close()
INPUTS = [
    "x", "norm_mix_g", "w_in", "shift_mu", "sb_out_g", "rw_w0", "rw_w2", "rw_a0", "rw_a2", "rw_g2", "rw_k_k", "rw_k_a",
    "rw_r_k", "rw_ln_w", "rw_ln_b", "w_out", "norm_ffn_g", "router_grp_w", "router_grp_b", "router_exp_w",
    "router_exp_b", "exp_w_gate", "exp_w_up", "exp_w_down", "final_norm_g", "attn_norm_2", "w_in_2",
    "hg_lb_logits_2", "hg_norm_2", "fox_f_bias_2", "fox_norm_2", "w_out_2", "ffn_norm_2", "w_group_2",
    "b_group_2", "w_expert_2", "b_expert_2", "w_gate_2", "w_up_2", "w_down_2", "final_norm_2",
]


def two_blocks_kernel(nc, io, out):
    with ExitStack() as ctx:
        m = Memory(nc, ctx)
        ring = [[nc.alloc_semaphore(f"experts{b}_ring{s}") for s in range(4)] for b in range(2)]
        w_out_sems = [nc.alloc_semaphore(f"w_out{b}") for b in range(2)]
        between = nc.dram_tensor("between_blocks", (1, S, D), F32, kind="Internal").ap()

        x = Mix1(m)
        ahead = {n: nc.alloc_semaphore(f"first_{n}") for n in ("rows", "ring0", "ring1")}
        setup_phase(nc, m, io, lambda sp: load_first(sp, m, io, x, ahead))

        g2s, _ = m.view(m.arena_size - HW, HW)
        phase_project1(nc, m, io, g2s, ahead)
        phase_stick(nc, m, x)
        phase_rwkv(nc, m, x, g2s, lambda sp: load_w_out(sp, m, io["w_out"], w_out_sems[0]))
        z = Moe(m, 32, 8, 1, 64, 1)
        z.weights = ("exp_w_gate", "exp_w_up", "exp_w_down")
        phase_out(nc, m, io, z, "out1", io["x"], w_out_sems[0], "norm_ffn_g",
                  ("router_grp_w", "router_grp_b", "router_exp_w", "router_exp_b"), ring[0])
        phase_moe(nc, m, io, z, "moe1", COLUMN["norm_ffn_g"], ring[0])

        phase_final(nc, m, z, "end1", io["final_norm_g"], between)

        m.open("mix2")
        y = Mix2(m)
        phase_project2(nc, m, io, y)
        phase_hgrn(nc, m, y)
        phase_fox(nc, m, y, lambda sp: load_w_out(sp, m, io["w_out_2"], w_out_sems[1]))
        z = Moe(m, 16, 4, 2, 128, 2)
        z.weights = ("w_gate_2", "w_up_2", "w_down_2")
        phase_out(nc, m, io, z, "out2", between, w_out_sems[1], "ffn_norm_2",
                  ("w_group_2", "b_group_2", "w_expert_2", "b_expert_2"), ring[1])
        phase_moe(nc, m, io, z, "moe2", COLUMN["ffn_norm_2"], ring[1])
        phase_final(nc, m, z, "end2", io["final_norm_2"], out)


def kernel(**inputs):
    import concourse.bacc as bacc
    from concourse.bass_utils import run_bass_kernel_spmd

    nc = bacc.Bacc("TRN2", target_bir_lowering=False, num_devices=1)
    arrays, io = {}, {}
    for name in INPUTS:
        a = np.ascontiguousarray(inputs[name])
        arrays[f"in_{name}"] = a
        io[name] = nc.dram_tensor(f"in_{name}", a.shape, mybir.dt.from_np(a.dtype), kind="ExternalInput").ap()
    out = nc.dram_tensor("out_0", (1, S, D), F32, kind="ExternalOutput").ap()
    two_blocks_kernel(nc, io, out)
    r = run_bass_kernel_spmd(nc, [arrays], core_ids=[0])
    return r.results[0]["out_0"]
```
